# Optimizing a Trainium2 kernel written in Bass

```python
import math
import jax, jax.numpy as jnp
from jax import lax
import numpy as np

D_MODEL = 2048
BATCH = 1
SEQ = 256
DEPTH = 1

HEAD_DIM = 128
N_MEM = 256
GRID_W = 64
DIL_PAIRS = ((128, 1), (512, 4), (2048, 16))
A_HEADS_PER_GROUP = 2
A_HEADS = A_HEADS_PER_GROUP * len(DIL_PAIRS)
A_BLOCK = 64
B_Q_HEADS = 6
B_KV_HEADS = 2
B_QBLOCK = 128
ROPE_THETA = 10000.0
C_HEADS = 4
N_BRANCH = 3
REL_BUCKETS = 32
REL_MAX_DIST = 1024
D_FF = -(-8 * D_MODEL // (3 * 256)) * 256
EPS = 1e-6
NEG = -1e30

A_W = A_HEADS * HEAD_DIM
A_OUT_W = A_HEADS_PER_GROUP * HEAD_DIM
B_QW = B_Q_HEADS * HEAD_DIM
B_KVW = B_KV_HEADS * HEAD_DIM
C_W = C_HEADS * HEAD_DIM
IN_SPLITS = (A_W, A_W, A_W, B_QW, B_KVW, B_KVW, C_W, N_BRANCH * D_MODEL)
IN_W = sum(IN_SPLITS)


def rms_norm(x, g):
    xf = x.astype(jnp.float32)
    y = xf * lax.rsqrt(jnp.mean(xf * xf, axis=-1, keepdims=True) + EPS)
    return (y * g.astype(jnp.float32)).astype(x.dtype)

def split_heads(t, h):
    return t.reshape(t.shape[0], t.shape[1], h, HEAD_DIM)

def t5_bucket(rel):
    nb = REL_BUCKETS // 2
    ret = jnp.where(rel > 0, nb, 0)
    n = jnp.abs(rel)
    max_exact = nb // 2
    large = max_exact + (jnp.log(jnp.maximum(n, 1).astype(jnp.float32) / max_exact)
                         / math.log(REL_MAX_DIST / max_exact) * (nb - max_exact)).astype(jnp.int32)
    large = jnp.minimum(large, nb - 1)
    return ret + jnp.where(n < max_exact, n, large)

def dilated_group(q, k, v, bias_tab, window, dil):
    b, s, h, dh = q.shape
    L = s // dil
    radius = window // (2 * dil)
    n = b * dil

    def to_res(t):
        return t.reshape(b, L, dil, h, dh).transpose(0, 2, 1, 3, 4).reshape(n, L, h, dh)

    qr, kr, vr = to_res(q), to_res(k), to_res(v)
    nb = -(-L // A_BLOCK)
    lp = nb * A_BLOCK
    side = -(-radius // A_BLOCK)
    pad = side * A_BLOCK
    wk = (2 * side + 1) * A_BLOCK
    qb = jnp.pad(qr, ((0, 0), (0, lp - L), (0, 0), (0, 0))).reshape(n, nb, A_BLOCK, h, dh)

    def band(t):
        tp = jnp.pad(t, ((0, 0), (pad, lp - L + pad), (0, 0), (0, 0))).reshape(n, nb + 2 * side, A_BLOCK, h, dh)
        return jnp.concatenate([tp[:, i:i + nb] for i in range(2 * side + 1)], axis=2)

    kb, vb = band(kr), band(vr)
    rel = (jnp.arange(wk) - pad)[None, :] - jnp.arange(A_BLOCK)[:, None]
    bias = bias_tab[t5_bucket(rel * dil)].transpose(2, 0, 1).astype(jnp.float32)
    k_pos = jnp.arange(nb)[:, None] * A_BLOCK - pad + jnp.arange(wk)[None, :]
    valid = (jnp.abs(rel) <= radius)[None] & ((k_pos >= 0) & (k_pos < L))[:, None, :]
    sc = jnp.einsum('nbqhd,nbkhd->nbhqk', qb, kb, preferred_element_type=jnp.float32) / math.sqrt(dh)
    sc = jnp.where(valid[None, :, None], sc + bias[None, None], NEG)
    m = jnp.max(sc, axis=-1, keepdims=True)
    p = jnp.exp(sc - m)
    l = jnp.sum(p, axis=-1, keepdims=True)
    o = jnp.einsum('nbhqk,nbkhd->nbqhd', p, vb.astype(jnp.float32))
    o = o / l[..., 0].transpose(0, 1, 3, 2)[..., None]
    lse = (m + jnp.log(l))[..., 0].transpose(0, 1, 3, 2)
    o = o.reshape(n, lp, h, dh)[:, :L]
    lse = lse.reshape(n, lp, h)[:, :L]
    o = o.reshape(b, dil, L, h, dh).transpose(0, 2, 1, 3, 4).reshape(b, s, h, dh)
    lse = lse.reshape(b, dil, L, h).transpose(0, 2, 1, 3).reshape(b, s, h)
    return o, lse

def axial_rope_tables(s):
    rows = s // GRID_W
    r = jnp.repeat(jnp.arange(rows), GRID_W).astype(jnp.float32)
    c = jnp.tile(jnp.arange(GRID_W), rows).astype(jnp.float32)
    nf = HEAD_DIM // 4
    inv = ROPE_THETA ** (-jnp.arange(nf, dtype=jnp.float32) / nf)
    ang = jnp.concatenate([r[:, None] * inv, c[:, None] * inv], axis=-1)
    return jnp.cos(ang), jnp.sin(ang)

def apply_rope(x, cos, sin):
    b, s, h, dh = x.shape
    xf = x.astype(jnp.float32).reshape(b, s, h, dh // 2, 2)
    x0, x1 = xf[..., 0], xf[..., 1]
    c, sn = cos[None, :, None, :], sin[None, :, None, :]
    out = jnp.stack([x0 * c - x1 * sn, x0 * sn + x1 * c], axis=-1)
    return out.reshape(b, s, h, dh).astype(x.dtype)

def gqa_blocks(q, k, v):
    b, s, hq, dh = q.shape
    g = hq // B_KV_HEADS
    nblk = s // B_QBLOCK
    qb = q.reshape(b, nblk, B_QBLOCK, B_KV_HEADS, g, dh).transpose(1, 0, 2, 3, 4, 5)

    def one_block(qq):
        sc = jnp.einsum('bqkgd,bskd->bkgqs', qq, k, preferred_element_type=jnp.float32) / math.sqrt(dh)
        p = jax.nn.softmax(sc, axis=-1)
        return jnp.einsum('bkgqs,bskd->bqkgd', p, v.astype(jnp.float32)).astype(q.dtype)

    o = lax.map(one_block, qb)
    return o.transpose(1, 0, 2, 3, 4, 5).reshape(b, s, hq * dh)

def first_inputs(seed: int = 0) -> dict:
    key = jax.random.key(seed)
    ks = jax.random.split(key, 24)
    f32 = jnp.float32

    def w(k, shape, fan_in):
        return jax.random.normal(k, shape, f32) * (fan_in ** -0.5)

    def gain(k, shape):
        return 1.0 + 0.05 * jax.random.normal(k, shape, f32)

    Dp = DEPTH
    return {
        "x": jax.random.normal(ks[0], (BATCH, SEQ, D_MODEL), f32),
        "mem": jax.random.normal(ks[1], (BATCH, N_MEM, D_MODEL), f32),
        "rel_bias": 0.5 * jax.random.normal(ks[2], (REL_BUCKETS, A_HEADS), f32),
        "g_mix": gain(ks[3], (Dp, D_MODEL)),
        "w_in": w(ks[4], (Dp, D_MODEL, IN_W), D_MODEL),
        "g_qa": gain(ks[5], (Dp, HEAD_DIM)),
        "g_ka": gain(ks[6], (Dp, HEAD_DIM)),
        "g_qb": gain(ks[7], (Dp, HEAD_DIM)),
        "g_kb": gain(ks[8], (Dp, HEAD_DIM)),
        "g_mem": gain(ks[9], (Dp, D_MODEL)),
        "w_mem_kv": w(ks[10], (Dp, D_MODEL, 2 * C_W), D_MODEL),
        "g_qc": gain(ks[11], (Dp, HEAD_DIM)),
        "g_kc": gain(ks[12], (Dp, HEAD_DIM)),
        "w_br_a": w(ks[13], (Dp, A_OUT_W, D_MODEL), A_OUT_W),
        "w_br_b": w(ks[14], (Dp, B_QW, D_MODEL), B_QW),
        "w_br_c": w(ks[15], (Dp, C_W, D_MODEL), C_W),
        "w_o": w(ks[16], (Dp, D_MODEL, D_MODEL), D_MODEL),
        "g_ffn": gain(ks[17], (Dp, D_MODEL)),
        "w_ffn_in": w(ks[18], (Dp, D_MODEL, 2 * D_FF), D_MODEL),
        "w_ffn_out": w(ks[19], (Dp, D_FF, D_MODEL), D_FF),
    }

def first_block(x, mem, rel_bias, g_mix, w_in, g_qa, g_ka, g_qb, g_kb, g_mem, w_mem_kv,
              g_qc, g_kc, w_br_a, w_br_b, w_br_c, w_o, g_ffn, w_ffn_in, w_ffn_out):
    b, s, _ = x.shape
    cos, sin = axial_rope_tables(s)
    offs = np.cumsum((0,) + IN_SPLITS)
    for layer in range(DEPTH):
        h = rms_norm(x, g_mix[layer])
        proj = h @ w_in[layer]
        qa, ka, va, qb, kb, vb, qc, gt = [proj[..., offs[i]:offs[i + 1]] for i in range(len(IN_SPLITS))]

        qa = rms_norm(split_heads(qa, A_HEADS), g_qa[layer])
        ka = rms_norm(split_heads(ka, A_HEADS), g_ka[layer])
        va = split_heads(va, A_HEADS)
        outs, lses = [], []
        for gi, (win, dil) in enumerate(DIL_PAIRS):
            sl = slice(gi * A_HEADS_PER_GROUP, (gi + 1) * A_HEADS_PER_GROUP)
            o, lse = dilated_group(qa[:, :, sl], ka[:, :, sl], va[:, :, sl], rel_bias[:, sl], win, dil)
            outs.append(o)
            lses.append(lse)
        wgt = jax.nn.softmax(jnp.stack(lses), axis=0)
        oa = jnp.sum(wgt[..., None] * jnp.stack(outs), axis=0).reshape(b, s, A_OUT_W).astype(x.dtype)

        qb = apply_rope(rms_norm(split_heads(qb, B_Q_HEADS), g_qb[layer]), cos, sin)
        kb = apply_rope(rms_norm(split_heads(kb, B_KV_HEADS), g_kb[layer]), cos, sin)
        ob = gqa_blocks(qb, kb, split_heads(vb, B_KV_HEADS))

        mkv = rms_norm(mem, g_mem[layer]) @ w_mem_kv[layer]
        kc = rms_norm(split_heads(mkv[..., :C_W], C_HEADS), g_kc[layer])
        vc = split_heads(mkv[..., C_W:], C_HEADS)
        qc = rms_norm(split_heads(qc, C_HEADS), g_qc[layer])
        sc = jnp.einsum('bqhd,bmhd->bhqm', qc, kc, preferred_element_type=jnp.float32) / math.sqrt(HEAD_DIM)
        pc = jax.nn.softmax(sc, axis=-1)
        oc = jnp.einsum('bhqm,bmhd->bqhd', pc, vc.astype(jnp.float32)).reshape(b, s, C_W).astype(x.dtype)

        gates = jax.nn.sigmoid(gt.astype(jnp.float32)).reshape(b, s, N_BRANCH, D_MODEL)
        merged = (gates[:, :, 0] * (oa @ w_br_a[layer]).astype(jnp.float32)
                  + gates[:, :, 1] * (ob @ w_br_b[layer]).astype(jnp.float32)
                  + gates[:, :, 2] * (oc @ w_br_c[layer]).astype(jnp.float32)).astype(x.dtype)
        x = x + merged @ w_o[layer]

        hf = rms_norm(x, g_ffn[layer]) @ w_ffn_in[layer]
        x = x + (jax.nn.silu(hf[..., :D_FF]) * hf[..., D_FF:]) @ w_ffn_out[layer]
    return x


CHUNK = 64
Q_BLOCK = 2 * CHUNK
MIX_WIDTH = D_MODEL
ATTN_WIDTH = MIX_WIDTH // 2
ATTN_HEADS = 8
ATTN_HEAD_DIM = ATTN_WIDTH // ATTN_HEADS
LRU_WIDTH = MIX_WIDTH - ATTN_WIDTH
LRU_BLOCKS = 8
LRU_BLOCK_DIM = LRU_WIDTH // LRU_BLOCKS
CONV_WIDTH = 4
LRU_C = 8.0
OFF_Q = 0
OFF_K = OFF_Q + ATTN_WIDTH
OFF_V = OFF_K + ATTN_WIDTH
OFF_F = OFF_V + ATTN_WIDTH
OFF_LX = OFF_F + ATTN_HEADS
OFF_LY = OFF_LX + LRU_WIDTH
IN_COLS = OFF_LY + LRU_WIDTH
PEER_HEADS = 8
PEER_N_KEYS = 128
PEER_N_EXPERTS = PEER_N_KEYS * PEER_N_KEYS
PEER_QUERY_DIM = 256
PEER_HALF = PEER_QUERY_DIM // 2
PEER_TOPK = 16
PEER_TOKEN_BLOCK = 128
N_ADA = 6


def _rmsnorm(x, g):
    xf = x.astype(jnp.float32)
    y = xf * lax.rsqrt(jnp.mean(xf * xf, axis=-1, keepdims=True) + EPS)
    return y.astype(x.dtype) * g

def _forgetting_attention(q, k, v, log_f):
    n_blocks = q.shape[2] // Q_BLOCK
    cum = jnp.cumsum(log_f, axis=-1)
    scale = ATTN_HEAD_DIM ** -0.5
    outs = []
    for blk in range(n_blocks):
        start = blk * Q_BLOCK
        end = start + Q_BLOCK
        qb = q[:, :, start:end]
        kb = k[:, :, :end]
        vb = v[:, :, :end]
        logits = jnp.einsum('bhqd,bhkd->bhqk', qb, kb).astype(jnp.float32) * scale
        logits = logits + cum[:, :, start:end, None] - cum[:, :, None, :end]
        mask = jnp.arange(end)[None, :] <= (start + jnp.arange(Q_BLOCK))[:, None]
        logits = jnp.where(mask, logits, -jnp.inf)
        p = jax.nn.softmax(logits, axis=-1)
        outs.append(jnp.einsum('bhqk,bhkd->bhqd', p.astype(v.dtype), vb))
    return jnp.concatenate(outs, axis=2)

def _causal_depthwise_conv(x, w, b):
    y = lax.conv_general_dilated(
        x, w[:, None, :], window_strides=(1,), padding=[(CONV_WIDTH - 1, 0)],
        dimension_numbers=('NWC', 'WIO', 'NWC'), feature_group_count=x.shape[-1])
    return y + b

def _rg_lru(xc, w_a, b_a, w_x, b_x, lam):
    B, S, _ = xc.shape
    xb = xc.reshape(B, S, LRU_BLOCKS, LRU_BLOCK_DIM)
    r = jax.nn.sigmoid(jnp.einsum('bsni,nij->bsnj', xb, w_a).reshape(B, S, LRU_WIDTH) + b_a)
    i = jax.nn.sigmoid(jnp.einsum('bsni,nij->bsnj', xb, w_x).reshape(B, S, LRU_WIDTH) + b_x)
    log_a = -LRU_C * r.astype(jnp.float32) * jax.nn.softplus(-lam.astype(jnp.float32))
    a = jnp.exp(log_a)
    bterm = jnp.sqrt(-jnp.expm1(2.0 * log_a)) * (i * xc).astype(jnp.float32)

    def combine(lhs, rhs):
        a1, b1 = lhs
        a2, b2 = rhs
        return a1 * a2, a2 * b1 + b2

    _, h = lax.associative_scan(combine, (a, bterm), axis=1)
    return h.astype(xc.dtype)

def _hybrid_mixer(h, w_in, b_f, conv_w, conv_b, lru_w_a, lru_b_a, lru_w_x, lru_b_x,
                  lru_lambda, g_attn_out, g_lru_out, w_out):
    B, S, _ = h.shape
    proj = h @ w_in

    def heads(t):
        return t.reshape(B, S, ATTN_HEADS, ATTN_HEAD_DIM).transpose(0, 2, 1, 3)

    q = heads(proj[..., OFF_Q:OFF_K])
    k = heads(proj[..., OFF_K:OFF_V])
    v = heads(proj[..., OFF_V:OFF_F])
    f_logit = (proj[..., OFF_F:OFF_LX] + b_f).astype(jnp.float32)
    log_f = jax.nn.log_sigmoid(f_logit).transpose(0, 2, 1)
    attn = _forgetting_attention(q, k, v, log_f)
    attn = attn.transpose(0, 2, 1, 3).reshape(B, S, ATTN_WIDTH)

    lx = proj[..., OFF_LX:OFF_LY]
    ly = proj[..., OFF_LY:IN_COLS]
    xc = _causal_depthwise_conv(lx, conv_w, conv_b)
    lru = _rg_lru(xc, lru_w_a, lru_b_a, lru_w_x, lru_b_x, lru_lambda) * jax.nn.gelu(ly)

    merged = jnp.concatenate([_rmsnorm(attn, g_attn_out), _rmsnorm(lru, g_lru_out)], axis=-1)
    return merged @ w_out

def _peer(h, w_q, k1, k2, u, vt):
    B, S, D = h.shape
    q = (h @ w_q).reshape(B, S, PEER_HEADS, 2, PEER_HALF)
    s1 = jnp.einsum('bshd,hnd->bshn', q[..., 0, :], k1).astype(jnp.float32)
    s2 = jnp.einsum('bshd,hnd->bshn', q[..., 1, :], k2).astype(jnp.float32)
    v1, i1 = lax.top_k(s1, PEER_TOPK)
    v2, i2 = lax.top_k(s2, PEER_TOPK)
    cand = (v1[..., :, None] + v2[..., None, :]).reshape(B, S, PEER_HEADS, PEER_TOPK * PEER_TOPK)
    vs, ic = lax.top_k(cand, PEER_TOPK)
    e = (jnp.take_along_axis(i1, ic // PEER_TOPK, axis=-1) * PEER_N_KEYS
         + jnp.take_along_axis(i2, ic % PEER_TOPK, axis=-1))
    w = jax.nn.softmax(vs, axis=-1).astype(h.dtype)

    nb = (B * S) // PEER_TOKEN_BLOCK
    hb = h.reshape(nb, PEER_TOKEN_BLOCK, D)
    eb = e.reshape(nb, PEER_TOKEN_BLOCK, PEER_HEADS, PEER_TOPK)
    wb = w.reshape(nb, PEER_TOKEN_BLOCK, PEER_HEADS, PEER_TOPK)

    def expert_block(args):
        hx, ex, wx = args
        ug = jnp.take(u, ex, axis=0)
        act = jax.nn.gelu(jnp.einsum('thkd,td->thk', ug, hx)) * wx
        vg = jnp.take(vt, ex, axis=0)
        return jnp.einsum('thk,thkd->td', act, vg)

    y = lax.map(expert_block, (hb, eb, wb))
    return y.reshape(B, S, D)

def second_inputs(seed: int = 0) -> dict:
    key = jax.random.key(seed)
    ks = jax.random.split(key, 26)
    f32 = jnp.float32
    L, D = DEPTH, D_MODEL

    def nrm(k, shape, scale):
        return jax.random.normal(k, shape, f32) * scale

    a0 = jax.random.uniform(ks[12], (L, LRU_WIDTH), f32, 0.9, 0.999) ** (1.0 / LRU_C)
    return {
        'x': nrm(ks[0], (BATCH, SEQ, D), 1.0),
        'c': nrm(ks[1], (BATCH, D), 1.0),
        'w_ada': nrm(ks[2], (L, D, N_ADA * D), 0.5 * D ** -0.5),
        'b_ada': nrm(ks[3], (L, N_ADA * D), 0.01),
        'g_mix': 1.0 + nrm(ks[4], (L, D), 0.05),
        'w_in': nrm(ks[5], (L, D, IN_COLS), D ** -0.5),
        'b_f': jax.random.uniform(ks[6], (L, ATTN_HEADS), f32, 1.0, 4.0),
        'conv_w': nrm(ks[7], (L, CONV_WIDTH, LRU_WIDTH), CONV_WIDTH ** -0.5),
        'conv_b': nrm(ks[8], (L, LRU_WIDTH), 0.01),
        'lru_w_a': nrm(ks[9], (L, LRU_BLOCKS, LRU_BLOCK_DIM, LRU_BLOCK_DIM), LRU_BLOCK_DIM ** -0.5),
        'lru_b_a': nrm(ks[10], (L, LRU_WIDTH), 0.01),
        'lru_w_x': nrm(ks[11], (L, LRU_BLOCKS, LRU_BLOCK_DIM, LRU_BLOCK_DIM), LRU_BLOCK_DIM ** -0.5),
        'lru_b_x': nrm(ks[13], (L, LRU_WIDTH), 0.01),
        'lru_lambda': jnp.log(a0) - jnp.log1p(-a0),
        'g_attn_out': 1.0 + nrm(ks[14], (L, ATTN_WIDTH), 0.05),
        'g_lru_out': 1.0 + nrm(ks[15], (L, LRU_WIDTH), 0.05),
        'w_out': nrm(ks[16], (L, MIX_WIDTH, D), MIX_WIDTH ** -0.5),
        'g_ffn': 1.0 + nrm(ks[17], (L, D), 0.05),
        'peer_w_q': nrm(ks[18], (L, D, PEER_HEADS * PEER_QUERY_DIM), D ** -0.5),
        'peer_k1': nrm(ks[19], (L, PEER_HEADS, PEER_N_KEYS, PEER_HALF), PEER_HALF ** -0.5),
        'peer_k2': nrm(ks[20], (L, PEER_HEADS, PEER_N_KEYS, PEER_HALF), PEER_HALF ** -0.5),
        'peer_u': nrm(ks[21], (L, PEER_N_EXPERTS, D), D ** -0.5),
        'peer_v': nrm(ks[22], (L, PEER_N_EXPERTS, D), 1.0),
        'g_final': 1.0 + nrm(ks[23], (D,), 0.05),
    }

def second_block(x, c, w_ada, b_ada, g_mix, w_in, b_f, conv_w, conv_b, lru_w_a, lru_b_a,
              lru_w_x, lru_b_x, lru_lambda, g_attn_out, g_lru_out, w_out, g_ffn,
              peer_w_q, peer_k1, peer_k2, peer_u, peer_v, g_final):
    sc = jax.nn.silu(c)
    for l in range(DEPTH):
        mod = sc @ w_ada[l] + b_ada[l]
        sh1, sc1, ga1, sh2, sc2, ga2 = jnp.split(mod, N_ADA, axis=-1)
        h = _rmsnorm(x, g_mix[l]) * (1.0 + sc1[:, None, :]) + sh1[:, None, :]
        mix = _hybrid_mixer(h, w_in[l], b_f[l], conv_w[l], conv_b[l], lru_w_a[l], lru_b_a[l],
                            lru_w_x[l], lru_b_x[l], lru_lambda[l], g_attn_out[l],
                            g_lru_out[l], w_out[l])
        x = x + ga1[:, None, :] * mix
        h = _rmsnorm(x, g_ffn[l]) * (1.0 + sc2[:, None, :]) + sh2[:, None, :]
        x = x + ga2[:, None, :] * _peer(h, peer_w_q[l], peer_k1[l], peer_k2[l], peer_u[l], peer_v[l])
    return _rmsnorm(x, g_final)


def setup_inputs(seed=0):
    out = dict(first_inputs(seed))
    for name, value in second_inputs(seed + 1).items():
        if name != "x":
            out[name + "_2"] = value
    return out


def reference(
    x, mem, rel_bias, g_mix, w_in, g_qa, g_ka, g_qb, g_kb, g_mem, w_mem_kv, g_qc, g_kc, w_br_a,
    w_br_b, w_br_c, w_o, g_ffn, w_ffn_in, w_ffn_out, c_2, w_ada_2, b_ada_2, g_mix_2, w_in_2,
    b_f_2, conv_w_2, conv_b_2, lru_w_a_2, lru_b_a_2, lru_w_x_2, lru_b_x_2, lru_lambda_2,
    g_attn_out_2, g_lru_out_2, w_out_2, g_ffn_2, peer_w_q_2, peer_k1_2, peer_k2_2, peer_u_2,
    peer_v_2, g_final_2,
):
    x = first_block(
        x, mem, rel_bias, g_mix, w_in, g_qa, g_ka, g_qb, g_kb, g_mem, w_mem_kv, g_qc, g_kc,
        w_br_a, w_br_b, w_br_c, w_o, g_ffn, w_ffn_in, w_ffn_out,
    )
    return second_block(
        x, c_2, w_ada_2, b_ada_2, g_mix_2, w_in_2, b_f_2, conv_w_2, conv_b_2, lru_w_a_2,
        lru_b_a_2, lru_w_x_2, lru_b_x_2, lru_lambda_2, g_attn_out_2, g_lru_out_2, w_out_2,
        g_ffn_2, peer_w_q_2, peer_k1_2, peer_k2_2, peer_u_2, peer_v_2, g_final_2,
    )


_drawn_inputs = setup_inputs


def setup_inputs(seed=0):
    import zlib

    import numpy as np

    out = dict(_drawn_inputs(seed))
    spreads = {}
    factors = {'g_mix': 3.485,
     'g_qa': 5.034,
     'g_ka': 5.51,
     'g_qb': 6.414,
     'g_kb': 6.907,
     'g_mem': 5.092,
     'g_qc': 6.806,
     'g_kc': 7.192,
     'conv_b_2': 19.491,
     'lru_b_a_2': 64.0,
     'lru_b_x_2': 64.0,
     'g_attn_out_2': 105.819,
     'g_lru_out_2': 111.903,
     'g_ffn': 5.381,
     'b_ada_2': 4.89,
     'g_mix_2': 3.933,
     'g_ffn_2': 17.398}
    for name, (base, spread) in spreads.items():
        noise = np.random.default_rng([zlib.crc32(name.encode()), seed]).standard_normal(out[name].shape)
        drawn = base * np.exp(spread * noise) if base else spread * noise
        out[name] = __import__('jax').numpy.asarray(drawn.astype(out[name].dtype))
    for name, factor in factors.items():
        out[name] = (out[name] * factor).astype(out[name].dtype)
    return out
```

```python
import math
import numpy as np
import concourse.bass as bass
from concourse import mybir

F32 = mybir.dt.float32
F32R = mybir.dt.float32r
U32 = mybir.dt.uint32
ALU = mybir.AluOpType
ACT = mybir.ActivationFunctionType
AX = mybir.AxisListType

P = 128
D = 2048
SEQ = 256
TOK = SEQ // P
KT = D // P
HD = 128
EPS = 1e-6
NEG = -1e30
SCALE = 1.0 / math.sqrt(HD)

A_HEADS, B_HEADS, B_KV, C_HEADS = 6, 6, 2, 4
ROPE_HEADS = B_HEADS + B_KV
HEADS = A_HEADS + B_HEADS + C_HEADS
D_FF = 5632
FF_GROUPS = D_FF // 512
ADA = 6 * D
ADA_SPLITS = ADA // 1024
H2 = 8
LRU = 1024
CONV = 4
N_KEYS = 128
EXPERTS = N_KEYS * N_KEYS
PEER_GROUPS = EXPERTS // 512
TOPK = 16
BUCKETS, MAX_DIST = 32, 1024
DILATIONS = (1, 4, 16)
RADIUS_STEPS = 64

Q_MEM = 0
Q_HEADS = Q_MEM + 2
Q_GATES = Q_HEADS + 8
Q_BRANCH = Q_GATES + 12
Q_WO = Q_BRANCH + 3
Q_FFN = Q_WO + 4
Q_IN2 = Q_FFN + 3 * FF_GROUPS
Q_OUT2 = Q_IN2 + 10
Q_PQ = Q_OUT2 + 4
Q_PEER = Q_PQ + 4
QUADS = Q_PEER + 2 * PEER_GROUPS

C_GMEM, C_GMIX, C_GFFN, C_GMIX2, C_GFFN2 = (16 * i for i in range(5))
C_HEAD = 80
C_CONVW = C_HEAD + 20
C_CONVB = C_CONVW + CONV * 8
C_BA = C_CONVB + 8
C_BX = C_BA + 8
C_LAM = C_BX + 8
C_GLRU = C_LAM + 8
C_GATT = C_GLRU + 8
C_BF = C_GATT + 8
NCOLS = C_BF + 1

FOLD_MEM, FOLD_X, FOLD_O, FOLD_M, FOLD_FFN, FOLD_MIX2, FOLD_ATT, FOLD_LRU, FOLD_PEER = 0, 4, 8, 11, 15, 19, 23, 25, 27


def program(nc, t):
    base0 = 16512
    K = 1024

    def at(name, shape, dt, off):
        return nc.alloc_sbuf_tensor_at(name, shape, dt, offset=base0 + off)

    raw = at("raw", [P, 4, 2048], F32, 0)
    hi = at("hi", [P, 4, 2048], F32R, 32 * K)
    lo = at("lo", [P, 4, 2048], F32R, 64 * K)
    XO = 96 * K
    x = at("x", [P, TOK, D], F32, XO)
    hTh = at("hTh", [P, KT, SEQ], F32R, 112 * K)
    hTl = at("hTl", [P, KT, SEQ], F32R, 128 * K)
    A = 144 * K
    memraw = at("memraw", [P, TOK, D], F32, 112 * K)
    memTh = at("memTh", [P, KT, SEQ], F32R, A)
    memTl = at("memTl", [P, KT, SEQ], F32R, A + 16 * K)
    qkT = at("qkT", [P, 24, SEQ], F32, A)
    vAB = at("vAB", [P, TOK, 8, HD], F32, A + 24 * K)
    kcT = at("kcT", [P, C_HEADS, SEQ], F32, A + 32 * K)
    vC = at("vC", [P, TOK, C_HEADS, HD], F32, A + 36 * K)
    hank = at("hank", [P, 2, 384], F32, A + 40 * K)
    rope = at("rope", [P, 2, TOK, HD], F32, A + 43 * K)
    stage = at("stage", [P, TOK, 512], F32, A + 45 * K)
    stage2 = at("stage2", [P, TOK, 512], F32, A + 49 * K)
    fold = at("fold", [P, 2, 4, SEQ], F32, A + 45 * K)
    probs = at("probs", [P, TOK, SEQ], F32, A + 45 * K)
    probsT = at("probsT", [P, TOK, SEQ], F32, A + 49 * K)
    gst = at("gst", [P, TOK, 512], F32, A + 53 * K)
    obuf = at("obuf", [P, TOK, HEADS, HD], F32, XO)
    tabs = at("tabs", [32, 6], F32, A + 38 * K)
    oneh = at("oneh", [32, 512], F32, A + 32 * K)
    dmask = at("dmask", [6, 512], F32, A + 34 * K)
    bvec = at("bvec", [6, 512], F32, A + 36 * K)
    oTh = at("oTh", [P, 12, SEQ], F32R, A)
    oTl = at("oTl", [P, 12, SEQ], F32R, A + 12 * K)
    merged = at("merged", [P, TOK, D], F32, A + 24 * K)
    gl = at("gl", [P, 3, TOK, 512], F32, XO)
    mt0 = at("mt0", [P, TOK, 512], F32, A + 40 * K)
    mt1 = at("mt1", [P, TOK, 512], F32, A + 53 * K)
    xn = at("xn", [P, TOK, D], F32, A + 24 * K)
    adaraw = at("adaraw", [P, 2, 2, 1024], F32, A)
    adaacc = at("adaacc", [P, 1024], F32, A + 16 * K)
    modrow = at("modrow", [1, 1024], F32, A + 20 * K)
    gact = at("gact", [P, TOK, 512], F32, A + 40 * K)
    fact = at("fact", [P, TOK, 512], F32, A + 53 * K)
    factTh = at("factTh", [P, 4, SEQ], F32R, A + 45 * K)
    factTl = at("factTl", [P, 4, SEQ], F32R, A + 49 * K)
    qkT2 = at("qkT2", [P, 16, SEQ], F32, A)
    v2 = at("v2", [P, TOK, LRU], F32, A + 16 * K)
    lxT = at("lxT", [P, 8, 260], F32, A + 24 * K)
    dec = at("dec", [P, 8, SEQ], F32, A + 24 * K)
    gyT = at("gyT", [P, 8, SEQ], F32, A + 33 * K)
    istage = at("istage", [P, 2, SEQ], F32, A + 41 * K)
    wf = at("wf", [P, KT, 8], F32, A + 43 * K)
    wfh = at("wfh", [P, KT, 8], F32R, A + 43 * K + 512)
    wfl = at("wfl", [P, KT, 8], F32R, A + 44 * K)
    lwx = at("lwx", [P, 8, P], F32, A + 49 * K)
    lwa = at("lwa", [P, 8, P], F32, A + 53 * K)
    uT = at("uT", [P, 8, SEQ], F32, XO)
    bx = at("bx", [P, 8, SEQ], F32, XO + 8 * K)
    sel = at("sel", [8, 8, SEQ], F32, A + 24 * K)
    probs2 = at("probs2", [P, 2, TOK, SEQ], F32, A + 41 * K)
    probsT2 = at("probsT2", [P, 2, TOK, SEQ], F32, A + 53 * K)
    att2 = at("att2", [P, TOK, H2, HD], F32, XO)
    lsq = at("lsq", [P, 8, SEQ], F32, XO + 8 * K)
    lgate = at("lgate", [8, 4, SEQ], F32, A + 49 * K)
    ga1 = at("ga1", [P, D], F32, A)
    mt2 = at("mt2", [P, TOK, 512], F32, A + 8 * K)
    lrs = at("lrs", [P, 2, SEQ], F32, A + 12 * K)
    pqT = at("pqT", [P, 16, SEQ], F32, A)
    keysT = at("keysT", [P, 16, P], F32, A + 16 * K)
    sc = at("sc", [P, TOK, 16, N_KEYS], F32, A + 24 * K)
    cand = at("cand", [P, 8, 256], F32, A)
    work = at("work", [P, 8, 256], F32, A + 8 * K)
    work2 = at("work2", [P, 8, 256], F32, A + 16 * K)
    top = at("top", [P, TOK, 16, TOPK], F32, A + 40 * K)
    topi = at("topi", [P, TOK, 16, TOPK], U32, A + 42 * K)
    topf = at("topf", [P, TOK, 16, TOPK], F32, A + 44 * K)
    picks = at("picks", [P, TOK, 3, 8, TOPK], F32, A + 46 * K)
    best = at("best", [P, TOK, 8, TOPK], F32, A + 49 * K)
    besti = at("besti", [P, TOK, 8, TOPK], U32, A + 50 * K)
    divi = at("divi", [P, 2, 8, TOPK], U32, A + 51 * K)
    divf = at("divf", [P, 2, 8, TOPK], F32, A + 52 * K)
    picksT = at("picksT", [P, 3, SEQ], F32, A + 40 * K)
    gacc = at("gacc", [P, TOK, 512], F32, A + 53 * K)
    ohA = at("ohA", [P, 2, 16, P], F32, A)
    ohB = at("ohB", [P, 2, 16, P], F32, A + 16 * K)
    wst = [at("wst0", [P, 16, P], F32, A + 32 * K), at("wst1", [P, 16, P], F32, A + 45 * K)]
    y = at("y", [P, TOK, D], F32, A)
    wc = at("wc", [P, TOK, 512], F32, A + 16 * K)
    pact = at("pact", [P, TOK, 512], F32, A + 24 * K)
    pactTh = at("pactTh", [P, 4, SEQ], F32R, A + 28 * K)
    pactTl = at("pactTl", [P, 4, SEQ], F32R, A + 32 * K)
    ga2 = at("ga2", [P, D], F32, A + 40 * K)
    gfin = at("gfin", [P, D], F32, A + 16 * K)

    CO = A + 57 * K
    ident = at("ident", [P, P], F32, CO)
    anti = at("anti", [P, P], F32, CO + 512)
    ones = at("ones", [P, P], F32, CO + 1 * K)
    iota = at("iota", [P, P], F32, CO + 1 * K + 512)
    cols = at("cols", [P, NCOLS], F32, CO + 2 * K)
    gb = at("gb", [P, 2, HD], F32, CO + 3 * K)
    causal = at("causal", [P, 384], F32, CO + 4 * K)
    small_at = [CO + 5 * K + 512]

    def small(name, shape, dt=F32):
        words = int(np.prod(shape[1:]))
        h = at(name, shape, dt, small_at[0])
        small_at[0] += -(-words * 4 // 32) * 32
        return h

    ssum = small("ssum", [P, TOK])
    rstd = small("rstd", [P, 2, TOK])
    hss = small("hss", [P, 3, 8])
    fs = small("fs", [P, TOK, 8])
    cs = small("cs", [P, 16])
    modT = small("modT", [P, 4, 16])
    gmod = small("gmod", [P, 16])
    lam = small("lam", [P, 4, 8])
    spn = small("spn", [P, 2, 8])
    negm = small("negm", [P, TOK, HEADS])
    lsum = small("lsum", [P, TOK, HEADS])
    fac = small("fac", [P, TOK, HEADS])
    cmb = small("cmb", [P, 2, TOK, 6])
    cmx = small("cmx", [P, 2, TOK, 2])
    assert base0 + small_at[0] <= 229368, small_at
    pk = at("pk", [P, 3, 16], F32, CO + 4 * K)
    wsm = at("wsm", [P, TOK, 8, 2], F32, CO + 4 * K + 256)

    ps = nc.alloc_psum_tensor("ps", [P, 8, 512], F32)

    def pair(b):
        return ps[:, b:b + 2, :]

    def quarters(b):
        return ps[:, b:b + 2, :].rearrange("p b (k t) -> p (b k) t", t=SEQ)

    def fold_bank(f):
        return 4 if FOLD_M <= f < FOLD_FFN else 4 + 2 * (f % 2)

    bias_d = nc.dram_tensor("bias_scratch", [6, 512], F32, kind="Internal").ap()
    gates_d = nc.dram_tensor("gates_scratch", [12, P, TOK * 512], F32, kind="Internal").ap()
    mod_d = nc.dram_tensor("mod_scratch", [ADA], F32, kind="Internal").ap()
    x_d = nc.dram_tensor("x_scratch", [P, TOK * D], F32, kind="Internal").ap()
    w_d = nc.dram_tensor("w_scratch", [SEQ, EXPERTS], F32, kind="Internal").ap()

    sems = {}

    def sem(name):
        if name not in sems:
            sems[name] = nc.alloc_semaphore(name)
        return sems[name]

    raw_in = [sem(f"raw_in{s}") for s in range(4)]
    hi_done, lo_done, piece_used = sem("hi_done"), sem("lo_done"), sem("piece_used")
    head_quads = [0, 2, 3, 4, 5, 6, 7]
    ADA_IN = [sem("ada_in0"), sem("ada_in1")]

    with nc.Block() as block:

        @block.sync
        def _(sp):
            sp.dma_start(memraw[:], t["mem"].rearrange("(k p) d -> p k d", p=P)).then_inc(sem("mem_in"), 16)
            sp.dma_start(x[:], t["x"].rearrange("(k p) d -> p k d", p=P)).then_inc(sem("x_in"), 16)

            def load(src, q, n):
                for s in range(4):
                    if not isinstance(q, int) or q >= 1:
                        sp.wait_ge(lo_done, 4 * q + (s - 3))
                    sp.dma_start(raw[:, s, :], src[4 * n + s]).then_inc(raw_in[s], 16)

            load(t["w_first"], 0, 0)
            with sp.Fori(1, Q_BRANCH) as n:
                load(t["w_first"], n, n)
            with sp.Fori(0, Q_FFN - Q_BRANCH) as n:
                load(t["w_merge"], n + Q_BRANCH, n)
            with sp.Fori(0, 3 * FF_GROUPS) as n:
                load(t["w_ffn"], n + Q_FFN, n)
            with sp.Fori(0, Q_PEER - Q_IN2) as n:
                load(t["w_second"], n + Q_IN2, n)
            with sp.Fori(0, 2 * PEER_GROUPS) as n:
                load(t["w_peer"], n + Q_PEER, n)
            sp.wait_ge(sem("final"), 2)
            sp.dma_start(t["out"].rearrange("(k p) d -> p k d", p=P), x[:]).then_inc(sem("out_st"), 16)
            sp.wait_ge(sem("out_st"), 16)

        @block.gpsimd
        def _(pool):
            for dst, src in ((ident, "ident"), (anti, "anti"), (cols, "cols"), (cs, "c"), (iota, "iota"),
                             (causal, "causal"), (tabs, "rel_bias"), (oneh, "oneh"), (dmask, "dmask"),
                             (rope, "rope")):
                pool.dma_start(dst[:], t[src]).then_inc(sem("const_in"), 16)
            pool.dma_start(gb[:, 0, :], t["g_qb"].to_broadcast([P, HD])).then_inc(sem("const_in"), 16)
            pool.dma_start(gb[:, 1, :], t["g_kb"].to_broadcast([P, HD])).then_inc(sem("const_in"), 16)
            pool.wait_ge(sem("bvec"), 1)
            pool.dma_start(bias_d, bvec[:]).then_inc(sem("bias_st"), 16)
            pool.wait_ge(sem("bias_st"), 16)

            def load_hankel(h):
                if h >= 2:
                    pool.wait_ge(sem("att_s"), h - 1)
                src = bass.AP(bias_d.tensor, h * 512, [[1, P], [1, 384]])
                pool.dma_start(hank[:, h % 2, :], src).then_inc(sem(f"hank_in{h % 2}"), 16)

            load_hankel(0)
            load_hankel(1)

            def store_gates(c):
                pool.wait_ge(sem("chunk_out"), Q_GATES + c + 1)
                pool.dma_start(gates_d[c], gst[:].rearrange("p k n -> p (k n)")).then_inc(sem("gate_st"), 16)

            for n in range(48):
                if n % 3 == 0 and n // 3 + 2 < A_HEADS:
                    load_hankel(n // 3 + 2)
                if n % 4 == 3:
                    store_gates(n // 4)
            pool.wait_ge(sem("gate_st"), 16 * 12)
            for j in range(4):
                if j == 0:
                    pool.wait_ge(sem("fold_tr"), FOLD_M)
                else:
                    pool.wait_ge(sem("merge"), j)
                pool.dma_start(gl[:].rearrange("p b k n -> p b (k n)"),
                               gates_d[j:12:4].rearrange("b p n -> p b n")).then_inc(sem("gl_in"), 16)
            pool.wait_ge(sem("merge"), 4)
            pool.dma_start(x[:], t["x"].rearrange("(k p) d -> p k d", p=P)).then_inc(sem("x_back"), 16)

            pool.wait_ge(piece_used, 4 * Q_WO)

            def ada_piece(a, j, first):
                if not first:
                    pool.wait_ge(sem("ada_used"), 8 * a + (j - 1))
                pool.dma_start(adaraw[:, j % 2, :, :].rearrange("p k n -> p (k n)"), t["w_ada"][8 * a + j])\
                    .then_inc(ADA_IN[j % 2], 16)

            def ada_row_in(a):
                pool.dma_start(modrow[:], t["b_ada"][a]).then_inc(sem("bada_in"), 16)

            def ada_row_out(a):
                pool.wait_ge(sem("modrow"), 2 * a)
                pool.dma_start(mod_d.rearrange("(a o n) -> a o n", o=1, n=1024)[a - 1],
                               modrow[0:1, :]).then_inc(sem("mod_st"), 16)
                pool.wait_ge(sem("mod_st"), 16 * a)

            for j in range(8):
                ada_piece(0, j, j < 2)
                if j == 3:
                    ada_row_in(0)
            with pool.Fori(1, ADA_SPLITS) as a:
                for j in range(8):
                    ada_piece(a, j, False)
                    if j == 3:
                        ada_row_out(a)
                        ada_row_in(a)
            ada_row_out(ADA_SPLITS)
            for k, part in enumerate((0, 1, 3, 4)):
                with nc.allow_non_contiguous_dma(reason="a column of the modulation for each partition"):
                    pool.dma_start(modT[:, k, :], mod_d[part * D:(part + 1) * D].rearrange("(k p) -> p k", p=P))\
                        .then_inc(sem("modT_in"), 16)
            pool.wait_ge(sem("xn_done"), 2 * 4)
            pool.dma_start(x_d, x[:].rearrange("p k n -> p (k n)")).then_inc(sem("x_st"), 16)
            pool.dma_start(wf[:], t["w_f"]).then_inc(sem("wf_in"), 16)
            pool.dma_start(lwa[:], t["lru_w_a"]).then_inc(sem("lw_in"), 16)
            pool.wait_ge(sem("fold_lo"), FOLD_ATT)
            pool.dma_start(lwx[:], t["lru_w_x"]).then_inc(sem("lw_in"), 16)
            pool.wait_ge(sem("scan"), 8)
            pool.dma_start(sel[:], t["sel"]).then_inc(sem("sel_in"), 16)
            pool.wait_ge(sem("fold_tr"), FOLD_LRU)
            pool.wait_ge(sem("lru_ms"), 1)
            pool.dma_start(x[:].rearrange("p k n -> p (k n)"), x_d).then_inc(sem("x_back"), 16)
            pool.dma_start(ga1[:], bass.AP(mod_d.tensor, 2 * D, [[0, P], [1, D]])).then_inc(sem("ga1_in"), 16)
            pool.wait_ge(sem("xn_done"), 2 * 5)
            pool.dma_start(keysT[:], t["keys"]).then_inc(sem("keys_in"), 16)
            def store_w(n, u):
                pool.wait_ge(sem("wst"), n + 1)
                pool.dma_start(w_d[bass.ds(n * 16, 16) if not isinstance(n, int) else slice(16 * n, 16 * n + 16)]
                               .rearrange("t (a b) -> a t b", b=N_KEYS), wst[u][:]).then_inc(sem(f"w_st{u}"), 16)

            with pool.Fori(0, SEQ // 32) as n:
                for u in range(2):
                    store_w(2 * n + u, u)
            for u in range(2):
                pool.wait_ge(sem(f"w_st{u}"), 16 * (SEQ // 32))
            pool.dma_start(wc[:], w_d[:, 0:512].rearrange("(k p) n -> p k n", p=P)).then_inc(sem("wc_in"), 16)
            with pool.Fori(1, PEER_GROUPS) as g:
                pool.wait_ge(sem("pmul"), g)
                pool.dma_start(wc[:], w_d[:, bass.ds(g * 512, 512)].rearrange("(k p) n -> p k n", p=P))\
                    .then_inc(sem("wc_in"), 16)
            pool.wait_ge(sem("pmul"), PEER_GROUPS)
            pool.dma_start(ga2[:], bass.AP(mod_d.tensor, 5 * D, [[0, P], [1, D]])).then_inc(sem("ga2_in"), 16)
            pool.dma_start(gfin[:], t["g_final"].to_broadcast([P, D])).then_inc(sem("gfin_in"), 16)

        @block.scalar
        def _(act):
            a_seq = [0]

            def round_piece(q, s):
                act.wait_ge(raw_in[s], 16 * q + 16)
                if not isinstance(q, int) or q >= 1:
                    act.wait_ge(piece_used, 4 * q + (s - 3))
                nc.scalar.copy(hi[:, s, :], raw[:, s, :]).then_inc(hi_done, 1)

            def norm(u, src):
                dst = src if u < 2 else xn
                for k in range(TOK):
                    nc.scalar.activation(fold[:].rearrange("p a b n -> p (a b n)"), src[:, k, :], ACT.Square,
                                         accum_out=ssum[:, k:k + 1]).then_inc(sem("sq_done"), 1)
                    act.wait_ge(sem("sq_done"), 2 * u + k + 1)
                act.wait_ge(sem("ms_done"), u + 1)
                nc.scalar.activation(rstd[:, 0, :], ssum[:], ACT.Sqrt).then_inc(sem("root_done"), 1)
                act.wait_ge(sem("rstd_done"), u + 1)
                for k in range(TOK):
                    nc.scalar.activation(dst[:, k, :], src[:, k, :], ACT.Copy, scale=rstd[:, 1, k:k + 1])\
                        .then_inc(sem("xn_done"), 1)

            def fold_hi(f, dst, at0):
                act.wait_ge(sem("fold_t"), f + 1)
                nc.scalar.copy(dst[:, at0:at0 + 4, :], fold[:, f % 2]).then_inc(sem("fold_hi"), 1)

            act.wait_ge(sem("mem_in"), 16)
            norm(0, memraw)
            for f in range(4):
                fold_hi(FOLD_MEM + f, memTh, 4 * f)
            for s in range(4):
                round_piece(0, s)
            act.wait_ge(sem("x_in"), 16)
            act.wait_ge(sem("fold_lo"), FOLD_X)
            norm(1, x)
            for f in range(4):
                fold_hi(FOLD_X + f, hTh, 4 * f)
            for q in range(Q_GATES):
                for s in range(4):
                    round_piece(q + 1, s)
                act.wait_ge(piece_used, 4 * q + 4)
                if q in head_quads:
                    n = head_quads.index(q)
                    if n == 0:
                        act.wait_ge(sem("fold_lo"), FOLD_O)
                    else:
                        act.wait_ge(sem("head_tr"), n)
                    nc.scalar.copy(stage[:], pair(2 * (q % 2))).then_inc(sem("chunk_out"), 1)
                    act.wait_ge(sem("head_ms"), n + 1)
                    nc.scalar.activation(hss[:, 1, :], hss[:, 0, :], ACT.Sqrt).then_inc(sem("head_root"), 1)
                else:
                    if q == 1:
                        act.wait_ge(sem("bias_st"), 16)
                    dst = vC[:] if q == 1 else vAB[:, :, 4 * (q - 8):4 * (q - 8) + 4, :]
                    src = pair(2 * (q % 2)).rearrange("p k (h d) -> p k h d", d=HD)
                    nc.scalar.copy(dst, src).then_inc(sem("chunk_out"), 1)
            for n in range(48):
                q, s = divmod(4 * Q_GATES + n, 4)
                round_piece(q + 1, s)
                if s == 3:
                    c = q - Q_GATES
                    if c >= 1:
                        act.wait_ge(sem("gate_st"), 16 * c)
                    act.wait_ge(piece_used, 4 * q + 4)
                    nc.scalar.activation(gst[:], pair(2 * (q % 2)), ACT.Tanh, scale=0.5)\
                        .then_inc(sem("chunk_out"), 1)
                if n % 3 == 0:
                    h = n // 3
                    act.wait_ge(sem("att_m"), h + 1)
                    if h >= 1:
                        act.wait_ge(sem("att_t"), h)
                    for k in range(TOK):
                        nc.scalar.activation(probs[:, k, :], ps[:, 4, SEQ * k:SEQ * k + SEQ], ACT.Exp,
                                             bias=negm[:, k, h:h + 1], accum_out=lsum[:, k, h:h + 1])\
                            .then_inc(sem("att_e"), 1)
            act.wait_ge(sem("cmb_d"), 1)
            nc.scalar.activation(cmb[:, 1], cmb[:, 0], ACT.Exp).then_inc(sem("cmb_e"), 1)
            for f in range(3):
                fold_hi(FOLD_O + f, oTh, 4 * f)
            for n in range(12):
                q, s = divmod(4 * Q_BRANCH + n, 4)
                round_piece(q + 1, s)
                if n % 3 == 2 and n >= 5:
                    fold_hi(FOLD_M + n // 3 - 1, hTh, 4 * (n // 3 - 1))
            fold_hi(FOLD_M + 3, hTh, 12)
            nc.scalar.activation(cs[:], cs[:], ACT.Silu).then_inc(sem("cs_done"), 1)
            for n in range(16):
                q, s = divmod(4 * Q_WO + n, 4)
                round_piece(q + 1, s)
            act.wait_ge(sem("x_ready"), 1)
            norm(2, x)
            for f in range(4):
                fold_hi(FOLD_FFN + f, hTh, 4 * f)

            def silu(g):
                act.wait_ge(piece_used, 4 * Q_FFN + 4 if isinstance(g, int) else 12 * g + 4 * Q_FFN)
                if not isinstance(g, int):
                    act.wait_ge(sem("fmul"), g)
                nc.scalar.activation(gact[:], pair(0), ACT.Silu).then_inc(sem("silu"), 1)

            def gate_up_down(b, j):
                round_piece(3 * b + (Q_FFN + 2 + j // 4 + 1), j % 4)

            for j in range(8):
                q, s = divmod(4 * Q_FFN + j, 4)
                round_piece(q + 1, s)
                if j == 3:
                    silu(0)

            def ffn_hi(b):
                act.wait_ge(sem("ffn_tr"), b + 1)
                nc.scalar.copy(factTh[:], quarters(4)).then_inc(sem("ffn_hi"), 1)

            with act.Fori(0, FF_GROUPS - 1) as b:
                for j in range(12):
                    gate_up_down(b, j)
                    if j == 1:
                        ffn_hi(b)
                    if j == 3:
                        silu(b + 1)
            ffn_hi(FF_GROUPS - 1)
            for j in range(4):
                round_piece(Q_IN2, j)
            act.wait_ge(sem("x_ready"), 2)
            norm(3, x)
            for f in range(4):
                fold_hi(FOLD_MIX2 + f, hTh, 4 * f)
            act.wait_ge(sem("wf_in"), 16)
            nc.scalar.copy(wfh[:], wf[:]).then_inc(sem("wfh"), 1)
            act.wait_ge(sem("lam_n"), 1)
            nc.scalar.activation(lam[:, 1, :], lam[:, 0, :], ACT.Exp).then_inc(sem("lam_e"), 1)

            for c in range(10):
                q = Q_IN2 + c
                for s in range(4):
                    round_piece(q + 1, s)
                act.wait_ge(piece_used, 4 * q + 4)
                if c < 8:
                    if c >= 1:
                        act.wait_ge(sem("in_tr"), c)
                    else:
                        act.wait_ge(sem("fold_lo"), FOLD_ATT)
                    nc.scalar.copy(stage[:], pair(2 * (c % 2))).then_inc(sem("in_out"), 1)
                else:
                    nc.scalar.copy(v2[:, :, 512 * (c - 8):512 * (c - 8) + 512], pair(2 * (c % 2)))\
                        .then_inc(sem("in_out"), 1)
                if c in (3, 4):
                    n = c - 3
                    act.wait_ge(sem("in_tr"), 3 + n)
                    nc.scalar.activation(gyT[:, 4 * n:4 * n + 4, :], quarters(4), ACT.Gelu_apprx_tanh)\
                        .then_inc(sem("gy_T"), 1)
                if c == 4:
                    for n in range(8):
                        act.wait_ge(sem("ri"), n + 1)
                        nc.scalar.activation(uT[:, n, :], ps[:, 6 + n % 2, 0:SEQ], ACT.Sigmoid,
                                             bias=cols[:, C_BA + n:C_BA + n + 1]).then_inc(sem("r_out"), 1)
                        if n >= 2:
                            act.wait_ge(sem("i_used"), n - 1)
                        nc.scalar.activation(istage[:, n % 2, :], ps[:, 6 + n % 2, SEQ:2 * SEQ], ACT.Sigmoid,
                                             bias=cols[:, C_BX + n:C_BX + n + 1]).then_inc(sem("i_out"), 1)
                    act.wait_ge(sem("sp_done"), 1)
                    act.wait_ge(sem("conv"), 8)
                    act.wait_ge(sem("r_out"), 8)
                    for n in range(8):
                        nc.scalar.activation(dec[:, n, :], uT[:, n, :], ACT.Exp, scale=spn[:, 0, n:n + 1])\
                            .then_inc(sem("dec"), 1)
                        nc.scalar.activation(uT[:, n, :], uT[:, n, :], ACT.Tanh, scale=spn[:, 1, n:n + 1])\
                            .then_inc(sem("tanh"), 1)
                if c == 6:
                    act.wait_ge(sem("tanh"), 8)
                    nc.scalar.activation(uT[:], uT[:], ACT.Sqrt).then_inc(sem("root2"), 1)
            act.wait_ge(sem("lg_abs"), 1)
            nc.scalar.activation(lgate[:, 1, :], lgate[:, 1, :], ACT.Exp, scale=-1.0).then_inc(sem("lg_exp"), 1)
            for h in range(H2):
                act.wait_ge(sem("m2"), h + 1)
                if h >= 2:
                    act.wait_ge(sem("t2"), h - 1)
                for k in range(TOK):
                    nc.scalar.activation(probs2[:, h % 2, k, :], ps[:, h % 2, SEQ * k:SEQ * k + SEQ], ACT.Exp,
                                         bias=negm[:, k, h:h + 1], accum_out=lsum[:, k, h:h + 1])\
                        .then_inc(sem("e2"), 1)
            act.wait_ge(sem("att2_n"), 1)
            for k in range(TOK):
                nc.scalar.activation(stage2[:].rearrange("p a b -> p (a b)"), att2[:, k].rearrange("p h d -> p (h d)"),
                                     ACT.Square, accum_out=ssum[:, k:k + 1]).then_inc(sem("ssq2"), 1)
                act.wait_ge(sem("ssq2"), k + 1)
            act.wait_ge(sem("ms2"), 1)
            nc.scalar.activation(rstd[:, 0, :], ssum[:], ACT.Sqrt).then_inc(sem("ms2_root"), 1)
            act.wait_ge(sem("rstd2"), 1)
            for k in range(TOK):
                nc.scalar.activation(att2[:, k], att2[:, k], ACT.Copy, scale=rstd[:, 1, k:k + 1])\
                    .then_inc(sem("att2_s"), 1)
            for f in range(2):
                fold_hi(FOLD_ATT + f, hTh, 4 * f)
            act.wait_ge(sem("lru_ms"), 1)
            nc.scalar.activation(lrs[:, 0, :], lrs[:, 0, :], ACT.Sqrt).then_inc(sem("lru_root"), 1)
            for f in range(2):
                fold_hi(FOLD_LRU + f, hTh, 8 + 4 * f)
            for c in range(4):
                for s in range(4):
                    round_piece(Q_OUT2 + c + 1, s)
            act.wait_ge(sem("x_ready"), 3)
            norm(4, x)
            for f in range(4):
                fold_hi(FOLD_PEER + f, hTh, 4 * f)
            for c in range(4):
                q = Q_PQ + c
                for s in range(4):
                    round_piece(q + 1, s)
                act.wait_ge(piece_used, 4 * q + 4)
                if c >= 1:
                    act.wait_ge(sem("pq_tr"), c)
                else:
                    act.wait_ge(sem("fold_lo"), FOLD_PEER + 4)
                nc.scalar.copy(stage[:], pair(2 * (c % 2))).then_inc(sem("pq_out"), 1)
            def gelu(g):
                act.wait_ge(piece_used, 4 * Q_PEER + 4 if isinstance(g, int) else 8 * g + 4 * Q_PEER)
                if not isinstance(g, int):
                    act.wait_ge(sem("pmul"), g)
                nc.scalar.activation(gacc[:], pair(0), ACT.Gelu_apprx_tanh).then_inc(sem("gelu"), 1)

            for s in range(4):
                round_piece(Q_PEER + 1, s)
            gelu(0)
            act.wait_ge(sem("wexp_in"), 1)
            nc.scalar.activation(picks[:, :, 2], picks[:, :, 2], ACT.Exp).then_inc(sem("wexp"), 1)

            def wst_out(n, u):
                act.wait_ge(sem("wmm"), n + 1)
                nc.scalar.copy(wst[u][:].rearrange("p t b -> p (t b)"),
                               ps[:, 4 * u:4 * u + 4, :].rearrange("p b n -> p (b n)")).then_inc(sem("wst"), 1)

            wst_out(0, 0)
            wst_out(1, 1)
            with act.Fori(1, SEQ // 32) as n:
                for u in range(2):
                    act.wait_ge(sem("wmm"), 2 * n + (u + 1))
                    act.wait_ge(sem(f"w_st{u}"), 16 * n)
                    nc.scalar.copy(wst[u][:].rearrange("p t b -> p (t b)"),
                                   ps[:, 4 * u:4 * u + 4, :].rearrange("p b n -> p (b n)")).then_inc(sem("wst"), 1)

            def peer_hi(b):
                act.wait_ge(sem("peer_tr"), b + 1)
                nc.scalar.copy(pactTh[:], quarters(4)).then_inc(sem("peer_hi"), 1)

            with act.Fori(0, PEER_GROUPS - 1) as b:
                for j in range(8):
                    round_piece(2 * b + (Q_PEER + 1 + j // 4 + 1), j % 4)
                    if j == 1:
                        peer_hi(b)
                    if j == 3:
                        gelu(b + 1)
            peer_hi(PEER_GROUPS - 1)
            act.wait_ge(sem("x_ready"), 4)
            for k in range(TOK):
                nc.scalar.activation(y[:, k, :], x[:, k, :], ACT.Square, accum_out=ssum[:, k:k + 1])\
                    .then_inc(sem("ssq3"), 1)
            act.wait_ge(sem("ms3"), 1)
            nc.scalar.activation(rstd[:, 0, :], ssum[:], ACT.Sqrt).then_inc(sem("ms3_root"), 1)

        @block.vector
        def _(dve):
            seq = [0]

            def step(ins):
                seq[0] += 1
                ins.then_inc(sem("dve_seq"), 1)
                dve.wait_ge(sem("dve_seq"), seq[0])

            V = nc.vector

            def rest_piece(q, s):
                dve.wait_ge(hi_done, 4 * q + (s + 1))
                if not isinstance(q, int) or q >= 1:
                    dve.wait_ge(piece_used, 4 * q + (s - 3))
                V.tensor_tensor(lo[:, s, :], raw[:, s, :], hi[:, s, :].bitcast(F32), ALU.subtract).then_inc(lo_done, 1)

            def rest_quad(q):
                for s in range(4):
                    rest_piece(q, s)

            def fold_lo(f, dst, at0):
                dve.wait_ge(sem("fold_hi"), f + 1)
                V.tensor_tensor(dst[0][:, at0:at0 + 4, :], fold[:, f % 2], dst[1][:, at0:at0 + 4, :].bitcast(F32),
                                ALU.subtract).then_inc(sem("fold_lo"), 1)

            def fold_ready(f, turned):
                if turned is not None:
                    dve.wait_ge(sem("fold_tr"), turned)
                if f >= 2:
                    dve.wait_ge(sem("fold_hi"), f - 1)
                    dve.wait_ge(sem("fold_lo"), f - 1)

            def norm(u, f0, scale_at, shift, scale_tile=None):
                dve.wait_ge(sem("sq_done"), 2 * u + 2)
                V.tensor_scalar(ssum[:], ssum[:], 1.0 / D, EPS, ALU.mult, ALU.add).then_inc(sem("ms_done"), 1)
                dve.wait_ge(sem("root_done"), u + 1)
                V.reciprocal(rstd[:, 1, :], rstd[:, 0, :]).then_inc(sem("rstd_done"), 1)
                src = cols if scale_tile is None else scale_tile
                th, tl = (memTh, memTl) if u == 0 else (hTh, hTl)
                for g in range(4):
                    f = f0 + g
                    turned = f + 1 if f < FOLD_LRU else f - 1
                    fold_ready(f, turned)
                    for k in range(4):
                        kt = 4 * g + k
                        col = src[:, scale_at + kt:scale_at + kt + 1]
                        if shift is None:
                            ins = V.tensor_scalar(fold[:, f % 2, k], quarters(fold_bank(f))[:, k], col, None, ALU.mult)
                        else:
                            ins = V.tensor_scalar(fold[:, f % 2, k], quarters(fold_bank(f))[:, k], col,
                                                  modT[:, shift, kt:kt + 1], ALU.mult, ALU.add)
                    ins.then_inc(sem("fold_t"), 1)
                    if g >= 1:
                        fold_lo(f - 1, (tl, th), 4 * g - 4)
                fold_lo(f0 + 3, (tl, th), 12)

            V.memset(ones[:], 1.0).then_inc(sem("ones"), 1)
            dve.wait_ge(sem("bias_mm"), 1)
            V.tensor_tensor(bvec[:], ps[0:6, 7, :], dmask[:], ALU.add).then_inc(sem("bvec"), 1)
            dve.wait_ge(sem("const_in"), 16 * 12)
            norm(0, FOLD_MEM, C_GMEM, None)
            rest_quad(0)
            norm(1, FOLD_X, C_GMIX, None)

            def head_norm(q):
                n = head_quads.index(q)
                dve.wait_ge(sem("chunk_out"), q + 1)
                h8 = stage[:].rearrange("p k (h d) -> p (k h) d", d=HD)
                s8 = stage2[:].rearrange("p k (h d) -> p (k h) d", d=HD)
                step(V.tensor_tensor(s8, h8, h8, ALU.mult))
                step(V.tensor_reduce(hss[:, 0, :], s8, AX.X, ALU.add))
                V.tensor_scalar(hss[:, 0, :], hss[:, 0, :], 1.0 / HD, EPS, ALU.mult, ALU.add)\
                    .then_inc(sem("head_ms"), 1)
                dve.wait_ge(sem("head_root"), n + 1)
                step(V.reciprocal(hss[:, 2, :], hss[:, 1, :]))
                rs = hss[:, 2, :].rearrange("p (h o) -> p h o", o=1).to_broadcast([P, 8, HD])
                if q < 6:
                    V.tensor_tensor(h8, h8, rs, ALU.mult).then_inc(sem("head_n"), 1)
                    return
                step(V.tensor_tensor(h8, h8, rs, ALU.mult))
                for k in range(TOK):
                    hk = stage[:, k, :].rearrange("p (h d) -> p h d", d=HD)
                    sk = stage2[:, k, :].rearrange("p (h d) -> p h d", d=HD)
                    runs = [(0, 4, 0)] if q == 6 else [(0, 2, 0), (2, 4, 1)]
                    for a, b, g in runs:
                        gain = gb[:, g, :].rearrange("p (o d) -> p o d", o=1).to_broadcast([P, b - a, HD])
                        step(V.tensor_tensor(hk[:, a:b], hk[:, a:b], gain, ALU.mult))
                    sin = rope[:, 1, k, :].rearrange("p (o d e) -> p o d e", o=1, e=2)
                    cos = rope[:, 0, k, :].rearrange("p (o d) -> p o d", o=1).to_broadcast([P, 4, HD])
                    h4 = stage[:, k, :].rearrange("p (h d e) -> p h d e", d=HD // 2, e=2)
                    s4 = stage2[:, k, :].rearrange("p (h d e) -> p h d e", d=HD // 2, e=2)
                    for e in range(2):
                        step(V.tensor_tensor(s4[:, :, :, e], h4[:, :, :, 1 - e],
                                             sin[:, :, :, e].to_broadcast([P, 4, HD // 2]), ALU.mult))
                    step(V.tensor_tensor(hk, hk, cos, ALU.mult))
                    ins = V.tensor_tensor(hk, hk, sk, ALU.add)
                ins.then_inc(sem("head_n"), 1)

            def head_out(q):
                n = head_quads.index(q)
                if q == 0:
                    dve.wait_ge(sem("bias_st"), 16)
                dve.wait_ge(sem("head_tr"), n + 1)
                for k in range(4):
                    src = quarters(4)[:, k]
                    if q == 0:
                        ins = V.tensor_scalar(kcT[:, k], src, cols[:, C_HEAD + 16 + k:C_HEAD + 17 + k], None, ALU.mult)
                        continue
                    h = 4 * (q - 2) + k
                    if h < 16:
                        scale = 1.0 if 6 <= h < 12 else SCALE
                        ins = V.tensor_scalar(qkT[:, h], src, cols[:, C_HEAD + h:C_HEAD + h + 1], scale,
                                              ALU.mult, ALU.mult)
                    else:
                        ins = V.tensor_scalar(qkT[:, h], src, SCALE if h < 22 else 1.0, None, ALU.mult)
                ins.then_inc(sem("head_T"), 1)

            dve.wait_ge(sem("const_in"), 16 * 12)
            for q in range(Q_GATES):
                rest_quad(q + 1)
                if q - 1 in head_quads:
                    head_out(q - 1)
                if q in head_quads:
                    head_norm(q)

            for n in range(48):
                q, s = divmod(4 * Q_GATES + n, 4)
                rest_piece(q + 1, s)
                h, part = divmod(n, 3)
                if part == 0:
                    dve.wait_ge(sem("att_s"), h + 1)
                    V.tensor_reduce(negm[:, :, h:h + 1], ps[:, 4, :].rearrange("p (k n) -> p k n", n=SEQ), AX.X,
                                    ALU.max, negate=True).then_inc(sem("att_m"), 1)
                elif part == 1:
                    dve.wait_ge(sem("att_t"), h + 1)
                    V.tensor_copy(probsT[:].rearrange("p k n -> p (k n)"), ps[:, 5, :]).then_inc(sem("att_p"), 1)
                else:
                    dve.wait_ge(sem("att_v"), h + 1)
                    V.tensor_copy(obuf[:, :, h, :], ps[:, 6, 0:SEQ].rearrange("p (k d) -> p k d", d=HD))\
                        .then_inc(sem("att_o"), 1)

            dve.wait_ge(sem("att_e"), 2 * HEADS)
            nA = negm[:, :, 0:6].rearrange("p k (g j) -> p k g j", j=2)
            lA = lsum[:, :, 0:6].rearrange("p k (g j) -> p k g j", j=2)
            d4 = cmb[:, 0].rearrange("p k (g j) -> p k g j", j=2)
            e4 = cmb[:, 1].rearrange("p k (g j) -> p k g j", j=2)
            step(V.tensor_tensor(cmx[:, 0], nA[:, :, 0], nA[:, :, 1], ALU.min))
            step(V.tensor_tensor(cmx[:, 0], cmx[:, 0], nA[:, :, 2], ALU.min))
            for g in range(3):
                ins = V.tensor_tensor(d4[:, :, g], cmx[:, 0], nA[:, :, g], ALU.subtract)
            ins.then_inc(sem("cmb_d"), 1)
            step(V.reciprocal(fac[:, :, 6:16], lsum[:, :, 6:16]))
            dve.wait_ge(sem("cmb_e"), 1)
            step(V.tensor_tensor(d4[:], e4, lA, ALU.mult))
            step(V.tensor_tensor(cmx[:, 0], d4[:, :, 0], d4[:, :, 1], ALU.add))
            step(V.tensor_tensor(cmx[:, 0], cmx[:, 0], d4[:, :, 2], ALU.add))
            step(V.reciprocal(cmx[:, 1], cmx[:, 0]))
            fA = fac[:, :, 0:6].rearrange("p k (g j) -> p k g j", j=2)
            for g in range(3):
                ins = V.tensor_tensor(fA[:, :, g], e4[:, :, g], cmx[:, 1], ALU.mult)
            step(ins)
            o32 = obuf[:].rearrange("p k h d -> p (k h) d")
            step(V.tensor_tensor(o32, o32, fac[:].rearrange("p k (h o) -> p (k h) o", o=1)
                                 .to_broadcast([P, TOK * HEADS, HD]), ALU.mult))
            step(V.tensor_tensor(obuf[:, :, 4:6, :], obuf[:, :, 4:6, :], obuf[:, :, 2:4, :], ALU.add))
            V.tensor_tensor(obuf[:, :, 4:6, :], obuf[:, :, 4:6, :], obuf[:, :, 0:2, :], ALU.add)\
                .then_inc(sem("o_ready"), 1)
            for f in range(FOLD_O, FOLD_M):
                fold_ready(f, f + 1)
                V.tensor_copy(fold[:, f % 2], quarters(fold_bank(f))).then_inc(sem("fold_t"), 1)
                fold_lo(f, (oTl, oTh), 4 * (f - FOLD_O))

            def merge(j):
                dve.wait_ge(sem("gl_in"), 16 * (j + 1))
                dve.wait_ge(piece_used, 4 * Q_BRANCH + 3 * j + 3)
                V.scalar_tensor_tensor(mt0[:], gl[:, 0], 1.0, pair(0), ALU.add, ALU.mult)
                step(V.scalar_tensor_tensor(mt1[:], gl[:, 1], 1.0, pair(2), ALU.add, ALU.mult))
                step(V.tensor_tensor(mt0[:], mt0[:], mt1[:], ALU.add))
                step(V.scalar_tensor_tensor(mt1[:], gl[:, 2], 1.0, pair(6), ALU.add, ALU.mult))
                V.tensor_tensor(merged[:, :, 512 * j:512 * j + 512], mt0[:], mt1[:], ALU.add).then_inc(sem("merge"), 1)

            def fold_merged(j):
                f = FOLD_M + j
                fold_ready(f, f + 1)
                V.tensor_scalar(fold[:, f % 2], quarters(fold_bank(f)), 0.5, None, ALU.mult).then_inc(sem("fold_t"), 1)
                fold_lo(f, (hTl, hTh), 4 * j)

            for n in range(12):
                q, s = divmod(4 * Q_BRANCH + n, 4)
                rest_piece(q + 1, s)
                if n % 3 == 2:
                    merge(n // 3)
                    if n >= 5:
                        fold_merged(n // 3 - 1)
            fold_merged(3)

            def ada_piece(a, j, first):
                dve.wait_ge(ADA_IN[j % 2], 64 * a + 16 * (j // 2 + 1))
                for k in range(2):
                    m = 2 * j + k
                    col = cs[:, m:m + 1]
                    src = adaraw[:, j % 2, k, :]
                    if not (first and m == 0):
                        dve.wait_ge(sem("ada_sum"), 16 * a + m)
                    if m == 0:
                        ins = V.tensor_scalar(adaacc[:], src, col, None, ALU.mult)
                    else:
                        ins = V.scalar_tensor_tensor(adaacc[:], src, col, adaacc[:], ALU.mult, ALU.add)
                    ins.then_inc(sem("ada_sum"), 1)
                dve.wait_ge(sem("ada_sum"), 16 * a + (2 * j + 2))
                dve.sem_inc(sem("ada_used"), 1)

            def ada_row(a, b):
                dve.wait_ge(sem("ada_mm"), a + 1)
                dve.wait_ge(sem("bada_in"), 16 * a + 16)
                for k in range(2):
                    V.tensor_tensor(modrow[0:1, 512 * k:512 * k + 512], ps[0:1, b + k, :],
                                    modrow[0:1, 512 * k:512 * k + 512], ALU.add).then_inc(sem("modrow"), 1)

            dve.wait_ge(sem("cs_done"), 1)
            for n in range(16):
                q, s = divmod(4 * Q_WO + n, 4)
                if s == 3:
                    dve.wait_ge(sem("x_back"), 16)
                    dve.wait_ge(piece_used, 4 * q + 4)
                    c = q - Q_WO
                    xc = x[:, :, 512 * c:512 * c + 512]
                    V.tensor_tensor(xc, xc, pair(2 * (c % 2)), ALU.add).then_inc(sem("wo_out"), 1)
                rest_piece(q + 1, s)
                ada_piece(n // 8, n % 8, n < 8)
                if n % 8 == 7:
                    ada_row(n // 8, 6)
            dve.wait_ge(sem("wo_out"), 4)
            dve.sem_inc(sem("x_ready"), 1)
            norm(2, FOLD_FFN, C_GFFN, None)

            def ffn_mul(g):
                dve.wait_ge(sem("silu"), g + 1)
                dve.wait_ge(piece_used, 4 * Q_FFN + 8 if isinstance(g, int) and g == 0 else 12 * g + (4 * Q_FFN + 4))
                V.tensor_tensor(fact[:], gact[:], pair(2), ALU.mult).then_inc(sem("fmul"), 1)

            def ffn_lo(b):
                dve.wait_ge(sem("ffn_hi"), b + 1)
                V.tensor_tensor(factTl[:], quarters(4), factTh[:].bitcast(F32), ALU.subtract).then_inc(sem("ffn_lo"), 1)

            def ffn_down(b, s, used):
                dve.wait_ge(piece_used, used)
                if not isinstance(b, int):
                    dve.wait_ge(sem("x_sum"), 4 * b + (s + 1))
                xc = x[:, :, 512 * s:512 * s + 512]
                V.tensor_tensor(xc, xc, pair(6 if s % 2 == 0 else 0), ALU.add).then_inc(sem("x_sum"), 1)

            dve.sem_inc(sem("x_sum"), 1)
            for j in range(8):
                q, s = divmod(4 * Q_FFN + j, 4)
                rest_piece(q + 1, s)
            ffn_mul(0)
            with dve.Fori(0, FF_GROUPS - 1) as b:
                for j in range(12):
                    if j >= 8:
                        ffn_down(b, j - 8, 12 * b + (4 * Q_FFN + 8 + j + 1))
                    rest_piece(3 * b + (Q_FFN + 3 + j // 4), j % 4)
                    if j == 1:
                        ffn_lo(b)
                    if j == 7:
                        ffn_mul(b + 1)
                    if 2 <= j <= 9:
                        ada_piece(b + 2, j - 2, False)
                ada_row(b + 2, 4)
            ffn_lo(FF_GROUPS - 1)
            for j in range(4):
                dve.wait_ge(sem("x_sum"), 4 * (FF_GROUPS - 1) + j + 1)
                ffn_down(FF_GROUPS - 1, j, 4 * Q_IN2 - 3 + j)
                rest_piece(Q_IN2, j)
            dve.wait_ge(sem("x_sum"), 4 * FF_GROUPS + 1)
            dve.sem_inc(sem("x_ready"), 1)
            dve.wait_ge(sem("modT_in"), 64)
            step(V.scalar_tensor_tensor(gmod[:], modT[:, 1, :], 1.0, cols[:, C_GMIX2:C_GMIX2 + 16], ALU.add, ALU.mult))
            norm(3, FOLD_MIX2, 0, 0, gmod)
            dve.wait_ge(sem("wfh"), 1)
            V.tensor_tensor(wfl[:], wf[:], wfh[:].bitcast(F32), ALU.subtract).then_inc(sem("wfl"), 1)

            def log1p(out, e, z, z2):
                step(V.tensor_scalar(z2, e, 2.0, None, ALU.add))
                step(V.reciprocal(z2, z2))
                step(V.tensor_tensor(z, e, z2, ALU.mult))
                step(V.tensor_tensor(z2, z, z, ALU.mult))
                step(V.tensor_scalar(out, z2, 2.0 / 17, 2.0 / 15, ALU.mult, ALU.add))
                for k in (13, 11, 9, 7, 5, 3, 1):
                    step(V.tensor_tensor(out, out, z2, ALU.mult))
                    step(V.tensor_scalar(out, out, 2.0 / k, None, ALU.add))
                step(V.tensor_tensor(out, out, z, ALU.mult))

            step(V.tensor_scalar(lam[:, 0, :], cols[:, C_LAM:C_LAM + 8], -1.0, None, ALU.mult))
            V.tensor_tensor(lam[:, 0, :], lam[:, 0, :], cols[:, C_LAM:C_LAM + 8], ALU.min).then_inc(sem("lam_n"), 1)
            dve.wait_ge(sem("lam_e"), 1)
            log1p(lam[:, 2, :], lam[:, 1, :], lam[:, 0, :], lam[:, 3, :])
            step(V.tensor_scalar(lam[:, 0, :], cols[:, C_LAM:C_LAM + 8], -1.0, 0.0, ALU.mult, ALU.max))
            step(V.tensor_tensor(lam[:, 0, :], lam[:, 0, :], lam[:, 2, :], ALU.add))
            V.tensor_scalar(spn[:, 0, :], lam[:, 0, :], -8.0, None, ALU.mult)
            V.tensor_scalar(spn[:, 1, :], lam[:, 0, :], 4.0, None, ALU.mult).then_inc(sem("sp_done"), 1)

            for c in range(10):
                rest_quad(Q_IN2 + c + 1)
                if c == 0:
                    dve.wait_ge(sem("fold_tr"), FOLD_ATT)
                    step(V.memset(lxT[:, :, 0:3], 0.0))
                if c in (1, 2):
                    dve.wait_ge(sem("in_tr"), c)
                    V.tensor_copy(lxT[:, 4 * c - 4:4 * c, 3:3 + SEQ], quarters(4)).then_inc(sem("lx_T"), 1)
                if c == 2:
                    dve.wait_ge(sem("x_st"), 16)
                    dve.wait_ge(sem("lx_T"), 2)
                    for j in range(CONV):
                        for n in range(8):
                            win = lxT[:, n, j:j + SEQ]
                            w = cols[:, C_CONVW + 8 * j + n:C_CONVW + 8 * j + n + 1]
                            if j == 0:
                                ins = V.tensor_scalar(bx[:, n], win, w, cols[:, C_CONVB + n:C_CONVB + n + 1],
                                                      ALU.mult, ALU.add)
                            else:
                                dve.wait_ge(sem("tap"), 8 * (j - 1) + n + 1)
                                ins = V.scalar_tensor_tensor(bx[:, n], win, w, bx[:, n], ALU.mult, ALU.add)
                            ins.then_inc(sem("tap") if j < CONV - 1 else sem("conv"), 1)
                if c == 4:
                    for n in range(8):
                        dve.wait_ge(sem("i_out"), n + 1)
                        V.tensor_tensor(bx[:, n], bx[:, n], istage[:, n % 2], ALU.mult).then_inc(sem("i_used"), 1)
                if c == 6:
                    dve.wait_ge(sem("dec"), 8)
                    dve.wait_ge(sem("i_used"), 8)
                    step(V.scalar_tensor_tensor(bx[:], dec[:], 1.0, bx[:], ALU.add, ALU.mult))
                if 5 <= c <= 8:
                    dve.wait_ge(sem("in_tr"), c)
                    V.tensor_scalar(qkT2[:, 4 * c - 20:4 * c - 16, :], quarters(4), SCALE if c < 7 else 1.0, None,
                                    ALU.mult).then_inc(sem("qk_T"), 1)
                if c == 7:
                    dve.wait_ge(sem("root2"), 1)
                    step(V.tensor_tensor(bx[:], bx[:], uT[:], ALU.mult))
                    for n in range(8):
                        ins = V.tensor_tensor_scan(uT[:, n], dec[:, n], bx[:, n], 0.0, ALU.mult, ALU.add)
                        ins.then_inc(sem("scan"), 1)
                    dve.wait_ge(sem("scan"), 8)
                    dve.wait_ge(sem("gy_T"), 2)
                    V.tensor_tensor(gyT[:], gyT[:], uT[:], ALU.mult).then_inc(sem("lru"), 1)
                if c == 8:
                    dve.wait_ge(sem("f_mm"), 1)
                    V.tensor_copy(fs[:].rearrange("p k h -> p (k h)"), ps[:, 7, 0:16]).then_inc(sem("fs"), 1)
            L = [lgate[:, r, :] for r in range(4)]
            dve.wait_ge(sem("f_tr"), 1)
            step(V.tensor_scalar(L[0], ps[0:8, 7, 128:128 + SEQ], cols[0:8, C_BF:C_BF + 1], None, ALU.add))
            step(V.tensor_scalar(L[1], L[0], -1.0, None, ALU.mult))
            V.tensor_tensor(L[1], L[1], L[0], ALU.max).then_inc(sem("lg_abs"), 1)
            dve.wait_ge(sem("lg_exp"), 1)
            log1p(L[1], L[1], L[2], L[3])
            step(V.tensor_scalar(L[0], L[0], 0.0, None, ALU.min))
            step(V.tensor_tensor(L[0], L[0], L[1], ALU.subtract))
            step(V.memset(L[3], 0.0))
            step(V.tensor_tensor_scan(L[1], L[0], L[3], 0.0, ALU.add, ALU.add))
            V.tensor_scalar(L[2], L[1], -1.0, None, ALU.mult).then_inc(sem("cum"), 1)

            def max2(h):
                dve.wait_ge(sem("s2"), h + 1)
                V.tensor_reduce(negm[:, :, h:h + 1], ps[:, h % 2, :].rearrange("p (k n) -> p k n", n=SEQ), AX.X,
                                ALU.max, negate=True).then_inc(sem("m2"), 1)

            max2(0)
            for h in range(H2):
                if h + 1 < H2:
                    max2(h + 1)
                dve.wait_ge(sem("t2"), h + 1)
                V.tensor_copy(probsT2[:, h % 2].rearrange("p k n -> p (k n)"), ps[:, 2 + h % 2, :])\
                    .then_inc(sem("p2"), 1)
                dve.wait_ge(sem("v2"), h + 1)
                V.tensor_copy(att2[:, :, h, :], ps[:, 4 + h % 2, 0:SEQ].rearrange("p (k d) -> p k d", d=HD))\
                    .then_inc(sem("o2"), 1)
            dve.wait_ge(sem("e2"), 2 * H2)
            dve.wait_ge(sem("o2"), H2)
            step(V.reciprocal(fac[:, :, 0:8], lsum[:, :, 0:8]))
            for k in range(TOK):
                f8 = fac[:, k, 0:8].rearrange("p (h o) -> p h o", o=1).to_broadcast([P, H2, HD])
                ins = V.tensor_tensor(att2[:, k], att2[:, k], f8, ALU.mult)
            ins.then_inc(sem("att2_n"), 1)
            dve.wait_ge(sem("lru"), 1)
            V.tensor_tensor(lsq[:], gyT[:], gyT[:], ALU.mult).then_inc(sem("lsq"), 1)
            dve.wait_ge(sem("ssq2"), 2)
            V.tensor_scalar(ssum[:], ssum[:], 1.0 / LRU, EPS, ALU.mult, ALU.add).then_inc(sem("ms2"), 1)
            dve.wait_ge(sem("ms2_root"), 1)
            V.reciprocal(rstd[:, 1, :], rstd[:, 0, :]).then_inc(sem("rstd2"), 1)
            for g in range(2):
                f = FOLD_ATT + g
                fold_ready(f, f + 1)
                for k in range(4):
                    col = cols[:, C_GATT + 4 * g + k:C_GATT + 4 * g + k + 1]
                    ins = V.tensor_scalar(fold[:, f % 2, k], quarters(fold_bank(f))[:, k], col, None, ALU.mult)
                ins.then_inc(sem("fold_t"), 1)
                fold_lo(f, (hTl, hTh), 4 * g)
            dve.wait_ge(sem("lsum_mm"), 1)
            V.tensor_scalar(lrs[:, 0, :], ps[:, 2, 0:SEQ], 1.0 / LRU, EPS, ALU.mult, ALU.add).then_inc(sem("lru_ms"), 1)
            dve.wait_ge(sem("lru_root"), 1)
            step(V.reciprocal(lrs[:, 1, :], lrs[:, 0, :]))
            for g in range(2):
                f = FOLD_LRU + g
                fold_ready(f, None)
                for k in range(4):
                    n = 4 * g + k
                    ins = V.scalar_tensor_tensor(fold[:, f % 2, k], gyT[:, n], cols[:, C_GLRU + n:C_GLRU + n + 1],
                                                 lrs[:, 1, :], ALU.mult, ALU.mult)
                ins.then_inc(sem("fold_t"), 1)
                fold_lo(f, (hTl, hTh), 8 + 4 * g)
            dve.wait_ge(sem("ga1_in"), 16)
            dve.wait_ge(sem("x_back"), 32)
            for c in range(4):
                q = Q_OUT2 + c
                rest_quad(q + 1)
                dve.wait_ge(piece_used, 4 * q + 4)
                cut = slice(512 * c, 512 * c + 512)
                gain = ga1[:, cut].rearrange("p (o n) -> p o n", o=1).to_broadcast([P, TOK, 512])
                V.tensor_tensor(mt2[:], pair(2 * (c % 2)), gain, ALU.mult).then_inc(sem("out2"), 1)
                dve.wait_ge(sem("out2"), c + 1)
                step(V.tensor_tensor(x[:, :, cut], x[:, :, cut], mt2[:], ALU.add))
            dve.sem_inc(sem("x_ready"), 1)
            step(V.scalar_tensor_tensor(gmod[:], modT[:, 3, :], 1.0, cols[:, C_GFFN2:C_GFFN2 + 16], ALU.add, ALU.mult))
            norm(4, FOLD_PEER, 0, 2, gmod)

            def pq_turned(c):
                dve.wait_ge(sem("pq_tr"), c + 1)
                V.tensor_copy(pqT[:, 4 * c:4 * c + 4, :], quarters(4)).then_inc(sem("pq_T"), 1)

            def scores_out(c):
                dve.wait_ge(sem("psc"), c + 1)
                if c == 0:
                    dve.wait_ge(sem("fold_tr"), FOLD_PEER + 4 - 2)
                V.tensor_copy(sc[:, :, 4 * c:4 * c + 4, :].rearrange("p k h n -> p k (h n)"), pair(6))\
                    .then_inc(sem("sc_out"), 1)

            for c in range(4):
                rest_quad(Q_PQ + c + 1)
                if c >= 1:
                    pq_turned(c - 1)
                if c >= 2:
                    scores_out(c - 2)
            pq_turned(3)
            scores_out(2)
            scores_out(3)
            dve.wait_ge(sem("sc_out"), 4)

            def top16(vals, idx, src, tmp, rows):
                for r in range(rows):
                    ins = V.max(vals[:, r, 0:8], src[:, r])
                step(ins)
                for r in range(rows):
                    V.max_index(idx[:, r, 0:8], vals[:, r, 0:8], src[:, r])
                for r in range(rows):
                    ins = V.match_replace(tmp[:, r], vals[:, r, 0:8], src[:, r], -3e38)
                step(ins)
                for r in range(rows):
                    ins = V.max(vals[:, r, 8:16], tmp[:, r])
                step(ins)
                for r in range(rows):
                    ins = V.max_index(idx[:, r, 8:16], vals[:, r, 8:16], tmp[:, r])
                step(ins)

            for k in range(TOK):
                top16(top[:, k], topi[:, k], sc[:, k], work[:].rearrange("p a (b n) -> p (a b) n", n=N_KEYS), 16)
            step(V.tensor_copy(topf[:].rearrange("p k h n -> p (k h n)"), topi[:].rearrange("p k h n -> p (k h n)")))
            for k in range(TOK):
                pairs = top[:, k].rearrange("p (h e) n -> p h e n", e=2)
                first = pairs[:, :, 0].rearrange("p h (n o) -> p h n o", o=1).to_broadcast([P, 8, TOPK, TOPK])
                second = pairs[:, :, 1].rearrange("p h (o n) -> p h o n", o=1).to_broadcast([P, 8, TOPK, TOPK])
                step(V.tensor_tensor(cand[:].rearrange("p h (a b) -> p h a b", b=TOPK), first, second, ALU.add))
                top16(best[:, k], besti[:, k], cand, work, 8)
                bi = besti[:, k]
                V.tensor_scalar(divi[:, 0], bi, 4, None, ALU.logical_shift_right)
                step(V.tensor_scalar(divi[:, 1], bi, 15, None, ALU.bitwise_and))
                step(V.tensor_copy(divf[:].rearrange("p e h n -> p (e h n)"), divi[:].rearrange("p e h n -> p (e h n)")))
                for e in range(2):
                    w4 = work[:].rearrange("p h (a b) -> p h a b", b=TOPK)
                    v4 = work2[:].rearrange("p h (a b) -> p h a b", b=TOPK)
                    place = iota[:, 0:16].rearrange("p (o q n) -> p o q n", o=1, q=1).to_broadcast([P, 8, TOPK, TOPK])
                    want = divf[:, e].rearrange("p h (n o) -> p h n o", o=1).to_broadcast([P, 8, TOPK, TOPK])
                    have = topf[:, k].rearrange("p (h e) n -> p h e n", e=2)[:, :, e]\
                        .rearrange("p h (o n) -> p h o n", o=1).to_broadcast([P, 8, TOPK, TOPK])
                    step(V.tensor_tensor(w4, place, want, ALU.is_equal))
                    step(V.tensor_tensor(v4, w4, have, ALU.mult))
                    step(V.tensor_reduce(picks[:, k, e], v4, AX.X, ALU.add))
                lead = best[:, k, :, 0:1].to_broadcast([P, 8, TOPK])
                ins = V.tensor_tensor(picks[:, k, 2], best[:, k], lead, ALU.subtract)
            ins.then_inc(sem("wexp_in"), 1)
            dve.wait_ge(sem("wexp"), 1)
            for k in range(TOK):
                ins = V.tensor_reduce(wsm[:, k, :, 0:1], picks[:, k, 2], AX.X, ALU.add)
            step(ins)
            step(V.reciprocal(wsm[:, :, :, 1:2], wsm[:, :, :, 0:1]))
            for k in range(TOK):
                ins = V.tensor_tensor(picks[:, k, 2], picks[:, k, 2], wsm[:, k, :, 1:2].to_broadcast([P, 8, TOPK]),
                                      ALU.mult)
            ins.then_inc(sem("picks"), 1)
            rest_quad(Q_PEER + 1)
            dve.wait_ge(sem("picks_tr"), 1)
            V.tensor_copy(picksT[:].rearrange("p a t -> p (a t)"),
                          ps[:, 6:8, :].rearrange("p b n -> p (b n)")[:, 0:3 * SEQ]).then_inc(sem("picksT"), 1)
            dve.wait_ge(sem("picksT"), 1)

            def one_hots(n, u, first):
                if not first:
                    dve.wait_ge(sem("wmm"), n - 1)
                    dve.wait_ge(sem("oh"), n)
                V.tensor_copy(pk[:], picksT[:, :, bass.ds(n * 16, 16)] if not isinstance(n, int)
                              else picksT[:, :, 16 * n:16 * n + 16]).then_inc(sem("pk"), 1)
                dve.wait_ge(sem("pk"), n + 1)
                for k in range(16):
                    V.tensor_scalar(ohA[:, u, k], iota[:], pk[:, 0, k:k + 1], None, ALU.is_equal)
                    ins = V.tensor_scalar(ohB[:, u, k], iota[:], pk[:, 1, k:k + 1], pk[:, 2, k:k + 1],
                                          ALU.is_equal, ALU.mult)
                ins.then_inc(sem("oh"), 1)

            one_hots(0, 0, True)
            dve.wait_ge(sem("oh"), 1)
            one_hots(1, 1, True)
            with dve.Fori(1, SEQ // 32) as m:
                for u in range(2):
                    one_hots(2 * m + u, u, False)

            def peer_mul(g, first):
                dve.wait_ge(sem("gelu"), g + 1)
                dve.wait_ge(sem("wc_in"), 16 * g + 16)
                if not first:
                    dve.wait_ge(sem("peer_tr"), g)
                V.tensor_tensor(pact[:], gacc[:], wc[:], ALU.mult).then_inc(sem("pmul"), 1)

            def peer_lo(b):
                dve.wait_ge(sem("peer_hi"), b + 1)
                V.tensor_tensor(pactTl[:], quarters(4), pactTh[:].bitcast(F32), ALU.subtract).then_inc(sem("peer_lo"), 1)

            def peer_down(b, s, used):
                dve.wait_ge(piece_used, used)
                dve.wait_ge(sem("y_sum"), 4 * b + (s + 1))
                yc = y[:, :, 512 * s:512 * s + 512]
                V.tensor_tensor(yc, yc, pair(6 if s % 2 == 0 else 2), ALU.add).then_inc(sem("y_sum"), 1)

            dve.wait_ge(sem("wmm"), SEQ // 16)
            V.memset(y[:], 0.0).then_inc(sem("y_sum"), 1)
            peer_mul(0, True)
            with dve.Fori(0, PEER_GROUPS - 1) as b:
                for j in range(8):
                    if j >= 4:
                        peer_down(b, j - 4, 8 * b + (4 * Q_PEER + 4 + j + 1))
                    rest_piece(2 * b + (Q_PEER + 2 + j // 4), j % 4)
                    if j == 1:
                        peer_lo(b)
                    if j == 4:
                        peer_mul(b + 1, False)
            peer_lo(PEER_GROUPS - 1)
            for j in range(4):
                peer_down(PEER_GROUPS - 1, j, 4 * QUADS - 3 + j)
            dve.wait_ge(sem("y_sum"), 4 * PEER_GROUPS + 1)
            dve.wait_ge(sem("ga2_in"), 16)
            step(V.tensor_tensor(y[:], y[:], ga2[:].rearrange("p (o n) -> p o n", o=1).to_broadcast([P, TOK, D]),
                                 ALU.mult))
            V.tensor_tensor(x[:], x[:], y[:], ALU.add).then_inc(sem("x_ready"), 1)
            dve.wait_ge(sem("ssq3"), 2)
            V.tensor_scalar(ssum[:], ssum[:], 1.0 / D, EPS, ALU.mult, ALU.add).then_inc(sem("ms3"), 1)
            dve.wait_ge(sem("ms3_root"), 1)
            step(V.reciprocal(rstd[:, 1, :], rstd[:, 0, :]))
            dve.wait_ge(sem("gfin_in"), 16)
            for k in range(TOK):
                V.scalar_tensor_tensor(x[:, k, :], x[:, k, :], rstd[:, 1, k:k + 1], gfin[:], ALU.mult, ALU.mult)\
                    .then_inc(sem("final"), 1)

        @block.tensor
        def _(pe):
            T = nc.tensor

            def split_products(out, th, tl, stat, s, cut, start, stop):
                T.matmul(out, th[stat], hi[:, s, cut], start=start, stop=False)
                T.matmul(out, th[stat], lo[:, s, cut], start=False, stop=False)
                return T.matmul(out, tl[stat], hi[:, s, cut], start=False, stop=stop)

            def wide_piece(q, s, b, th=None, tl=None):
                th, tl = (hTh, hTl) if th is None else (th, tl)
                pe.wait_ge(lo_done, 4 * q + (s + 1))
                for k in range(4):
                    for m in range(TOK):
                        ins = split_products(ps[:, b + m, :], th, tl,
                                             (slice(None), 4 * s + k, slice(P * m, P * m + P)), s,
                                             slice(512 * k, 512 * k + 512), s == 0 and k == 0, s == 3 and k == 3)
                ins.then_inc(piece_used, 1)

            def down_piece(q, s, b, th, tl):
                pe.wait_ge(lo_done, 4 * q + (s + 1))
                for m in range(TOK):
                    for k in range(4):
                        ins = split_products(ps[:, b + m, :], th, tl, (slice(None), k, slice(P * m, P * m + P)), s,
                                             slice(512 * k, 512 * k + 512), k == 0, k == 3)
                ins.then_inc(piece_used, 1)

            def turn(b, tiles):
                for k in range(4):
                    for m in range(TOK):
                        ins = T.transpose(quarters(b)[:, k, P * m:P * m + P], tiles(k, m), ident[:])
                return ins

            def fold_turn(f, tiles):
                free = f if FOLD_M <= f < FOLD_FFN else f - 1
                if free >= 1:
                    pe.wait_ge(sem("fold_t"), free)
                turn(fold_bank(f), tiles).then_inc(sem("fold_tr"), 1)

            def norm_turns(f0, src, u):
                pe.wait_ge(sem("xn_done"), 2 * u + 2)
                for g in range(4):
                    fold_turn(f0 + g, lambda k, m: src[:, m, P * (4 * g + k):P * (4 * g + k) + P])

            pe.wait_ge(sem("const_in"), 16 * 12)
            T.matmul(ps[0:6, 7, :], tabs[:], oneh[:], start=True, stop=True).then_inc(sem("bias_mm"), 1)
            norm_turns(FOLD_MEM, memraw, 0)
            pe.wait_ge(sem("fold_lo"), FOLD_X)
            for s in range(4):
                wide_piece(0, s, 0, memTh, memTl)
            pe.wait_ge(sem("bvec"), 1)
            norm_turns(FOLD_X, x, 1)

            def head_turn(q):
                n = head_quads.index(q)
                pe.wait_ge(sem("head_n"), n + 1)
                if n >= 1:
                    pe.wait_ge(sem("head_T"), n)
                else:
                    pe.wait_ge(sem("fold_t"), FOLD_O)
                turn(4, lambda k, m: stage[:, m, HD * k:HD * k + HD]).then_inc(sem("head_tr"), 1)

            for q in range(1, Q_GATES):
                if q == 2:
                    pe.wait_ge(sem("fold_lo"), FOLD_O)
                if q >= 2:
                    pe.wait_ge(sem("chunk_out"), q - 1)
                for s in range(4):
                    if q == 1:
                        wide_piece(q, s, 2, memTh, memTl)
                    else:
                        wide_piece(q, s, 2 * (q % 2))
                if q - 1 in head_quads:
                    head_turn(q - 1)

            heads = [(h, 6 + h, h) for h in range(6)]
            heads += [(16 + j, 22 + j // 3, 6 + j // 3) for j in range(B_HEADS)]
            heads += [(12 + j, None, j) for j in range(C_HEADS)]
            for n in range(48):
                q, s = divmod(4 * Q_GATES + n, 4)
                if s == 0:
                    pe.wait_ge(sem("chunk_out"), q - 1)
                wide_piece(q, s, 2 * (q % 2))
                h, part = divmod(n, 3)
                qi, ki, vi = heads[h]
                if part == 0:
                    if h == 0:
                        pe.wait_ge(sem("head_T"), 7)
                    if h >= 1:
                        pe.wait_ge(sem("att_e"), 2 * h)
                    if h < A_HEADS:
                        pe.wait_ge(sem(f"hank_in{h % 2}"), 16 * (h // 2 + 1))
                    for m in range(TOK):
                        keys = kcT[:, h - 12] if ki is None else qkT[:, ki]
                        out = ps[:, 4, SEQ * m:SEQ * m + SEQ]
                        ins = T.matmul(out, qkT[:, qi, P * m:P * m + P], keys, start=True, stop=h >= A_HEADS)
                        if h < A_HEADS:
                            at0 = P * (1 - m)
                            ins = T.matmul(out, anti[:], hank[:, h % 2, at0:at0 + SEQ], start=False, stop=True)
                    ins.then_inc(sem("att_s"), 1)
                elif part == 1:
                    pe.wait_ge(sem("att_e"), 2 * h + 2)
                    if h >= 1:
                        pe.wait_ge(sem("att_p"), h)
                    for m in range(TOK):
                        for k in range(TOK):
                            ins = T.transpose(ps[:, 5, SEQ * k + P * m:SEQ * k + P * m + P],
                                              probs[:, m, P * k:P * k + P], ident[:])
                    ins.then_inc(sem("att_t"), 1)
                else:
                    pe.wait_ge(sem("att_p"), h + 1)
                    if h == 0:
                        pe.wait_ge(sem("chunk_out"), Q_GATES)
                    if h >= 1:
                        pe.wait_ge(sem("att_o"), h)
                    for m in range(TOK):
                        for k in range(TOK):
                            val = vC[:, k, vi] if ki is None else vAB[:, k, vi]
                            ins = T.matmul(ps[:, 6, HD * m:HD * m + HD], probsT[:, k, P * m:P * m + P], val,
                                           start=k == 0, stop=k == 1)
                    ins.then_inc(sem("att_v"), 1)

            pe.wait_ge(sem("o_ready"), 1)
            for f in range(FOLD_O, FOLD_M):
                fold_turn(f, lambda k, m: obuf[:, m, 4 + 4 * (f - FOLD_O) + k])
            pe.wait_ge(sem("fold_lo"), FOLD_M)
            pe.wait_ge(sem("chunk_out"), Q_BRANCH)

            def merged_turn(j):
                pe.wait_ge(sem("merge"), j + 1)
                fold_turn(FOLD_M + j, lambda k, m: merged[:, m, P * (4 * j + k):P * (4 * j + k) + P])

            for n in range(12):
                q, s = divmod(4 * Q_BRANCH + n, 4)
                j, part = divmod(n, 3)
                pe.wait_ge(lo_done, 4 * q + s + 1)
                if part == 0 and j >= 1:
                    pe.wait_ge(sem("merge"), j)
                for k in range(4):
                    kt = 4 * part + k
                    b = 0 if kt < 2 else 2 if kt < 8 else 6
                    for m in range(TOK):
                        ins = split_products(ps[:, b + m, :], oTh, oTl, (slice(None), kt, slice(P * m, P * m + P)), s,
                                             slice(512 * k, 512 * k + 512), kt in (0, 2, 8), kt in (1, 7, 11))
                ins.then_inc(piece_used, 1)
                if part == 2 and j >= 1:
                    merged_turn(j - 1)
            merged_turn(3)
            pe.wait_ge(sem("fold_lo"), FOLD_FFN)

            def ada_sum(a, b):
                pe.wait_ge(sem("ada_sum"), 16 * a + 16)
                for k in range(2):
                    ins = T.matmul(ps[0:1, b + k, :], ones[:, 0:1], adaacc[:, 512 * k:512 * k + 512],
                                   start=True, stop=True)
                ins.then_inc(sem("ada_mm"), 1)

            for n in range(16):
                q, s = divmod(4 * Q_WO + n, 4)
                c = q - Q_WO
                if s == 0 and c >= 2:
                    pe.wait_ge(sem("wo_out"), c - 1)
                wide_piece(q, s, 2 * (c % 2))
                if n % 8 == 7:
                    ada_sum(n // 8, 6)
            norm_turns(FOLD_FFN, xn, 2)
            pe.wait_ge(sem("wo_out"), 4)
            pe.wait_ge(sem("fold_lo"), FOLD_MIX2)

            def ffn_turn(b):
                pe.wait_ge(sem("fmul"), b + 1)
                turn(4, lambda k, m: fact[:, m, P * k:P * k + P]).then_inc(sem("ffn_tr"), 1)

            def ffn_down(b, q, s):
                if s == 0:
                    pe.wait_ge(sem("ffn_lo"), b + 1)
                if s >= 2:
                    pe.wait_ge(sem("x_sum"), 4 * b + s)
                elif s == 0 and not isinstance(b, int):
                    pe.wait_ge(sem("x_sum"), 4 * b + 1)
                down_piece(q, s, 6 if s % 2 == 0 else 0, factTh, factTl)

            for s in range(4):
                wide_piece(Q_FFN, s, 0)
            for s in range(4):
                wide_piece(Q_FFN + 1, s, 2)
            with pe.Fori(0, FF_GROUPS - 1) as b:
                for j in range(12):
                    q, s = 3 * b + (Q_FFN + 2 + j // 4), j % 4
                    if j == 0:
                        pe.wait_ge(sem("silu"), b + 1)
                        pe.wait_ge(sem("x_sum"), 4 * b + 1)
                    if j == 4:
                        pe.wait_ge(sem("fmul"), b + 1)
                    if j == 9:
                        pe.wait_ge(sem("silu"), b + 2)
                    if j < 8:
                        wide_piece(q, s, 0 if j < 4 else 2)
                    else:
                        ffn_down(b, q, s)
                    if j == 1:
                        pe.wait_ge(sem("modrow"), 2 * b + 4)
                        ffn_turn(b)
                ada_sum(b + 2, 4)
            pe.wait_ge(sem("modrow"), 2 * ADA_SPLITS)
            ffn_turn(FF_GROUPS - 1)
            pe.wait_ge(sem("x_sum"), 4 * (FF_GROUPS - 1) + 1)
            for s in range(4):
                ffn_down(FF_GROUPS - 1, Q_IN2 - 1, s)
            norm_turns(FOLD_MIX2, xn, 3)
            pe.wait_ge(sem("x_sum"), 4 * FF_GROUPS + 1)
            pe.wait_ge(sem("fold_lo"), FOLD_ATT)

            def in_turn(c):
                pe.wait_ge(sem("in_out"), c + 1)
                if c == 0:
                    pe.wait_ge(sem("fold_t"), FOLD_ATT)
                elif c <= 2:
                    pe.wait_ge(sem("lx_T"), c)
                elif c <= 4:
                    pe.wait_ge(sem("gy_T"), c - 2)
                else:
                    pe.wait_ge(sem("qk_T"), c - 4)
                turn(4, lambda k, m: stage[:, m, P * k:P * k + P]).then_inc(sem("in_tr"), 1)

            for c in range(10):
                if c >= 2:
                    pe.wait_ge(sem("in_out"), c - 1)
                for s in range(4):
                    wide_piece(Q_IN2 + c, s, 2 * (c % 2))
                if 1 <= c <= 8:
                    in_turn(c - 1)
                if c == 4:
                    pe.wait_ge(sem("lw_in"), 32)
                    for n in range(8):
                        pe.wait_ge(sem("conv"), n + 1)
                        if n >= 2:
                            pe.wait_ge(sem("i_out"), n - 1)
                        T.matmul(ps[:, 6 + n % 2, 0:SEQ], lwa[:, n], bx[:, n], start=True, stop=True)
                        T.matmul(ps[:, 6 + n % 2, SEQ:2 * SEQ], lwx[:, n], bx[:, n], start=True, stop=True)\
                            .then_inc(sem("ri"), 1)
                if c == 7:
                    pe.wait_ge(sem("wfl"), 1)
                    pe.wait_ge(sem("i_out"), 8)
                    for m in range(TOK):
                        for k in range(KT):
                            for j, (a, b) in enumerate(((hTh, wfh), (hTh, wfl), (hTl, wfh))):
                                ins = T.matmul(ps[:, 7, 8 * m:8 * m + 8], a[:, k, P * m:P * m + P], b[:, k, :],
                                               start=k == 0 and j == 0, stop=k == KT - 1 and j == 2)
                    ins.then_inc(sem("f_mm"), 1)
                if c == 9:
                    pe.wait_ge(sem("fs"), 1)
                    for m in range(TOK):
                        ins = T.transpose(ps[0:8, 7, 128 + P * m:128 + P * m + P], fs[:, m, :], ident[:])
                    ins.then_inc(sem("f_tr"), 1)

            def scores2(h):
                if h >= 2:
                    pe.wait_ge(sem("e2"), 2 * h - 2)
                for m in range(TOK):
                    out = ps[:, h % 2, SEQ * m:SEQ * m + SEQ]
                    at0 = P * (1 - m)
                    T.matmul(out, qkT2[:, h, P * m:P * m + P], qkT2[:, 8 + h, :], start=True, stop=False)
                    T.matmul(out, lgate[:, 1, P * m:P * m + P], sel[:, h, :], start=False, stop=False)
                    T.matmul(out, sel[:, h, 0:P], lgate[:, 2, :], start=False, stop=False)
                    ins = T.matmul(out, ident[:], causal[:, at0:at0 + SEQ], start=False, stop=True)
                ins.then_inc(sem("s2"), 1)

            pe.wait_ge(sem("sel_in"), 16)
            pe.wait_ge(sem("cum"), 1)
            pe.wait_ge(sem("qk_T"), 4)
            pe.wait_ge(sem("in_out"), 10)
            scores2(0)
            for h in range(H2):
                if h + 1 < H2:
                    scores2(h + 1)
                pe.wait_ge(sem("e2"), 2 * h + 2)
                if h >= 2:
                    pe.wait_ge(sem("p2"), h - 1)
                for m in range(TOK):
                    for k in range(TOK):
                        ins = T.transpose(ps[:, 2 + h % 2, SEQ * k + P * m:SEQ * k + P * m + P],
                                          probs2[:, h % 2, m, P * k:P * k + P], ident[:])
                ins.then_inc(sem("t2"), 1)
                pe.wait_ge(sem("p2"), h + 1)
                if h >= 2:
                    pe.wait_ge(sem("o2"), h - 1)
                for m in range(TOK):
                    for k in range(TOK):
                        ins = T.matmul(ps[:, 4 + h % 2, HD * m:HD * m + HD], probsT2[:, h % 2, k, P * m:P * m + P],
                                       v2[:, k, HD * h:HD * h + HD], start=k == 0, stop=k == 1)
                ins.then_inc(sem("v2"), 1)
            pe.wait_ge(sem("lsq"), 1)
            pe.wait_ge(sem("p2"), H2)
            for n in range(8):
                ins = T.matmul(ps[:, 2, 0:SEQ], ones[:], lsq[:, n], start=n == 0, stop=n == 7)
            ins.then_inc(sem("lsum_mm"), 1)
            pe.wait_ge(sem("att2_s"), 2)
            pe.wait_ge(sem("o2"), H2)
            for g in range(2):
                fold_turn(FOLD_ATT + g, lambda k, m: att2[:, m, 4 * g + k])
            pe.wait_ge(sem("lru_ms"), 1)
            pe.wait_ge(sem("fold_lo"), FOLD_PEER)
            for c in range(4):
                if c >= 2:
                    pe.wait_ge(sem("out2"), c - 1)
                for s in range(4):
                    wide_piece(Q_OUT2 + c, s, 2 * (c % 2))
            norm_turns(FOLD_PEER, xn, 4)
            pe.wait_ge(sem("fold_lo"), FOLD_PEER + 4)

            def pq_turn(c):
                pe.wait_ge(sem("pq_out"), c + 1)
                if c == 0:
                    pe.wait_ge(sem("out2"), 4)
                    pe.wait_ge(sem("fold_t"), FOLD_PEER + 4)
                else:
                    pe.wait_ge(sem("pq_T"), c)
                turn(4, lambda k, m: stage[:, m, P * k:P * k + P]).then_inc(sem("pq_tr"), 1)

            def key_scores(c):
                pe.wait_ge(sem("keys_in"), 16)
                pe.wait_ge(sem("pq_T"), c + 1)
                if c >= 1:
                    pe.wait_ge(sem("sc_out"), c)
                for k in range(4):
                    for m in range(TOK):
                        ins = T.matmul(ps[:, 6 + m, P * k:P * k + P], pqT[:, 4 * c + k, P * m:P * m + P],
                                       keysT[:, 4 * c + k], start=True, stop=True)
                ins.then_inc(sem("psc"), 1)

            for c in range(4):
                if c >= 2:
                    pe.wait_ge(sem("pq_out"), c - 1)
                if c == 0:
                    pe.wait_ge(sem("out2"), 4)
                for s in range(4):
                    wide_piece(Q_PQ + c, s, 2 * (c % 2))
                if c >= 1:
                    pq_turn(c - 1)
                if c >= 2:
                    key_scores(c - 2)
            pq_turn(3)
            key_scores(2)
            key_scores(3)
            pe.wait_ge(sem("pq_out"), 4)
            for s in range(4):
                wide_piece(Q_PEER, s, 0)
            pe.wait_ge(sem("picks"), 1)
            pe.wait_ge(sem("sc_out"), 4)
            for e in range(3):
                for m in range(TOK):
                    c0 = SEQ * e + P * m
                    ins = T.transpose(ps[:, 6 + c0 // 512, c0 % 512:c0 % 512 + P],
                                      picks[:, m, e].rearrange("p h n -> p (h n)"), ident[:])
            ins.then_inc(sem("picks_tr"), 1)

            def expert_weights(n, u, first):
                pe.wait_ge(sem("oh"), n + 1)
                if not first:
                    pe.wait_ge(sem("wst"), n - 1)
                for k in range(16):
                    ins = T.matmul(ps[:, 4 * u + k // 4, P * (k % 4):P * (k % 4) + P], ohA[:, u, k], ohB[:, u, k],
                                   start=True, stop=True)
                ins.then_inc(sem("wmm"), 1)

            pe.wait_ge(sem("gelu"), 1)
            pe.wait_ge(sem("picksT"), 1)
            expert_weights(0, 0, True)
            expert_weights(1, 1, True)
            with pe.Fori(1, SEQ // 32) as n:
                for u in range(2):
                    expert_weights(2 * n + u, u, False)
            pe.wait_ge(sem("wst"), SEQ // 16)

            def peer_turn(b):
                pe.wait_ge(sem("pmul"), b + 1)
                turn(4, lambda k, m: pact[:, m, P * k:P * k + P]).then_inc(sem("peer_tr"), 1)

            def peer_down(b, q, s):
                if s == 0:
                    pe.wait_ge(sem("peer_lo"), b + 1)
                pe.wait_ge(sem("y_sum"), 4 * b + max(s - 1, 0) + (1 if s else 0))
                down_piece(q, s, 6 if s % 2 == 0 else 2, pactTh, pactTl)

            with pe.Fori(0, PEER_GROUPS - 1) as b:
                for j in range(8):
                    q, s = 2 * b + (Q_PEER + 1 + j // 4), j % 4
                    if j == 0:
                        pe.wait_ge(sem("gelu"), b + 1)
                    if j < 4:
                        wide_piece(q, s, 0)
                    else:
                        peer_down(b, q, s)
                    if j == 1:
                        peer_turn(b)
            peer_turn(PEER_GROUPS - 1)
            for s in range(4):
                peer_down(PEER_GROUPS - 1, QUADS - 1, s)


def _tables():
    eye = np.eye(P, dtype=np.float32)
    d = np.arange(-255, 257, dtype=np.int64)
    half = BUCKETS // 2
    exact = half // 2
    n = np.abs(d)
    large = exact + (np.log(np.maximum(n, 1).astype(np.float32) / np.float32(exact))
                     / np.float32(math.log(MAX_DIST / exact)) * np.float32(half - exact)).astype(np.int32)
    bucket = np.where(d > 0, half, 0) + np.where(n < exact, n, np.minimum(large, half - 1))
    oneh = (bucket[None, :] == np.arange(BUCKETS)[:, None]).astype(np.float32)
    dmask = np.zeros((6, 512), np.float32)
    for g, dil in enumerate(DILATIONS):
        dmask[2 * g:2 * g + 2] = np.where((d % dil == 0) & (n <= RADIUS_STEPS * dil), 0.0, NEG)
    r = np.repeat(np.arange(SEQ // 64), 64).astype(np.float32)
    c = np.tile(np.arange(64), SEQ // 64).astype(np.float32)
    inv = (np.float32(10000.0) ** (-np.arange(HD // 4, dtype=np.float32) / np.float32(HD // 4))).astype(np.float32)
    ang = np.concatenate([r[:, None] * inv, c[:, None] * inv], axis=-1)
    cos, sin = np.repeat(np.cos(ang), 2, axis=1), np.repeat(np.sin(ang), 2, axis=1)
    sin[:, 0::2] *= -1
    rope = np.stack([cos, sin]).reshape(2, TOK, P, HD).transpose(2, 0, 1, 3)
    f = np.arange(384)[None, :] - P
    causal = np.where(f <= np.arange(P)[:, None], 0.0, NEG)
    sel = np.repeat(np.eye(8, dtype=np.float32)[:, :, None], SEQ, axis=2)
    return {"ident": eye, "anti": eye[::-1], "iota": np.tile(np.arange(P, dtype=np.float32), (P, 1)),
            "oneh": oneh, "dmask": dmask, "rope": rope, "causal": causal, "sel": sel}


def _wide(w):
    k, n = w.shape
    return w.reshape(k // 2048, 4, 4, P, n // 512, 512).transpose(4, 0, 1, 3, 2, 5).reshape(-1, P, 2048)


def _down(w):
    k, n = w.shape
    return w.reshape(k // 512, 4, P, n // 512, 512).transpose(0, 3, 2, 1, 4).reshape(-1, P, 2048)


def _columns(v):
    return v.reshape(-1, P).T


def kernel(**inputs):
    import concourse.bacc as bacc
    from concourse.bass_utils import run_bass_kernel_spmd

    v = {k: np.asarray(a) for k, a in inputs.items()}
    w_in = v["w_in"][0]
    A_W, B_Q, B_K, C_W = 768, 768, 256, 512
    o = np.cumsum([0, A_W, A_W, A_W, B_Q, B_K, B_K, C_W, 3 * D])
    qa, ka, va, qb, kb, vb, qc, gt = [w_in[:, o[i]:o[i + 1]] for i in range(8)]
    w_mem = v["w_mem_kv"][0]
    first = np.concatenate([_wide(w_mem)] + [_wide(a) for a in (
        np.concatenate([qa, ka, qc, qb, kb, va, vb], axis=1), gt)])
    branch = np.concatenate([v["w_br_a"][0], v["w_br_b"][0], v["w_br_c"][0]])
    branch = branch.reshape(3, 4, P, 4, 512).transpose(3, 0, 2, 1, 4).reshape(-1, P, 2048)
    merge = np.concatenate([branch, _wide(v["w_o"][0])])
    gate, up = _wide(v["w_ffn_in"][0][:, :D_FF]), _wide(v["w_ffn_in"][0][:, D_FF:])
    down = _down(v["w_ffn_out"][0])
    g4, u4, d4 = (a.reshape(FF_GROUPS, 4, P, 2048) for a in (gate, up, down))
    order = [g4[0], u4[0]]
    for g in range(1, FF_GROUPS):
        order += [g4[g], u4[g], d4[g - 1]]
    ffn = np.concatenate(order + [d4[-1]])
    w2 = v["w_in_2"][0]
    second = np.concatenate([_wide(a) for a in (
        w2[:, 3080:4104], w2[:, 4104:5128], w2[:, 0:3072], v["w_out_2"][0], v["peer_w_q_2"][0])])
    pu = _wide(v["peer_u_2"][0].T).reshape(PEER_GROUPS, 4, P, 2048)
    pv = _down(v["peer_v_2"][0]).reshape(PEER_GROUPS, 4, P, 2048)
    order = [pu[0]]
    for g in range(1, PEER_GROUPS):
        order += [pu[g], pv[g - 1]]
    peer = np.concatenate(order + [pv[-1]])
    cols = np.zeros((P, NCOLS), np.float32)
    for at0, name in ((C_GMEM, "g_mem"), (C_GMIX, "g_mix"), (C_GFFN, "g_ffn"), (C_GMIX2, "g_mix_2"), (C_GFFN2, "g_ffn_2")):
        cols[:, at0:at0 + 16] = _columns(v[name][0])
    for at0, n, name in ((0, 6, "g_qa"), (6, 6, "g_ka"), (12, 4, "g_qc"), (16, 4, "g_kc")):
        cols[:, C_HEAD + at0:C_HEAD + at0 + n] = v[name][0][:, None]
    for j in range(CONV):
        cols[:, C_CONVW + 8 * j:C_CONVW + 8 * j + 8] = _columns(v["conv_w_2"][0, j])
    for at0, name in ((C_CONVB, "conv_b_2"), (C_BA, "lru_b_a_2"), (C_BX, "lru_b_x_2"), (C_LAM, "lru_lambda_2"),
                      (C_GLRU, "g_lru_out_2"), (C_GATT, "g_attn_out_2")):
        cols[:, at0:at0 + 8] = _columns(v[name][0])
    cols[0:8, C_BF] = v["b_f_2"][0]
    keys = np.stack([v["peer_k1_2"][0], v["peer_k2_2"][0]], axis=1).reshape(16, N_KEYS, P).transpose(2, 0, 1)
    arrays = {
        "x": v["x"][0], "mem": v["mem"][0], "w_first": first, "w_merge": merge, "w_ffn": ffn,
        "w_second": second, "w_peer": peer, "cols": cols, "rel_bias": v["rel_bias"],
        "g_qb": v["g_qb"], "g_kb": v["g_kb"], "c": _columns(v["c_2"][0]),
        "w_ada": v["w_ada_2"][0].reshape(8, 2, P, ADA_SPLITS, 1024).transpose(3, 0, 2, 1, 4).reshape(-1, P, 2048),
        "b_ada": v["b_ada_2"][0].reshape(ADA_SPLITS, 1, 1024),
        "w_f": w2[:, 3072:3080].reshape(KT, P, 8).transpose(1, 0, 2),
        "lru_w_a": v["lru_w_a_2"][0].transpose(1, 0, 2), "lru_w_x": v["lru_w_x_2"][0].transpose(1, 0, 2),
        "keys": keys, "g_final": v["g_final_2"].reshape(1, D), **_tables()}
    arrays = {f"in_{k}": np.ascontiguousarray(a, dtype=np.float32) for k, a in arrays.items()}
    nc = bacc.Bacc("TRN2", target_bir_lowering=False, num_devices=1)
    aps = {k[3:]: nc.dram_tensor(k, a.shape, F32, kind="ExternalInput").ap() for k, a in arrays.items()}
    aps["out"] = nc.dram_tensor("out", (SEQ, D), F32, kind="ExternalOutput").ap()
    program(nc, aps)
    r = run_bass_kernel_spmd(nc, [arrays], core_ids=[0])
    return np.asarray(r.results[0]["out"]).reshape(1, SEQ, D)
```

```python
import math
import numpy as np
import concourse.bass as bass
from concourse import mybir

F32 = mybir.dt.float32
F32R = mybir.dt.float32r
U32 = mybir.dt.uint32
ALU = mybir.AluOpType
ACT = mybir.ActivationFunctionType
AX = mybir.AxisListType

P = 128
D = 2048
SEQ = 256
TOK = SEQ // P
KT = D // P
HD = 128
EPS = 1e-6
NEG = -1e30
SCALE = 1.0 / math.sqrt(HD)

A_HEADS, B_HEADS, B_KV, C_HEADS = 6, 6, 2, 4
ROPE_HEADS = B_HEADS + B_KV
HEADS = A_HEADS + B_HEADS + C_HEADS
D_FF = 5632
FF_GROUPS = D_FF // 512
ADA = 6 * D
ADA_SPLITS = ADA // 1024
H2 = 8
LRU = 1024
CONV = 4
N_KEYS = 128
EXPERTS = N_KEYS * N_KEYS
PEER_GROUPS = EXPERTS // 512
TOPK = 16
BUCKETS, MAX_DIST = 32, 1024
DILATIONS = (1, 4, 16)
RADIUS_STEPS = 64
EARLY_TOP = 6
EARLY = EARLY_TOP + 5
assert EARLY_TOP % 2 == 0 and (EARLY - 1) % 2 == 0

Q_MEM = 0
Q_HEADS = Q_MEM + 2
Q_GATES = Q_HEADS + 8
Q_BRANCH = Q_GATES + 12
Q_WO = Q_BRANCH + 3
Q_FFN = Q_WO + 4
Q_IN2 = Q_FFN + 3 * FF_GROUPS
Q_OUT2 = Q_IN2 + 10
Q_PQ = Q_OUT2 + 4
Q_PEER = Q_PQ + 4
QUADS = Q_PEER + 2 * PEER_GROUPS

C_GMEM, C_GMIX, C_GFFN, C_GMIX2, C_GFFN2 = (16 * i for i in range(5))
C_HEAD = 80
C_CONVW = C_HEAD + 20
C_CONVB = C_CONVW + CONV * 8
C_BA = C_CONVB + 8
C_BX = C_BA + 8
C_LAM = C_BX + 8
C_GLRU = C_LAM + 8
C_GATT = C_GLRU + 8
C_BF = C_GATT + 8
NCOLS = C_BF + 1

FOLD_MEM, FOLD_X, FOLD_O, FOLD_M, FOLD_FFN, FOLD_MIX2, FOLD_ATT, FOLD_LRU, FOLD_PEER = 0, 4, 8, 11, 15, 19, 23, 25, 27


def program(nc, t):
    base0 = 16512
    K = 1024

    def at(name, shape, dt, off):
        return nc.alloc_sbuf_tensor_at(name, shape, dt, offset=base0 + off)

    raw = at("raw", [P, 4, 2048], F32, 0)
    hi = at("hi", [P, 4, 2048], F32R, 32 * K)
    lo = at("lo", [P, 4, 2048], F32R, 64 * K)
    XO = 96 * K
    x = at("x", [P, TOK, D], F32, XO)
    hTh = at("hTh", [P, KT, SEQ], F32R, 112 * K)
    hTl = at("hTl", [P, KT, SEQ], F32R, 128 * K)
    A = 144 * K
    memraw = at("memraw", [P, TOK, D], F32, 112 * K)
    memTh = at("memTh", [P, KT, SEQ], F32R, A)
    memTl = at("memTl", [P, KT, SEQ], F32R, A + 16 * K)
    qkT = at("qkT", [P, 24, SEQ], F32, A)
    vAB = at("vAB", [P, TOK, 8, HD], F32, A + 24 * K)
    kcT = at("kcT", [P, C_HEADS, SEQ], F32, A + 32 * K)
    vC = at("vC", [P, TOK, C_HEADS, HD], F32, A + 36 * K)
    hank = at("hank", [P, 2, 384], F32, A + 40 * K)
    rope = at("rope", [P, 2, TOK, HD], F32, A + 43 * K)
    stage = at("stage", [P, TOK, 512], F32, A + 45 * K)
    stage2 = at("stage2", [P, TOK, 512], F32, A + 49 * K)
    fold = at("fold", [P, 2, 4, SEQ], F32, A + 45 * K)
    probs = at("probs", [P, TOK, SEQ], F32, A + 45 * K)
    probsT = at("probsT", [P, TOK, SEQ], F32, A + 49 * K)
    gst = at("gst", [P, TOK, 512], F32, A + 53 * K)
    obuf = at("obuf", [P, TOK, HEADS, HD], F32, XO)
    tabs = at("tabs", [32, 6], F32, A + 38 * K)
    oneh = at("oneh", [32, 512], F32, A + 32 * K)
    dmask = at("dmask", [6, 512], F32, A + 34 * K)
    bvec = at("bvec", [6, 512], F32, A + 36 * K)
    oTh = at("oTh", [P, 12, SEQ], F32R, A)
    oTl = at("oTl", [P, 12, SEQ], F32R, A + 12 * K)
    merged = at("merged", [P, TOK, D], F32, A + 24 * K)
    gl = at("gl", [P, 4, TOK, 512], F32, XO)
    mt0 = at("mt0", [P, TOK, 512], F32, A + 40 * K)
    mt1 = at("mt1", [P, TOK, 512], F32, A + 53 * K)
    xn = at("xn", [P, TOK, D], F32, A + 24 * K)
    adaraw = at("adaraw", [P, 2, 2, 1024], F32, A)
    adaacc = at("adaacc", [P, 1024], F32, A + 16 * K)
    modrow = at("modrow", [1, 1024], F32, A + 20 * K)
    gact = at("gact", [P, TOK, 512], F32, A + 40 * K)
    fact = at("fact", [P, TOK, 512], F32, A + 53 * K)
    factTh = at("factTh", [P, 4, SEQ], F32R, A + 45 * K)
    factTl = at("factTl", [P, 4, SEQ], F32R, A + 49 * K)
    qkT2 = at("qkT2", [P, 16, SEQ], F32, A)
    v2 = at("v2", [P, TOK, LRU], F32, A + 16 * K)
    lxT = at("lxT", [P, 8, 260], F32, A + 24 * K)
    dec = at("dec", [P, 8, SEQ], F32, A + 24 * K)
    gyT = at("gyT", [P, 8, SEQ], F32, A + 33 * K)
    istage = at("istage", [P, 2, SEQ], F32, A + 41 * K)
    wf = at("wf", [P, KT, 8], F32, A + 43 * K)
    wfh = at("wfh", [P, KT, 8], F32R, A + 43 * K + 512)
    wfl = at("wfl", [P, KT, 8], F32R, A + 44 * K)
    lwx = at("lwx", [P, 8, P], F32, A + 49 * K)
    lwa = at("lwa", [P, 8, P], F32, A + 53 * K)
    uT = at("uT", [P, 8, SEQ], F32, XO)
    bx = at("bx", [P, 8, SEQ], F32, XO + 8 * K)
    sel = at("sel", [8, 8, SEQ], F32, A + 24 * K)
    probs2 = at("probs2", [P, 2, TOK, SEQ], F32, A + 41 * K)
    probsT2 = at("probsT2", [P, 2, TOK, SEQ], F32, A + 53 * K)
    att2 = at("att2", [P, TOK, H2, HD], F32, XO)
    lsq = at("lsq", [P, 8, SEQ], F32, XO + 8 * K)
    lgate = at("lgate", [8, 4, SEQ], F32, A + 49 * K)
    ga1 = at("ga1", [P, D], F32, A)
    mt2 = at("mt2", [P, TOK, 512], F32, A + 8 * K)
    lrs = at("lrs", [P, 2, SEQ], F32, A + 12 * K)
    pqT = at("pqT", [P, 16, SEQ], F32, A)
    keysT = at("keysT", [P, 16, P], F32, A + 16 * K)
    sc = at("sc", [P, TOK, 16, N_KEYS], F32, A + 24 * K)
    cand = at("cand", [P, 8, 256], F32, A)
    work = at("work", [P, 8, 256], F32, A + 8 * K)
    work2 = at("work2", [P, 8, 256], F32, A + 16 * K)
    top = at("top", [P, TOK, 16, TOPK], F32, A + 40 * K)
    topi = at("topi", [P, TOK, 16, TOPK], U32, A + 42 * K)
    topf = at("topf", [P, TOK, 16, TOPK], F32, A + 44 * K)
    picks = at("picks", [P, TOK, 3, 8, TOPK], F32, A + 46 * K)
    best = at("best", [P, TOK, 8, TOPK], F32, A + 49 * K)
    besti = at("besti", [P, TOK, 8, TOPK], U32, A + 50 * K)
    divi = at("divi", [P, 2, 8, TOPK], U32, A + 51 * K)
    divf = at("divf", [P, 2, 8, TOPK], F32, A + 52 * K)
    picksT = at("picksT", [P, 3, SEQ], F32, A + 40 * K)
    gacc = at("gacc", [P, TOK, 512], F32, A + 53 * K)
    oh = at("oh", [P, 2, 2, 8, P], F32, A + 24 * K)
    wst = at("wst", [P, 2, 8, P], F32, A + 16 * K)
    y = at("y", [P, TOK, D], F32, A)
    wc = at("wc", [P, 2, TOK, 512], F32, A + 16 * K)
    pact = at("pact", [P, TOK, 512], F32, A + 24 * K)
    pactTh = at("pactTh", [P, 2, 4, SEQ], F32R, A + 28 * K)
    pactTl = at("pactTl", [P, 2, 4, SEQ], F32R, A + 36 * K)
    hid = at("hid", [P, 2, TOK, 512], F32, A + 44 * K)
    ga2 = at("ga2", [P, D], F32, A + 40 * K)
    gfin = at("gfin", [P, D], F32, A + 16 * K)

    CO = A + 57 * K
    ident = at("ident", [P, P], F32, CO)
    anti = at("anti", [P, P], F32, CO + 512)
    ones = at("ones", [P, P], F32, CO + 1 * K)
    iota = at("iota", [P, P], F32, CO + 1 * K + 512)
    cols = at("cols", [P, NCOLS], F32, CO + 2 * K)
    gb = at("gb", [P, 2, HD], F32, CO + 3 * K)
    causal = at("causal", [P, 384], F32, CO + 4 * K)
    small_at = [CO + 5 * K + 512]

    def small(name, shape, dt=F32):
        words = int(np.prod(shape[1:]))
        h = at(name, shape, dt, small_at[0])
        small_at[0] += -(-words * 4 // 32) * 32
        return h

    ssum = small("ssum", [P, TOK])
    sq = small("sq", [P, TOK, 4])
    rstd = small("rstd", [P, 2, TOK])
    hss = small("hss", [P, 3, 8])
    fs = small("fs", [P, TOK, 8])
    cs = small("cs", [P, 16])
    modT = small("modT", [P, 4, 16])
    gmod = small("gmod", [P, 16])
    lam = small("lam", [P, 4, 8])
    spn = small("spn", [P, 2, 8])
    negm = small("negm", [P, TOK, HEADS])
    lsum = small("lsum", [P, TOK, HEADS])
    fac = small("fac", [P, TOK, HEADS])
    cmb = small("cmb", [P, 2, TOK, 6])
    cmx = small("cmx", [P, 2, TOK, 2])
    assert base0 + small_at[0] <= 229368, small_at
    wsm = at("wsm", [P, TOK, 8, 2], F32, CO + 4 * K)

    ps = nc.alloc_psum_tensor("ps", [P, 8, 512], F32)

    def pair(b):
        return ps[:, b:b + 2, :]

    def quarters(b):
        return ps[:, b:b + 2, :].rearrange("p b (k t) -> p (b k) t", t=SEQ)

    def fold_bank(f):
        return 4 if FOLD_M <= f < FOLD_FFN else 4 + 2 * (f % 2)

    bias_d = nc.dram_tensor("bias_scratch", [6, 512], F32, kind="Internal").ap()
    gates_d = nc.dram_tensor("gates_scratch", [12, P, TOK * 512], F32, kind="Internal").ap()
    mod_d = nc.dram_tensor("mod_scratch", [ADA], F32, kind="Internal").ap()
    x_d = nc.dram_tensor("x_scratch", [P, TOK * D], F32, kind="Internal").ap()
    w_d = nc.dram_tensor("w_scratch", [SEQ, EXPERTS], F32, kind="Internal").ap()
    hid_d = nc.dram_tensor("hidden_scratch", [EARLY - 1, P, TOK * 512], F32, kind="Internal").ap()

    sems = {}

    def sem(name):
        if name not in sems:
            sems[name] = nc.alloc_semaphore(name)
        return sems[name]

    raw_in = [sem(f"raw_in{s}") for s in range(4)]
    hi_done, lo_done, piece_used = sem("hi_done"), sem("lo_done"), sem("piece_used")
    head_quads = [0, 2, 3, 4, 5, 6, 7]
    ADA_IN = [sem("ada_in0"), sem("ada_in1")]

    with nc.Block() as block:

        @block.sync
        def _(sp):
            sp.dma_start(ident[:], t["ident"]).then_inc(sem("ident_in"), 16)
            for c in range(4):
                cut = slice(512 * c, 512 * c + 512)
                sp.dma_start(memraw[:, :, cut], t["mem"].rearrange("(k p) d -> p k d", p=P)[:, :, cut])\
                    .then_inc(sem(f"mem_in{c // 2}"), 16)
            sp.dma_start(cols[:], t["cols"]).then_inc(sem("cols_in"), 16)

            def load(src, q, n):
                for s in range(4):
                    if not isinstance(q, int) or q >= 1:
                        sp.wait_ge(lo_done, 4 * q + (s - 3))
                    sp.dma_start(raw[:, s, :], src[4 * n + s]).then_inc(raw_in[s], 16)

            load(t["w_first"], 0, 0)
            sp.dma_start(x[:], t["x"].rearrange("(k p) d -> p k d", p=P)).then_inc(sem("x_in"), 16)
            for dst, src in ((anti, "anti"), (cs, "c"), (iota, "iota"), (causal, "causal"), (tabs, "rel_bias"),
                             (oneh, "oneh"), (dmask, "dmask"), (rope, "rope")):
                sp.dma_start(dst[:], t[src]).then_inc(sem("const_in"), 16)
            sp.dma_start(gb[:, 0, :], t["g_qb"].to_broadcast([P, HD])).then_inc(sem("const_in"), 16)
            sp.dma_start(gb[:, 1, :], t["g_kb"].to_broadcast([P, HD])).then_inc(sem("const_in"), 16)
            with sp.Fori(1, Q_BRANCH) as n:
                load(t["w_first"], n, n)
            with sp.Fori(0, Q_FFN - Q_BRANCH) as n:
                load(t["w_merge"], n + Q_BRANCH, n)
            with sp.Fori(0, 3 * FF_GROUPS) as n:
                load(t["w_ffn"], n + Q_FFN, n)
            with sp.Fori(0, Q_PEER - Q_IN2) as n:
                load(t["w_second"], n + Q_IN2, n)
            with sp.Fori(0, 2 * PEER_GROUPS) as n:
                load(t["w_peer"], n + Q_PEER, n)
            sp.wait_ge(sem("final"), 2)
            sp.dma_start(t["out"].rearrange("(k p) d -> p k d", p=P), x[:]).then_inc(sem("out_st"), 16)
            sp.wait_ge(sem("out_st"), 16)

        @block.gpsimd
        def _(pool):
            def rest_piece(q, s):
                pool.wait_ge(hi_done, 4 * q + (s + 1))
                if not isinstance(q, int) or q >= 1:
                    pool.wait_ge(piece_used, 4 * q + (s - 3))
                nc.gpsimd.tensor_tensor(lo[:, s, :], raw[:, s, :], hi[:, s, :].bitcast(F32), ALU.subtract)\
                    .then_inc(lo_done, 1)

            for s in range(4):
                rest_piece(0, s)
            pool.wait_ge(sem("bvec"), 1)
            pool.dma_start(bias_d, bvec[:]).then_inc(sem("bias_st"), 16)
            pool.wait_ge(sem("bias_st"), 16)

            def load_hankel(h):
                if h >= 2:
                    pool.wait_ge(sem("att_s"), h - 1)
                src = bass.AP(bias_d.tensor, h * 512, [[1, P], [1, 384]])
                pool.dma_start(hank[:, h % 2, :], src).then_inc(sem(f"hank_in{h % 2}"), 16)

            load_hankel(0)
            load_hankel(1)

            def store_gates(c):
                pool.wait_ge(sem("chunk_out"), Q_GATES + c + 1)
                pool.dma_start(gates_d[c], gst[:].rearrange("p k n -> p (k n)")).then_inc(sem("gate_st"), 16)

            for n in range(48):
                if n % 3 == 0 and n // 3 + 2 < A_HEADS:
                    load_hankel(n // 3 + 2)
                if n % 4 == 3:
                    store_gates(n // 4)
            pool.wait_ge(lo_done, 4 * (Q_BRANCH + 1))
            for n in range(12):
                rest_piece(Q_BRANCH + 1 + n // 4, n % 4)
            pool.wait_ge(sem("merge"), 4)
            pool.dma_start(x[:], t["x"].rearrange("(k p) d -> p k d", p=P)).then_inc(sem("x_back"), 16)

            pool.wait_ge(piece_used, 4 * Q_WO)

            def ada_piece(a, j, first):
                if not first:
                    pool.wait_ge(sem("ada_used"), 8 * a + (j - 1))
                pool.dma_start(adaraw[:, j % 2, :, :].rearrange("p k n -> p (k n)"), t["w_ada"][8 * a + j])\
                    .then_inc(ADA_IN[j % 2], 16)

            def ada_row_in(a):
                pool.dma_start(modrow[:], t["b_ada"][a]).then_inc(sem("bada_in"), 16)

            def ada_row_out(a):
                pool.wait_ge(sem("modrow"), 2 * a)
                pool.dma_start(mod_d.rearrange("(a o n) -> a o n", o=1, n=1024)[a - 1],
                               modrow[0:1, :]).then_inc(sem("mod_st"), 16)
                pool.wait_ge(sem("mod_st"), 16 * a)

            for j in range(8):
                ada_piece(0, j, j < 2)
                if j == 3:
                    ada_row_in(0)
            with pool.Fori(1, ADA_SPLITS) as a:
                for j in range(8):
                    ada_piece(a, j, False)
                    if j == 3:
                        ada_row_out(a)
                        ada_row_in(a)
            ada_row_out(ADA_SPLITS)
            for k, part in enumerate((0, 1, 3, 4)):
                with nc.allow_non_contiguous_dma(reason="a column of the modulation for each partition"):
                    pool.dma_start(modT[:, k, :], mod_d[part * D:(part + 1) * D].rearrange("(k p) -> p k", p=P))\
                        .then_inc(sem("modT_in"), 16)
            pool.wait_ge(sem("xn_done"), 8 * 4)
            pool.dma_start(x_d, x[:].rearrange("p k n -> p (k n)")).then_inc(sem("x_st"), 16)
            pool.dma_start(wf[:], t["w_f"]).then_inc(sem("wf_in"), 16)
            pool.dma_start(lwa[:], t["lru_w_a"]).then_inc(sem("lw_in"), 16)
            pool.wait_ge(sem("fold_lo"), FOLD_ATT)
            pool.dma_start(lwx[:], t["lru_w_x"]).then_inc(sem("lw_in"), 16)
            pool.wait_ge(sem("scan"), 8)
            pool.dma_start(sel[:], t["sel"]).then_inc(sem("sel_in"), 16)
            pool.wait_ge(sem("fold_tr"), FOLD_LRU)
            pool.wait_ge(sem("lru_ms"), 1)
            pool.dma_start(x[:].rearrange("p k n -> p (k n)"), x_d).then_inc(sem("x_back"), 16)
            pool.dma_start(ga1[:], bass.AP(mod_d.tensor, 2 * D, [[0, P], [1, D]])).then_inc(sem("ga1_in"), 16)
            pool.wait_ge(sem("xn_done"), 8 * 5)
            pool.dma_start(keysT[:], t["keys"]).then_inc(sem("keys_in"), 16)

            pool.wait_ge(lo_done, 4 * (Q_PEER + 1))
            with pool.Fori(0, EARLY - 1) as g:
                for s in range(4):
                    rest_piece(g + (Q_PEER + 1), s)

            def load_group(g, u):
                pool.dma_start(wc[:, u], (w_d[:, bass.ds(g * 512, 512)] if not isinstance(g, int) else
                                          w_d[:, 512 * g:512 * g + 512]).rearrange("(k p) n -> p k n", p=P))\
                    .then_inc(sem(f"wc_in{u}"), 16)
                if not isinstance(g, int) or g < EARLY - 1:
                    pool.dma_start(hid[:, u].rearrange("p k n -> p (k n)"), hid_d[g]).then_inc(sem(f"hid_in{u}"), 16)

            for u in range(2):
                pool.wait_ge(sem(f"w_st{u}"), 16 * (SEQ // 16))
            pool.wait_ge(sem("hid_st"), 16 * (EARLY - 1))
            load_group(0, 0)
            load_group(1, 1)
            with pool.Fori(1, (EARLY - 1) // 2) as m:
                for u in range(2):
                    pool.wait_ge(sem("pmul"), 2 * m + (u - 1))
                    load_group(2 * m + u, u)
            pool.wait_ge(sem("pmul"), EARLY - 2)
            load_group(EARLY - 1, 0)
            with pool.Fori(EARLY, PEER_GROUPS) as g:
                pool.wait_ge(sem("pmul"), g)
                pool.dma_start(wc[:, 0], w_d[:, bass.ds(g * 512, 512)].rearrange("(k p) n -> p k n", p=P))\
                    .then_inc(sem("wc_in0"), 16)
            pool.wait_ge(sem("pmul"), PEER_GROUPS)
            pool.dma_start(ga2[:], bass.AP(mod_d.tensor, 5 * D, [[0, P], [1, D]])).then_inc(sem("tail_in"), 16)
            pool.dma_start(gfin[:], t["g_final"].to_broadcast([P, D])).then_inc(sem("tail_in"), 16)

        @block.scalar
        def _(act):
            a_seq = [0]

            def round_piece(q, s):
                act.wait_ge(raw_in[s], 16 * q + 16)
                if not isinstance(q, int) or q >= 1:
                    act.wait_ge(piece_used, 4 * q + (s - 3))
                nc.scalar.copy(hi[:, s, :], raw[:, s, :]).then_inc(hi_done, 1)

            def squares(u, c, src):
                for k in range(TOK):
                    n = 8 * u + 2 * c + k
                    if n >= 2:
                        act.wait_ge(sem("sq_done"), n - 1)
                    nc.scalar.activation(gst[:, k], src[:, k, 512 * c:512 * c + 512], ACT.Square,
                                         accum_out=sq[:, k, c:c + 1]).then_inc(sem("sq_done"), 1)

            def norm(u, src, f0, dst_t, between=lambda g: None):
                dst = src if u < 2 else xn
                act.wait_ge(sem("ms_done"), u + 1)
                nc.scalar.activation(rstd[:, 0, :], ssum[:], ACT.Sqrt).then_inc(sem("root_done"), 1)
                act.wait_ge(sem("rstd_done"), u + 1)

                def scaled(c):
                    for k in range(TOK):
                        cut = slice(512 * c, 512 * c + 512)
                        nc.scalar.activation(dst[:, k, cut], src[:, k, cut], ACT.Copy, scale=rstd[:, 1, k:k + 1])\
                            .then_inc(sem("xn_done"), 1)

                scaled(0)
                scaled(1)
                for g in range(4):
                    fold_hi(f0 + g, dst_t, 4 * g)
                    between(g)
                    if g < 2:
                        scaled(g + 2)

            def fold_hi(f, dst, at0):
                act.wait_ge(sem("fold_t"), f + 1)
                nc.scalar.copy(dst[:, at0:at0 + 4, :], fold[:, f % 2]).then_inc(sem("fold_hi"), 1)

            for c in range(4):
                act.wait_ge(sem(f"mem_in{c // 2}"), 32)
                squares(0, c, memraw)
            norm(0, memraw, FOLD_MEM, memTh, lambda g: round_piece(0, g))
            act.wait_ge(sem("x_in"), 16)
            for c in range(4):
                squares(1, c, x)
            for s in range(2):
                round_piece(1, s)
            act.wait_ge(sem("fold_tr"), FOLD_X)
            norm(1, x, FOLD_X, hTh, lambda g: round_piece(1, 2 + g) if g < 2 else None)
            for q in range(Q_GATES):
                if q >= 1:
                    for s in range(4):
                        round_piece(q + 1, s)
                act.wait_ge(piece_used, 4 * q + 4)
                if q in head_quads:
                    n = head_quads.index(q)
                    if n == 0:
                        act.wait_ge(sem("fold_lo"), FOLD_O)
                    else:
                        act.wait_ge(sem("head_tr"), n)
                    nc.scalar.copy(stage[:], pair(2 * (q % 2))).then_inc(sem("chunk_out"), 1)
                    act.wait_ge(sem("head_ms"), n + 1)
                    nc.scalar.activation(hss[:, 1, :], hss[:, 0, :], ACT.Sqrt).then_inc(sem("head_root"), 1)
                else:
                    if q == 1:
                        act.wait_ge(sem("bias_st"), 16)
                    dst = vC[:] if q == 1 else vAB[:, :, 4 * (q - 8):4 * (q - 8) + 4, :]
                    src = pair(2 * (q % 2)).rearrange("p k (h d) -> p k h d", d=HD)
                    nc.scalar.copy(dst, src).then_inc(sem("chunk_out"), 1)
            for n in range(48):
                q, s = divmod(4 * Q_GATES + n, 4)
                round_piece(q + 1, s)
                if s == 3:
                    c = q - Q_GATES
                    if c >= 1:
                        act.wait_ge(sem("gate_st"), 16 * c)
                    act.wait_ge(piece_used, 4 * q + 4)
                    nc.scalar.activation(gst[:], pair(2 * (q % 2)), ACT.Tanh, scale=0.5)\
                        .then_inc(sem("chunk_out"), 1)
                if n % 3 == 0:
                    h = n // 3
                    act.wait_ge(sem("att_m"), h + 1)
                    if h >= 1:
                        act.wait_ge(sem("att_t"), h)
                    for k in range(TOK):
                        nc.scalar.activation(probs[:, k, :], ps[:, 4, SEQ * k:SEQ * k + SEQ], ACT.Exp,
                                             bias=negm[:, k, h:h + 1], accum_out=lsum[:, k, h:h + 1])\
                            .then_inc(sem("att_e"), 1)
                if n == 19:
                    act.wait_ge(sem("cmb_d"), 1)
                    nc.scalar.activation(cmb[:, 1], cmb[:, 0], ACT.Exp).then_inc(sem("cmb_e"), 1)
            for f in range(3):
                fold_hi(FOLD_O + f, oTh, 4 * f)

            def load_gate(n):
                j, part = divmod(n, 3)
                act.dma_start(gl[:, n % 4].rearrange("p k n -> p (k n)"), gates_d[4 * part + j])\
                    .then_inc(sem(f"gl_in{n % 4}"), 16)

            act.wait_ge(sem("gate_st"), 16 * 12)
            act.wait_ge(sem("fold_tr"), FOLD_M)
            for n in range(3):
                load_gate(n)
            for n in range(12):
                q, s = divmod(4 * Q_BRANCH + n, 4)
                round_piece(q + 1, s)
                if n + 3 < 12:
                    if n >= 1:
                        act.wait_ge(sem("gated"), n)
                    load_gate(n + 3)
                if n % 3 == 1 and n >= 4:
                    fold_hi(FOLD_M + n // 3 - 1, hTh, 4 * (n // 3 - 1))
            nc.scalar.activation(cs[:], cs[:], ACT.Silu).then_inc(sem("cs_done"), 1)
            for n in range(16):
                q, s = divmod(4 * Q_WO + n, 4)
                round_piece(q + 1, s)
                if n == 0:
                    fold_hi(FOLD_M + 3, hTh, 12)
                if n % 4 == 1 and n >= 4:
                    act.wait_ge(sem("wo_out"), n // 4)
                    squares(2, n // 4 - 1, x)
            act.wait_ge(sem("wo_out"), 4)
            squares(2, 3, x)
            norm(2, x, FOLD_FFN, hTh)

            def silu(g):
                act.wait_ge(piece_used, 4 * Q_FFN + 4 if isinstance(g, int) else 12 * g + 4 * Q_FFN)
                if not isinstance(g, int):
                    act.wait_ge(sem("fmul"), g)
                nc.scalar.activation(gact[:], pair(0), ACT.Silu).then_inc(sem("silu"), 1)

            def gate_up_down(b, j):
                round_piece(3 * b + (Q_FFN + 2 + j // 4 + 1), j % 4)

            for j in range(8):
                q, s = divmod(4 * Q_FFN + j, 4)
                round_piece(q + 1, s)
                if j == 3:
                    silu(0)

            def ffn_hi(b):
                act.wait_ge(sem("ffn_tr"), b + 1)
                nc.scalar.copy(factTh[:], quarters(4)).then_inc(sem("ffn_hi"), 1)

            with act.Fori(0, FF_GROUPS - 1) as b:
                for j in range(12):
                    gate_up_down(b, j)
                    if j == 1:
                        ffn_hi(b)
                    if j == 3:
                        silu(b + 1)
            ffn_hi(FF_GROUPS - 1)
            for j in range(5):
                if j < 4:
                    round_piece(Q_IN2, j)
                if j >= 1:
                    act.wait_ge(sem("x_sum"), 4 * (FF_GROUPS - 1) + j + 1)
                    squares(3, j - 1, x)
            norm(3, x, FOLD_MIX2, hTh)
            act.wait_ge(sem("wf_in"), 16)
            nc.scalar.copy(wfh[:], wf[:]).then_inc(sem("wfh"), 1)
            act.wait_ge(sem("lam_n"), 1)
            nc.scalar.activation(lam[:, 1, :], lam[:, 0, :], ACT.Exp).then_inc(sem("lam_e"), 1)

            for c in range(10):
                q = Q_IN2 + c
                for s in range(4):
                    round_piece(q + 1, s)
                act.wait_ge(piece_used, 4 * q + 4)
                if c < 8:
                    if c >= 1:
                        act.wait_ge(sem("in_tr"), c)
                    else:
                        act.wait_ge(sem("fold_lo"), FOLD_ATT)
                    nc.scalar.copy(stage[:], pair(2 * (c % 2))).then_inc(sem("in_out"), 1)
                else:
                    nc.scalar.copy(v2[:, :, 512 * (c - 8):512 * (c - 8) + 512], pair(2 * (c % 2)))\
                        .then_inc(sem("in_out"), 1)
                if c in (3, 4):
                    n = c - 3
                    act.wait_ge(sem("in_tr"), 3 + n)
                    nc.scalar.activation(gyT[:, 4 * n:4 * n + 4, :], quarters(4), ACT.Gelu_apprx_tanh)\
                        .then_inc(sem("gy_T"), 1)
                if c == 4:
                    for n in range(8):
                        act.wait_ge(sem("ri"), n + 1)
                        nc.scalar.activation(uT[:, n, :], ps[:, 6 + n % 2, 0:SEQ], ACT.Sigmoid,
                                             bias=cols[:, C_BA + n:C_BA + n + 1]).then_inc(sem("r_out"), 1)
                        if n >= 2:
                            act.wait_ge(sem("i_used"), n - 1)
                        nc.scalar.activation(istage[:, n % 2, :], ps[:, 6 + n % 2, SEQ:2 * SEQ], ACT.Sigmoid,
                                             bias=cols[:, C_BX + n:C_BX + n + 1]).then_inc(sem("i_out"), 1)
                    act.wait_ge(sem("sp_done"), 1)
                    act.wait_ge(sem("conv"), 8)
                    act.wait_ge(sem("r_out"), 8)
                    for n in range(8):
                        nc.scalar.activation(dec[:, n, :], uT[:, n, :], ACT.Exp, scale=spn[:, 0, n:n + 1])\
                            .then_inc(sem("dec"), 1)
                        nc.scalar.activation(uT[:, n, :], uT[:, n, :], ACT.Tanh, scale=spn[:, 1, n:n + 1])\
                            .then_inc(sem("tanh"), 1)
                if c == 6:
                    act.wait_ge(sem("tanh"), 8)
                    nc.scalar.activation(uT[:], uT[:], ACT.Sqrt).then_inc(sem("root2"), 1)
            act.wait_ge(sem("lg_abs"), 1)
            nc.scalar.activation(lgate[:, 1, :], lgate[:, 1, :], ACT.Exp, scale=-1.0).then_inc(sem("lg_exp"), 1)
            for h in range(H2):
                act.wait_ge(sem("m2"), h + 1)
                if h >= 2:
                    act.wait_ge(sem("t2"), h - 1)
                for k in range(TOK):
                    nc.scalar.activation(probs2[:, h % 2, k, :], ps[:, h % 2, SEQ * k:SEQ * k + SEQ], ACT.Exp,
                                         bias=negm[:, k, h:h + 1], accum_out=lsum[:, k, h:h + 1])\
                        .then_inc(sem("e2"), 1)
            act.wait_ge(sem("att2_n"), 1)
            for k in range(TOK):
                nc.scalar.activation(stage2[:].rearrange("p a b -> p (a b)"), att2[:, k].rearrange("p h d -> p (h d)"),
                                     ACT.Square, accum_out=ssum[:, k:k + 1]).then_inc(sem("ssq2"), 1)
                act.wait_ge(sem("ssq2"), k + 1)
            act.wait_ge(sem("ms2"), 1)
            nc.scalar.activation(rstd[:, 0, :], ssum[:], ACT.Sqrt).then_inc(sem("ms2_root"), 1)
            act.wait_ge(sem("rstd2"), 1)
            for k in range(TOK):
                nc.scalar.activation(att2[:, k], att2[:, k], ACT.Copy, scale=rstd[:, 1, k:k + 1])\
                    .then_inc(sem("att2_s"), 1)
            for f in range(2):
                fold_hi(FOLD_ATT + f, hTh, 4 * f)
            act.wait_ge(sem("lru_ms"), 1)
            nc.scalar.activation(lrs[:, 0, :], lrs[:, 0, :], ACT.Sqrt).then_inc(sem("lru_root"), 1)
            for f in range(2):
                fold_hi(FOLD_LRU + f, hTh, 8 + 4 * f)
            for c in range(4):
                for s in range(4):
                    round_piece(Q_OUT2 + c + 1, s)
                    if s == 1 and c >= 1:
                        act.wait_ge(sem("out2_sum"), c)
                        squares(4, c - 1, x)
            act.wait_ge(sem("out2_sum"), 4)
            squares(4, 3, x)
            norm(4, x, FOLD_PEER, hTh)
            for c in range(4):
                q = Q_PQ + c
                for s in range(4):
                    round_piece(q + 1, s)
                act.wait_ge(piece_used, 4 * q + 4)
                if c >= 1:
                    act.wait_ge(sem("pq_tr"), c)
                else:
                    act.wait_ge(sem("fold_lo"), FOLD_PEER + 4)
                nc.scalar.copy(stage[:], pair(2 * (c % 2))).then_inc(sem("pq_out"), 1)

            def gelu(g, u, out=True):
                act.wait_ge(piece_used, 4 * g + 4 * (Q_PEER + 1))
                if not isinstance(g, int) or g > 0:
                    act.wait_ge(sem("hid_st"), 16 * g)
                nc.scalar.activation(gacc[:], pair(2 * u), ACT.Gelu_apprx_tanh).then_inc(sem("gelu"), 1)
                if out:
                    act.wait_ge(sem("gelu"), g + 1)
                    act.dma_start(hid_d[g], gacc[:].rearrange("p k n -> p (k n)")).then_inc(sem("hid_st"), 16)

            def early_group(g, u, mid):
                for s in range(4):
                    round_piece(g + (Q_PEER + 1), s)
                    mid(s)
                gelu(g, u)

            early_group(0, 0, lambda s: None)
            early_group(1, 1, lambda s: None)
            with act.Fori(1, EARLY_TOP // 2 - 1) as m:
                for u in range(2):
                    early_group(2 * m + u, u, lambda s: None)

            def choice_exp(s):
                if s == 1:
                    act.wait_ge(sem("wexp_in"), 1)
                    nc.scalar.activation(picks[:, :, 2], picks[:, :, 2], ACT.Exp).then_inc(sem("wexp"), 1)

            early_group(EARLY_TOP - 2, 0, lambda s: None)
            early_group(EARLY_TOP - 1, 1, choice_exp)

            def weights_out(i, v, first):
                act.wait_ge(sem("wmm"), 2 * i + (v + 1))
                if not first:
                    act.wait_ge(sem(f"w_st{v}"), 16 * i)
                nc.scalar.copy(wst[:, v].rearrange("p t b -> p (t b)"),
                               ps[:, 4 + 2 * v:6 + 2 * v, :].rearrange("p b n -> p (b n)")).then_inc(sem("wst"), 1)
                act.wait_ge(sem("wst"), 2 * i + (v + 1))
                rows = slice(16 * i + 8 * v, 16 * i + 8 * v + 8) if isinstance(i, int) else bass.ds(16 * i + 8 * v, 8)
                act.dma_start(w_d[rows].rearrange("t (a b) -> a t b", b=N_KEYS), wst[:, v]).then_inc(sem(f"w_st{v}"), 16)

            def weights_pair(i, first=False):
                for v in range(2):
                    weights_out(i, v, first)

            early_group(EARLY_TOP, 0, lambda s: weights_pair(s, s == 0))
            early_group(EARLY_TOP + 1, 1, lambda s: weights_pair(4 + s))
            early_group(EARLY_TOP + 2, 0, lambda s: weights_pair(8 + s))
            early_group(EARLY_TOP + 3, 1, lambda s: weights_pair(12 + s))

            def peer_hi(b, u):
                act.wait_ge(sem("peer_tr"), b + 1)
                nc.scalar.copy(pactTh[:, u], quarters(4)).then_inc(sem("peer_hi"), 1)

            for s in range(4):
                round_piece(Q_PEER + EARLY, s)
                if s == 2:
                    peer_hi(0, 0)
            gelu(EARLY - 1, 0, out=False)

            def down_group(b, u, turn=True):
                for j in range(4):
                    round_piece(b + (Q_PEER + EARLY + 1), j)
                    if j == 2 and turn:
                        act.wait_ge(piece_used, 4 * b + 4 * (Q_PEER + EARLY))
                        peer_hi(b + 1, 1 - u)

            with act.Fori(0, (EARLY - 1) // 2 - 1) as m:
                for u in range(2):
                    down_group(2 * m + u, u)
            down_group(EARLY - 3, 0)
            down_group(EARLY - 2, 1, turn=False)

            with act.Fori(EARLY - 1, PEER_GROUPS - 1) as b:
                for j in range(8):
                    round_piece(2 * b + (Q_PEER + 1 + j // 4 + 1), j % 4)
                    if j == 1:
                        peer_hi(b, 0)
                    if j == 3:
                        act.wait_ge(piece_used, 8 * b + (4 * Q_PEER + 8))
                        act.wait_ge(sem("pmul"), b + 1)
                        nc.scalar.activation(gacc[:], pair(0), ACT.Gelu_apprx_tanh).then_inc(sem("gelu"), 1)
            peer_hi(PEER_GROUPS - 1, 0)
            act.wait_ge(sem("x_ready"), 1)
            for k in range(TOK):
                nc.scalar.activation(y[:, k, :], x[:, k, :], ACT.Square, accum_out=ssum[:, k:k + 1])\
                    .then_inc(sem("sq_done"), 1)
            act.wait_ge(sem("ms_done"), 6)
            nc.scalar.activation(rstd[:, 0, :], ssum[:], ACT.Sqrt).then_inc(sem("root_done"), 1)

        @block.vector
        def _(dve):
            seq = [0]

            def step(ins):
                seq[0] += 1
                ins.then_inc(sem("dve_seq"), 1)
                dve.wait_ge(sem("dve_seq"), seq[0])

            V = nc.vector

            def rest_piece(q, s):
                dve.wait_ge(hi_done, 4 * q + (s + 1))
                if not isinstance(q, int) or q >= 1:
                    dve.wait_ge(piece_used, 4 * q + (s - 3))
                V.tensor_tensor(lo[:, s, :], raw[:, s, :], hi[:, s, :].bitcast(F32), ALU.subtract).then_inc(lo_done, 1)

            def rest_quad(q):
                for s in range(4):
                    rest_piece(q, s)

            def fold_lo(f, dst, at0):
                dve.wait_ge(sem("fold_hi"), f + 1)
                V.tensor_tensor(dst[0][:, at0:at0 + 4, :], fold[:, f % 2], dst[1][:, at0:at0 + 4, :].bitcast(F32),
                                ALU.subtract).then_inc(sem("fold_lo"), 1)

            def fold_ready(f, turned):
                if turned is not None:
                    dve.wait_ge(sem("fold_tr"), turned)
                if f >= 2:
                    dve.wait_ge(sem("fold_hi"), f - 1)
                    dve.wait_ge(sem("fold_lo"), f - 1)

            def stats(u):
                dve.wait_ge(sem("sq_done"), 8 * u + 8)
                step(V.tensor_reduce(ssum[:], sq[:], AX.X, ALU.add))
                V.tensor_scalar(ssum[:], ssum[:], 1.0 / D, EPS, ALU.mult, ALU.add).then_inc(sem("ms_done"), 1)
                dve.wait_ge(sem("root_done"), u + 1)
                V.reciprocal(rstd[:, 1, :], rstd[:, 0, :]).then_inc(sem("rstd_done"), 1)

            def folds(u, f0, scale_at, shift, scale_tile=None, between=lambda g: None):
                src = cols if scale_tile is None else scale_tile
                th, tl = (memTh, memTl) if u == 0 else (hTh, hTl)
                for g in range(4):
                    f = f0 + g
                    turned = f + 1 if f < FOLD_LRU else f - 1
                    fold_ready(f, turned)
                    for k in range(4):
                        kt = 4 * g + k
                        col = src[:, scale_at + kt:scale_at + kt + 1]
                        if shift is None:
                            ins = V.tensor_scalar(fold[:, f % 2, k], quarters(fold_bank(f))[:, k], col, None, ALU.mult)
                        else:
                            ins = V.tensor_scalar(fold[:, f % 2, k], quarters(fold_bank(f))[:, k], col,
                                                  modT[:, shift, kt:kt + 1], ALU.mult, ALU.add)
                    ins.then_inc(sem("fold_t"), 1)
                    if g >= 1:
                        fold_lo(f - 1, (tl, th), 4 * g - 4)
                        between(g - 1)
                fold_lo(f0 + 3, (tl, th), 12)
                between(3)

            step(V.memset(ones[:], 1.0))
            stats(0)
            dve.wait_ge(sem("cols_in"), 16)
            folds(0, FOLD_MEM, C_GMEM, None)
            stats(1)
            dve.wait_ge(sem("const_in"), 16 * 10)
            dve.wait_ge(sem("bias_mm"), 1)
            V.tensor_tensor(bvec[:], ps[0:6, 7, :], dmask[:], ALU.add).then_inc(sem("bvec"), 1)
            rest_piece(1, 0)
            rest_piece(1, 1)
            folds(1, FOLD_X, C_GMIX, None, between=lambda g: rest_piece(1, 2 + g) if g < 2 else None)

            def head_norm(q):
                n = head_quads.index(q)
                dve.wait_ge(sem("chunk_out"), q + 1)
                h8 = stage[:].rearrange("p k (h d) -> p (k h) d", d=HD)
                s8 = stage2[:].rearrange("p k (h d) -> p (k h) d", d=HD)
                step(V.tensor_tensor(s8, h8, h8, ALU.mult))
                step(V.tensor_reduce(hss[:, 0, :], s8, AX.X, ALU.add))
                V.tensor_scalar(hss[:, 0, :], hss[:, 0, :], 1.0 / HD, EPS, ALU.mult, ALU.add)\
                    .then_inc(sem("head_ms"), 1)
                dve.wait_ge(sem("head_root"), n + 1)
                step(V.reciprocal(hss[:, 2, :], hss[:, 1, :]))
                rs = hss[:, 2, :].rearrange("p (h o) -> p h o", o=1).to_broadcast([P, 8, HD])
                if q < 6:
                    V.tensor_tensor(h8, h8, rs, ALU.mult).then_inc(sem("head_n"), 1)
                    return
                step(V.tensor_tensor(h8, h8, rs, ALU.mult))
                for k in range(TOK):
                    hk = stage[:, k, :].rearrange("p (h d) -> p h d", d=HD)
                    sk = stage2[:, k, :].rearrange("p (h d) -> p h d", d=HD)
                    runs = [(0, 4, 0)] if q == 6 else [(0, 2, 0), (2, 4, 1)]
                    for a, b, g in runs:
                        gain = gb[:, g, :].rearrange("p (o d) -> p o d", o=1).to_broadcast([P, b - a, HD])
                        step(V.tensor_tensor(hk[:, a:b], hk[:, a:b], gain, ALU.mult))
                    sin = rope[:, 1, k, :].rearrange("p (o d e) -> p o d e", o=1, e=2)
                    cos = rope[:, 0, k, :].rearrange("p (o d) -> p o d", o=1).to_broadcast([P, 4, HD])
                    h4 = stage[:, k, :].rearrange("p (h d e) -> p h d e", d=HD // 2, e=2)
                    s4 = stage2[:, k, :].rearrange("p (h d e) -> p h d e", d=HD // 2, e=2)
                    for e in range(2):
                        step(V.tensor_tensor(s4[:, :, :, e], h4[:, :, :, 1 - e],
                                             sin[:, :, :, e].to_broadcast([P, 4, HD // 2]), ALU.mult))
                    step(V.tensor_tensor(hk, hk, cos, ALU.mult))
                    ins = V.tensor_tensor(hk, hk, sk, ALU.add)
                ins.then_inc(sem("head_n"), 1)

            def head_out(q):
                n = head_quads.index(q)
                if q == 0:
                    dve.wait_ge(sem("bias_st"), 16)
                dve.wait_ge(sem("head_tr"), n + 1)
                for k in range(4):
                    src = quarters(4)[:, k]
                    if q == 0:
                        ins = V.tensor_scalar(kcT[:, k], src, cols[:, C_HEAD + 16 + k:C_HEAD + 17 + k], None, ALU.mult)
                        continue
                    h = 4 * (q - 2) + k
                    if h < 16:
                        scale = 1.0 if 6 <= h < 12 else SCALE
                        ins = V.tensor_scalar(qkT[:, h], src, cols[:, C_HEAD + h:C_HEAD + h + 1], scale,
                                              ALU.mult, ALU.mult)
                    else:
                        ins = V.tensor_scalar(qkT[:, h], src, SCALE if h < 22 else 1.0, None, ALU.mult)
                ins.then_inc(sem("head_T"), 1)

            for q in range(Q_GATES):
                if q >= 1:
                    rest_quad(q + 1)
                if q - 1 in head_quads:
                    head_out(q - 1)
                if q in head_quads:
                    head_norm(q)

            nA = negm[:, :, 0:6].rearrange("p k (g j) -> p k g j", j=2)
            lA = lsum[:, :, 0:6].rearrange("p k (g j) -> p k g j", j=2)
            d4 = cmb[:, 0].rearrange("p k (g j) -> p k g j", j=2)
            e4 = cmb[:, 1].rearrange("p k (g j) -> p k g j", j=2)

            def group_maxima():
                step(V.tensor_tensor(cmx[:, 0], nA[:, :, 0], nA[:, :, 1], ALU.min))
                step(V.tensor_tensor(cmx[:, 0], cmx[:, 0], nA[:, :, 2], ALU.min))
                for g in range(3):
                    ins = V.tensor_tensor(d4[:, :, g], cmx[:, 0], nA[:, :, g], ALU.subtract)
                ins.then_inc(sem("cmb_d"), 1)

            def join_groups():
                dve.wait_ge(sem("cmb_e"), 1)
                step(V.tensor_tensor(d4[:], e4, lA, ALU.mult))
                step(V.tensor_tensor(cmx[:, 0], d4[:, :, 0], d4[:, :, 1], ALU.add))
                step(V.tensor_tensor(cmx[:, 0], cmx[:, 0], d4[:, :, 2], ALU.add))
                step(V.reciprocal(cmx[:, 1], cmx[:, 0]))
                fA = fac[:, :, 0:6].rearrange("p k (g j) -> p k g j", j=2)
                for g in range(3):
                    ins = V.tensor_tensor(fA[:, :, g], e4[:, :, g], cmx[:, 1], ALU.mult)
                step(ins)
                for k in range(TOK):
                    f6 = fac[:, k, 0:6].rearrange("p (h o) -> p h o", o=1).to_broadcast([P, 6, HD])
                    ins = V.tensor_tensor(obuf[:, k, 0:6], obuf[:, k, 0:6], f6, ALU.mult)
                step(ins)
                step(V.tensor_tensor(obuf[:, :, 4:6, :], obuf[:, :, 4:6, :], obuf[:, :, 2:4, :], ALU.add))
                V.tensor_tensor(obuf[:, :, 4:6, :], obuf[:, :, 4:6, :], obuf[:, :, 0:2, :], ALU.add)\
                    .then_inc(sem("o_ready"), 1)

            for n in range(48):
                q, s = divmod(4 * Q_GATES + n, 4)
                rest_piece(q + 1, s)
                h, part = divmod(n, 3)
                if part == 0:
                    dve.wait_ge(sem("att_s"), h + 1)
                    V.tensor_reduce(negm[:, :, h:h + 1], ps[:, 4, :].rearrange("p (k n) -> p k n", n=SEQ), AX.X,
                                    ALU.max, negate=True).then_inc(sem("att_m"), 1)
                elif part == 1:
                    dve.wait_ge(sem("att_t"), h + 1)
                    V.tensor_copy(probsT[:].rearrange("p k n -> p (k n)"), ps[:, 5, :]).then_inc(sem("att_p"), 1)
                else:
                    dve.wait_ge(sem("att_v"), h + 1)
                    if h < A_HEADS:
                        V.tensor_copy(obuf[:, :, h, :], ps[:, 6, 0:SEQ].rearrange("p (k d) -> p k d", d=HD))\
                            .then_inc(sem("att_o"), 1)
                    else:
                        step(V.reciprocal(fac[:, :, h:h + 1], lsum[:, :, h:h + 1]))
                        for k in range(TOK):
                            ins = V.tensor_scalar(obuf[:, k, h, :], ps[:, 6, HD * k:HD * k + HD], fac[:, k, h:h + 1],
                                                  None, ALU.mult)
                        ins.then_inc(sem("att_o"), 1)
                if n == 18:
                    group_maxima()
                if n == 20:
                    join_groups()
            for f in range(FOLD_O, FOLD_M):
                fold_ready(f, f + 1)
                V.tensor_copy(fold[:, f % 2], quarters(fold_bank(f))).then_inc(sem("fold_t"), 1)
                fold_lo(f, (oTl, oTh), 4 * (f - FOLD_O))

            def merge(j, part):
                n = 3 * j + part
                dve.wait_ge(sem(f"gl_in{n % 4}"), 16 * (n // 4 + 1))
                dve.wait_ge(piece_used, 4 * Q_BRANCH + n + 1)
                to, banks = (mt0, mt1, mt1)[part], (0, 2, 6)[part]
                V.scalar_tensor_tensor(to[:], gl[:, n % 4], 1.0, pair(banks), ALU.add, ALU.mult)\
                    .then_inc(sem("gated"), 1)
                dve.wait_ge(sem("gated"), n + 1)
                if part == 1:
                    step(V.tensor_tensor(mt0[:], mt0[:], mt1[:], ALU.add))
                if part == 2:
                    V.tensor_tensor(merged[:, :, 512 * j:512 * j + 512], mt0[:], mt1[:], ALU.add)\
                        .then_inc(sem("merge"), 1)
                    dve.wait_ge(sem("merge"), j + 1)

            def fold_merged(j):
                f = FOLD_M + j
                fold_ready(f, f + 1)
                V.tensor_scalar(fold[:, f % 2], quarters(fold_bank(f)), 0.5, None, ALU.mult).then_inc(sem("fold_t"), 1)
                fold_lo(f, (hTl, hTh), 4 * j)

            for n in range(12):
                merge(n // 3, n % 3)
                if n % 3 == 1 and n >= 4:
                    fold_merged(n // 3 - 1)

            def ada_piece(a, j, first):
                dve.wait_ge(ADA_IN[j % 2], 64 * a + 16 * (j // 2 + 1))
                for k in range(2):
                    m = 2 * j + k
                    col = cs[:, m:m + 1]
                    src = adaraw[:, j % 2, k, :]
                    if not (first and m == 0):
                        dve.wait_ge(sem("ada_sum"), 16 * a + m)
                    if m == 0:
                        ins = V.tensor_scalar(adaacc[:], src, col, None, ALU.mult)
                    else:
                        ins = V.scalar_tensor_tensor(adaacc[:], src, col, adaacc[:], ALU.mult, ALU.add)
                    ins.then_inc(sem("ada_sum"), 1)
                dve.wait_ge(sem("ada_sum"), 16 * a + (2 * j + 2))
                dve.sem_inc(sem("ada_used"), 1)

            def ada_row(a, b):
                dve.wait_ge(sem("ada_mm"), a + 1)
                dve.wait_ge(sem("bada_in"), 16 * a + 16)
                for k in range(2):
                    V.tensor_tensor(modrow[0:1, 512 * k:512 * k + 512], ps[0:1, b + k, :],
                                    modrow[0:1, 512 * k:512 * k + 512], ALU.add).then_inc(sem("modrow"), 1)

            dve.wait_ge(sem("cs_done"), 1)
            dve.wait_ge(lo_done, 4 * (Q_WO + 1))
            for n in range(16):
                q, s = divmod(4 * Q_WO + n, 4)
                if s == 3:
                    dve.wait_ge(sem("x_back"), 16)
                    dve.wait_ge(piece_used, 4 * q + 4)
                    c = q - Q_WO
                    xc = x[:, :, 512 * c:512 * c + 512]
                    V.tensor_tensor(xc, xc, pair(2 * (c % 2)), ALU.add).then_inc(sem("wo_out"), 1)
                rest_piece(q + 1, s)
                if n == 0:
                    fold_merged(3)
                if n % 2 == 0:
                    ada_piece(0, n // 2, True)
            stats(2)
            ada_row(0, 6)
            folds(2, FOLD_FFN, C_GFFN, None)

            def ffn_mul(g):
                dve.wait_ge(sem("silu"), g + 1)
                dve.wait_ge(piece_used, 4 * Q_FFN + 8 if isinstance(g, int) and g == 0 else 12 * g + (4 * Q_FFN + 4))
                V.tensor_tensor(fact[:], gact[:], pair(2), ALU.mult).then_inc(sem("fmul"), 1)

            def ffn_lo(b):
                dve.wait_ge(sem("ffn_hi"), b + 1)
                V.tensor_tensor(factTl[:], quarters(4), factTh[:].bitcast(F32), ALU.subtract).then_inc(sem("ffn_lo"), 1)

            def ffn_down(b, s, used):
                dve.wait_ge(piece_used, used)
                if not isinstance(b, int):
                    dve.wait_ge(sem("x_sum"), 4 * b + (s + 1))
                xc = x[:, :, 512 * s:512 * s + 512]
                V.tensor_tensor(xc, xc, pair(6 if s % 2 == 0 else 0), ALU.add).then_inc(sem("x_sum"), 1)

            dve.sem_inc(sem("x_sum"), 1)
            for j in range(8):
                q, s = divmod(4 * Q_FFN + j, 4)
                rest_piece(q + 1, s)
                for a in ((0,), (1,), (2,), (3, 4), (5,), (6,), (7,), ())[j]:
                    ada_piece(1, a, False)
            ffn_mul(0)
            ada_row(1, 4)
            with dve.Fori(0, FF_GROUPS - 1) as b:
                for j in range(12):
                    if j >= 8:
                        ffn_down(b, j - 8, 12 * b + (4 * Q_FFN + 8 + j + 1))
                    rest_piece(3 * b + (Q_FFN + 3 + j // 4), j % 4)
                    if j == 1:
                        ffn_lo(b)
                    if j == 7:
                        ffn_mul(b + 1)
                    if j < 8:
                        ada_piece(b + 2, j, False)
                ada_row(b + 2, 4)
            ffn_lo(FF_GROUPS - 1)
            for j in range(4):
                dve.wait_ge(sem("x_sum"), 4 * (FF_GROUPS - 1) + j + 1)
                ffn_down(FF_GROUPS - 1, j, 4 * Q_IN2 - 3 + j)
                rest_piece(Q_IN2, j)
            stats(3)
            dve.wait_ge(sem("modT_in"), 64)
            step(V.scalar_tensor_tensor(gmod[:], modT[:, 1, :], 1.0, cols[:, C_GMIX2:C_GMIX2 + 16], ALU.add, ALU.mult))
            folds(3, FOLD_MIX2, 0, 0, gmod)
            dve.wait_ge(sem("wfh"), 1)
            V.tensor_tensor(wfl[:], wf[:], wfh[:].bitcast(F32), ALU.subtract).then_inc(sem("wfl"), 1)

            def log1p(out, e, z, z2):
                step(V.tensor_scalar(z2, e, 2.0, None, ALU.add))
                step(V.reciprocal(z2, z2))
                step(V.tensor_tensor(z, e, z2, ALU.mult))
                step(V.tensor_tensor(z2, z, z, ALU.mult))
                step(V.tensor_scalar(out, z2, 2.0 / 17, 2.0 / 15, ALU.mult, ALU.add))
                for k in (13, 11, 9, 7, 5, 3, 1):
                    step(V.tensor_tensor(out, out, z2, ALU.mult))
                    step(V.tensor_scalar(out, out, 2.0 / k, None, ALU.add))
                step(V.tensor_tensor(out, out, z, ALU.mult))

            step(V.tensor_scalar(lam[:, 0, :], cols[:, C_LAM:C_LAM + 8], -1.0, None, ALU.mult))
            V.tensor_tensor(lam[:, 0, :], lam[:, 0, :], cols[:, C_LAM:C_LAM + 8], ALU.min).then_inc(sem("lam_n"), 1)
            dve.wait_ge(sem("lam_e"), 1)
            log1p(lam[:, 2, :], lam[:, 1, :], lam[:, 0, :], lam[:, 3, :])
            step(V.tensor_scalar(lam[:, 0, :], cols[:, C_LAM:C_LAM + 8], -1.0, 0.0, ALU.mult, ALU.max))
            step(V.tensor_tensor(lam[:, 0, :], lam[:, 0, :], lam[:, 2, :], ALU.add))
            V.tensor_scalar(spn[:, 0, :], lam[:, 0, :], -8.0, None, ALU.mult)
            V.tensor_scalar(spn[:, 1, :], lam[:, 0, :], 4.0, None, ALU.mult).then_inc(sem("sp_done"), 1)

            for c in range(10):
                rest_quad(Q_IN2 + c + 1)
                if c == 0:
                    dve.wait_ge(sem("fold_tr"), FOLD_ATT)
                    step(V.memset(lxT[:, :, 0:3], 0.0))
                if c in (1, 2):
                    dve.wait_ge(sem("in_tr"), c)
                    V.tensor_copy(lxT[:, 4 * c - 4:4 * c, 3:3 + SEQ], quarters(4)).then_inc(sem("lx_T"), 1)
                if c == 2:
                    dve.wait_ge(sem("x_st"), 16)
                    dve.wait_ge(sem("lx_T"), 2)
                    for j in range(CONV):
                        for n in range(8):
                            win = lxT[:, n, j:j + SEQ]
                            w = cols[:, C_CONVW + 8 * j + n:C_CONVW + 8 * j + n + 1]
                            if j == 0:
                                ins = V.tensor_scalar(bx[:, n], win, w, cols[:, C_CONVB + n:C_CONVB + n + 1],
                                                      ALU.mult, ALU.add)
                            else:
                                dve.wait_ge(sem("tap"), 8 * (j - 1) + n + 1)
                                ins = V.scalar_tensor_tensor(bx[:, n], win, w, bx[:, n], ALU.mult, ALU.add)
                            ins.then_inc(sem("tap") if j < CONV - 1 else sem("conv"), 1)
                if c == 4:
                    for n in range(8):
                        dve.wait_ge(sem("i_out"), n + 1)
                        V.tensor_tensor(bx[:, n], bx[:, n], istage[:, n % 2], ALU.mult).then_inc(sem("i_used"), 1)
                if c == 6:
                    dve.wait_ge(sem("dec"), 8)
                    dve.wait_ge(sem("i_used"), 8)
                    step(V.scalar_tensor_tensor(bx[:], dec[:], 1.0, bx[:], ALU.add, ALU.mult))
                if 5 <= c <= 8:
                    dve.wait_ge(sem("in_tr"), c)
                    V.tensor_scalar(qkT2[:, 4 * c - 20:4 * c - 16, :], quarters(4), SCALE if c < 7 else 1.0, None,
                                    ALU.mult).then_inc(sem("qk_T"), 1)
                if c == 7:
                    dve.wait_ge(sem("root2"), 1)
                    step(V.tensor_tensor(bx[:], bx[:], uT[:], ALU.mult))
                    for n in range(8):
                        ins = V.tensor_tensor_scan(uT[:, n], dec[:, n], bx[:, n], 0.0, ALU.mult, ALU.add)
                        ins.then_inc(sem("scan"), 1)
                    dve.wait_ge(sem("scan"), 8)
                    dve.wait_ge(sem("gy_T"), 2)
                    V.tensor_tensor(gyT[:], gyT[:], uT[:], ALU.mult).then_inc(sem("lru"), 1)
                if c == 8:
                    dve.wait_ge(sem("f_mm"), 1)
                    V.tensor_copy(fs[:].rearrange("p k h -> p (k h)"), ps[:, 7, 0:16]).then_inc(sem("fs"), 1)
            L = [lgate[:, r, :] for r in range(4)]
            dve.wait_ge(sem("f_tr"), 1)
            step(V.tensor_scalar(L[0], ps[0:8, 7, 128:128 + SEQ], cols[0:8, C_BF:C_BF + 1], None, ALU.add))
            step(V.tensor_scalar(L[1], L[0], -1.0, None, ALU.mult))
            V.tensor_tensor(L[1], L[1], L[0], ALU.max).then_inc(sem("lg_abs"), 1)
            dve.wait_ge(sem("lg_exp"), 1)
            log1p(L[1], L[1], L[2], L[3])
            step(V.tensor_scalar(L[0], L[0], 0.0, None, ALU.min))
            step(V.tensor_tensor(L[0], L[0], L[1], ALU.subtract))
            step(V.memset(L[3], 0.0))
            step(V.tensor_tensor_scan(L[1], L[0], L[3], 0.0, ALU.add, ALU.add))
            V.tensor_scalar(L[2], L[1], -1.0, None, ALU.mult).then_inc(sem("cum"), 1)

            def max2(h):
                dve.wait_ge(sem("s2"), h + 1)
                V.tensor_reduce(negm[:, :, h:h + 1], ps[:, h % 2, :].rearrange("p (k n) -> p k n", n=SEQ), AX.X,
                                ALU.max, negate=True).then_inc(sem("m2"), 1)

            max2(0)
            for h in range(H2):
                if h + 1 < H2:
                    max2(h + 1)
                dve.wait_ge(sem("t2"), h + 1)
                V.tensor_copy(probsT2[:, h % 2].rearrange("p k n -> p (k n)"), ps[:, 2 + h % 2, :])\
                    .then_inc(sem("p2"), 1)
                dve.wait_ge(sem("v2"), h + 1)
                V.tensor_copy(att2[:, :, h, :], ps[:, 4 + h % 2, 0:SEQ].rearrange("p (k d) -> p k d", d=HD))\
                    .then_inc(sem("o2"), 1)
            dve.wait_ge(sem("e2"), 2 * H2)
            dve.wait_ge(sem("o2"), H2)
            step(V.reciprocal(fac[:, :, 0:8], lsum[:, :, 0:8]))
            for k in range(TOK):
                f8 = fac[:, k, 0:8].rearrange("p (h o) -> p h o", o=1).to_broadcast([P, H2, HD])
                ins = V.tensor_tensor(att2[:, k], att2[:, k], f8, ALU.mult)
            ins.then_inc(sem("att2_n"), 1)
            dve.wait_ge(sem("lru"), 1)
            V.tensor_tensor(lsq[:], gyT[:], gyT[:], ALU.mult).then_inc(sem("lsq"), 1)
            dve.wait_ge(sem("ssq2"), 2)
            V.tensor_scalar(ssum[:], ssum[:], 1.0 / LRU, EPS, ALU.mult, ALU.add).then_inc(sem("ms2"), 1)
            dve.wait_ge(sem("ms2_root"), 1)
            V.reciprocal(rstd[:, 1, :], rstd[:, 0, :]).then_inc(sem("rstd2"), 1)
            for g in range(2):
                f = FOLD_ATT + g
                fold_ready(f, f + 1)
                for k in range(4):
                    col = cols[:, C_GATT + 4 * g + k:C_GATT + 4 * g + k + 1]
                    ins = V.tensor_scalar(fold[:, f % 2, k], quarters(fold_bank(f))[:, k], col, None, ALU.mult)
                ins.then_inc(sem("fold_t"), 1)
                fold_lo(f, (hTl, hTh), 4 * g)
            dve.wait_ge(sem("lsum_mm"), 1)
            V.tensor_scalar(lrs[:, 0, :], ps[:, 2, 0:SEQ], 1.0 / LRU, EPS, ALU.mult, ALU.add).then_inc(sem("lru_ms"), 1)
            dve.wait_ge(sem("lru_root"), 1)
            step(V.reciprocal(lrs[:, 1, :], lrs[:, 0, :]))
            for g in range(2):
                f = FOLD_LRU + g
                fold_ready(f, None)
                for k in range(4):
                    n = 4 * g + k
                    ins = V.scalar_tensor_tensor(fold[:, f % 2, k], gyT[:, n], cols[:, C_GLRU + n:C_GLRU + n + 1],
                                                 lrs[:, 1, :], ALU.mult, ALU.mult)
                ins.then_inc(sem("fold_t"), 1)
                fold_lo(f, (hTl, hTh), 8 + 4 * g)
            dve.wait_ge(sem("ga1_in"), 16)
            dve.wait_ge(sem("x_back"), 32)
            for c in range(4):
                q = Q_OUT2 + c
                rest_quad(q + 1)
                dve.wait_ge(piece_used, 4 * q + 4)
                cut = slice(512 * c, 512 * c + 512)
                gain = ga1[:, cut].rearrange("p (o n) -> p o n", o=1).to_broadcast([P, TOK, 512])
                V.tensor_tensor(mt2[:], pair(2 * (c % 2)), gain, ALU.mult).then_inc(sem("out2"), 1)
                dve.wait_ge(sem("out2"), c + 1)
                V.tensor_tensor(x[:, :, cut], x[:, :, cut], mt2[:], ALU.add).then_inc(sem("out2_sum"), 1)
                dve.wait_ge(sem("out2_sum"), c + 1)
            step(V.scalar_tensor_tensor(gmod[:], modT[:, 3, :], 1.0, cols[:, C_GFFN2:C_GFFN2 + 16], ALU.add, ALU.mult))
            stats(4)
            folds(4, FOLD_PEER, 0, 2, gmod)

            def pq_turned(c):
                dve.wait_ge(sem("pq_tr"), c + 1)
                V.tensor_copy(pqT[:, 4 * c:4 * c + 4, :], quarters(4)).then_inc(sem("pq_T"), 1)

            def scores_out(c):
                dve.wait_ge(sem("psc"), c + 1)
                if c == 0:
                    dve.wait_ge(sem("fold_tr"), FOLD_PEER + 4 - 2)
                V.tensor_copy(sc[:, :, 4 * c:4 * c + 4, :].rearrange("p k h n -> p k (h n)"), pair(6))\
                    .then_inc(sem("sc_out"), 1)

            for c in range(4):
                rest_quad(Q_PQ + c + 1)
                if c >= 1:
                    pq_turned(c - 1)
                if c >= 2:
                    scores_out(c - 2)
            pq_turned(3)
            scores_out(2)
            scores_out(3)
            dve.wait_ge(sem("sc_out"), 4)

            def top16(vals, idx, src, tmp, rows):
                for r in range(rows):
                    ins = V.max(vals[:, r, 0:8], src[:, r])
                step(ins)
                for r in range(rows):
                    V.max_index(idx[:, r, 0:8], vals[:, r, 0:8], src[:, r])
                for r in range(rows):
                    ins = V.match_replace(tmp[:, r], vals[:, r, 0:8], src[:, r], -3e38)
                step(ins)
                for r in range(rows):
                    ins = V.max(vals[:, r, 8:16], tmp[:, r])
                step(ins)
                for r in range(rows):
                    ins = V.max_index(idx[:, r, 8:16], vals[:, r, 8:16], tmp[:, r])
                step(ins)

            for k in range(TOK):
                top16(top[:, k], topi[:, k], sc[:, k], work[:].rearrange("p a (b n) -> p (a b) n", n=N_KEYS), 16)
            step(V.tensor_copy(topf[:].rearrange("p k h n -> p (k h n)"), topi[:].rearrange("p k h n -> p (k h n)")))
            for k in range(TOK):
                pairs = top[:, k].rearrange("p (h e) n -> p h e n", e=2)
                first = pairs[:, :, 0].rearrange("p h (n o) -> p h n o", o=1).to_broadcast([P, 8, TOPK, TOPK])
                second = pairs[:, :, 1].rearrange("p h (o n) -> p h o n", o=1).to_broadcast([P, 8, TOPK, TOPK])
                step(V.tensor_tensor(cand[:].rearrange("p h (a b) -> p h a b", b=TOPK), first, second, ALU.add))
                top16(best[:, k], besti[:, k], cand, work, 8)
                bi = besti[:, k]
                V.tensor_scalar(divi[:, 0], bi, 4, None, ALU.logical_shift_right)
                step(V.tensor_scalar(divi[:, 1], bi, 15, None, ALU.bitwise_and))
                step(V.tensor_copy(divf[:].rearrange("p e h n -> p (e h n)"), divi[:].rearrange("p e h n -> p (e h n)")))
                for e in range(2):
                    w4 = work[:].rearrange("p h (a b) -> p h a b", b=TOPK)
                    v4 = work2[:].rearrange("p h (a b) -> p h a b", b=TOPK)
                    place = iota[:, 0:16].rearrange("p (o q n) -> p o q n", o=1, q=1).to_broadcast([P, 8, TOPK, TOPK])
                    want = divf[:, e].rearrange("p h (n o) -> p h n o", o=1).to_broadcast([P, 8, TOPK, TOPK])
                    have = topf[:, k].rearrange("p (h e) n -> p h e n", e=2)[:, :, e]\
                        .rearrange("p h (o n) -> p h o n", o=1).to_broadcast([P, 8, TOPK, TOPK])
                    step(V.tensor_tensor(w4, place, want, ALU.is_equal))
                    step(V.tensor_tensor(v4, w4, have, ALU.mult))
                    step(V.tensor_reduce(picks[:, k, e], v4, AX.X, ALU.add))
                lead = best[:, k, :, 0:1].to_broadcast([P, 8, TOPK])
                ins = V.tensor_tensor(picks[:, k, 2], best[:, k], lead, ALU.subtract)
            ins.then_inc(sem("wexp_in"), 1)
            dve.wait_ge(sem("wexp"), 1)
            for k in range(TOK):
                ins = V.tensor_reduce(wsm[:, k, :, 0:1], picks[:, k, 2], AX.X, ALU.add)
            step(ins)
            step(V.reciprocal(wsm[:, :, :, 1:2], wsm[:, :, :, 0:1]))
            for k in range(TOK):
                ins = V.tensor_tensor(picks[:, k, 2], picks[:, k, 2], wsm[:, k, :, 1:2].to_broadcast([P, 8, TOPK]),
                                      ALU.mult)
            ins.then_inc(sem("picks"), 1)
            dve.wait_ge(sem("picks_tr"), 1)
            V.tensor_copy(picksT[:].rearrange("p a t -> p (a t)"),
                          ps[:, 6:8, :].rearrange("p b n -> p (b n)")[:, 0:3 * SEQ]).then_inc(sem("picksT"), 1)
            dve.wait_ge(sem("picksT"), 1)

            def one_hots(i, v, first):
                if not first:
                    dve.wait_ge(sem("wmm"), 2 * i + (v - 1))
                tok = slice(16 * i + 8 * v, 16 * i + 8 * v + 8) if isinstance(i, int) else bass.ds(16 * i + 8 * v, 8)
                row = iota[:].rearrange("p (o b) -> p o b", o=1).to_broadcast([P, 8, P])
                for e in range(2):
                    key = picksT[:, e, tok].rearrange("p (t o) -> p t o", o=1).to_broadcast([P, 8, P])
                    ins = V.tensor_tensor(oh[:, v, e], row, key, ALU.is_equal)
                ins.then_inc(sem("oh_raw"), 1)
                dve.wait_ge(sem("oh_raw"), 2 * i + (v + 1))
                weight = picksT[:, 2, tok].rearrange("p (t o) -> p t o", o=1).to_broadcast([P, 8, P])
                V.tensor_tensor(oh[:, v, 1], oh[:, v, 1], weight, ALU.mult).then_inc(sem("oh"), 1)

            one_hots(0, 0, True)
            one_hots(0, 1, True)
            with dve.Fori(1, SEQ // 16) as i:
                for v in range(2):
                    one_hots(i, v, False)

            def peer_mul(g, u, hidden, used):
                dve.wait_ge(sem(f"wc_in{u}"), used)
                if not isinstance(g, int) or g > 0:
                    dve.wait_ge(sem("peer_tr"), g)
                V.tensor_tensor(pact[:], hidden, wc[:, u], ALU.mult).then_inc(sem("pmul"), 1)

            def early_mul(g, u, m):
                dve.wait_ge(sem(f"hid_in{u}"), 16 * m + 16)
                peer_mul(g, u, hid[:, u], 16 * m + 16)

            def peer_lo(b, u):
                dve.wait_ge(sem("peer_hi"), b + 1)
                V.tensor_tensor(pactTl[:, u], quarters(4), pactTh[:, u].bitcast(F32), ALU.subtract)\
                    .then_inc(sem("peer_lo"), 1)

            def peer_down(b, s, used):
                dve.wait_ge(piece_used, used)
                dve.wait_ge(sem("y_sum"), 4 * b + (s + 2))
                yc = y[:, :, 512 * s:512 * s + 512]
                V.tensor_tensor(yc, yc, pair(6 if s % 2 == 0 else 2), ALU.add).then_inc(sem("y_sum"), 1)

            dve.wait_ge(sem("sc_out"), 4)
            V.memset(y[:], 0.0).then_inc(sem("y_sum"), 2)
            dve.wait_ge(sem("wmm"), SEQ // 8)
            dve.wait_ge(lo_done, 4 * (Q_PEER + EARLY))
            for j in range(4):
                rest_piece(Q_PEER + EARLY, j)
                if j == 1:
                    early_mul(0, 0, 0)
                if j == 2:
                    peer_lo(0, 0)
                    early_mul(1, 1, 0)

            def down_group(b, u, m):
                for j in range(4):
                    rest_piece(b + (Q_PEER + EARLY + 1), j)
                    peer_down(b, j, 4 * b + (4 * (Q_PEER + EARLY) + j + 1))
                    if j == 2 and m is not None:
                        peer_lo(b + 1, 1 - u)
                        early_mul(b + 2, u, m + 1)

            with dve.Fori(0, (EARLY - 1) // 2 - 1) as m:
                for u in range(2):
                    down_group(2 * m + u, u, m)
            for b in (EARLY - 3, EARLY - 2):
                for j in range(4):
                    rest_piece(b + (Q_PEER + EARLY + 1), j)
                    peer_down(b, j, 4 * b + (4 * (Q_PEER + EARLY) + j + 1))
                    if j == 2 and b == EARLY - 3:
                        peer_lo(b + 1, 1)
                        dve.wait_ge(sem("gelu"), EARLY)
                        peer_mul(EARLY - 1, 0, gacc[:], 16 * ((EARLY + 1) // 2))
            with dve.Fori(EARLY - 1, PEER_GROUPS - 1) as b:
                for j in range(8):
                    if j >= 4:
                        peer_down(b, j - 4, 8 * b + (4 * Q_PEER + 4 + j + 1))
                    rest_piece(2 * b + (Q_PEER + 2 + j // 4), j % 4)
                    if j == 1:
                        peer_lo(b, 0)
                    if j == 4:
                        dve.wait_ge(sem("gelu"), b + 2)
                        peer_mul(b + 1, 0, gacc[:], 16 * b + 16 * (2 - EARLY + (EARLY + 1) // 2))
            peer_lo(PEER_GROUPS - 1, 0)
            for j in range(4):
                peer_down(PEER_GROUPS - 1, j, 4 * QUADS - 3 + j)
            dve.wait_ge(sem("y_sum"), 4 * PEER_GROUPS + 2)
            dve.wait_ge(sem("tail_in"), 32)
            step(V.tensor_tensor(y[:], y[:], ga2[:].rearrange("p (o n) -> p o n", o=1).to_broadcast([P, TOK, D]),
                                 ALU.mult))
            V.tensor_tensor(x[:], x[:], y[:], ALU.add).then_inc(sem("x_ready"), 1)
            dve.wait_ge(sem("sq_done"), 8 * 5 + 2)
            V.tensor_scalar(ssum[:], ssum[:], 1.0 / D, EPS, ALU.mult, ALU.add).then_inc(sem("ms_done"), 1)
            dve.wait_ge(sem("root_done"), 6)
            step(V.reciprocal(rstd[:, 1, :], rstd[:, 0, :]))
            dve.wait_ge(sem("tail_in"), 32)
            for k in range(TOK):
                V.scalar_tensor_tensor(x[:, k, :], x[:, k, :], rstd[:, 1, k:k + 1], gfin[:], ALU.mult, ALU.mult)\
                    .then_inc(sem("final"), 1)

        @block.tensor
        def _(pe):
            T = nc.tensor

            def split_products(out, th, tl, stat, s, cut, start, stop):
                T.matmul(out, th[stat], hi[:, s, cut], start=start, stop=False)
                T.matmul(out, th[stat], lo[:, s, cut], start=False, stop=False)
                return T.matmul(out, tl[stat], hi[:, s, cut], start=False, stop=stop)

            def wide_piece(q, s, b, th=None, tl=None):
                th, tl = (hTh, hTl) if th is None else (th, tl)
                pe.wait_ge(lo_done, 4 * q + (s + 1))
                for k in range(4):
                    for m in range(TOK):
                        ins = split_products(ps[:, b + m, :], th, tl,
                                             (slice(None), 4 * s + k, slice(P * m, P * m + P)), s,
                                             slice(512 * k, 512 * k + 512), s == 0 and k == 0, s == 3 and k == 3)
                ins.then_inc(piece_used, 1)

            def down_piece(q, s, b, th, tl):
                pe.wait_ge(lo_done, 4 * q + (s + 1))
                for m in range(TOK):
                    for k in range(4):
                        ins = split_products(ps[:, b + m, :], th, tl, (slice(None), k, slice(P * m, P * m + P)), s,
                                             slice(512 * k, 512 * k + 512), k == 0, k == 3)
                ins.then_inc(piece_used, 1)

            def turn(b, tiles):
                for k in range(4):
                    for m in range(TOK):
                        ins = T.transpose(quarters(b)[:, k, P * m:P * m + P], tiles(k, m), ident[:])
                return ins

            def fold_turn(f, tiles):
                free = f if FOLD_M <= f < FOLD_FFN else f - 1
                if free >= 1:
                    pe.wait_ge(sem("fold_t"), free)
                turn(fold_bank(f), tiles).then_inc(sem("fold_tr"), 1)

            def norm_turn(f0, g, src, u):
                pe.wait_ge(sem("xn_done"), 8 * u + 2 * g + 2)
                fold_turn(f0 + g, lambda k, m: src[:, m, P * (4 * g + k):P * (4 * g + k) + P])

            def normed_quad(f0, src, u, q, b, th=None, tl=None):
                for g in range(3):
                    norm_turn(f0, g, src, u)
                for s in range(4):
                    pe.wait_ge(sem("fold_lo"), f0 + s + 1)
                    wide_piece(q, s, b, th, tl)
                    if s == 0:
                        norm_turn(f0, 3, src, u)

            pe.wait_ge(sem("ident_in"), 16)
            normed_quad(FOLD_MEM, memraw, 0, 0, 0, memTh, memTl)
            pe.wait_ge(sem("const_in"), 16 * 10)
            pe.wait_ge(sem("fold_t"), FOLD_X)
            T.matmul(ps[0:6, 7, :], tabs[:], oneh[:], start=True, stop=True).then_inc(sem("bias_mm"), 1)
            wide_piece(1, 0, 2, memTh, memTl)
            pe.wait_ge(sem("bvec"), 1)
            for g in range(3):
                norm_turn(FOLD_X, g, x, 1)
            wide_piece(1, 1, 2, memTh, memTl)
            norm_turn(FOLD_X, 3, x, 1)
            for s in (2, 3):
                wide_piece(1, s, 2, memTh, memTl)

            def head_turn(q):
                n = head_quads.index(q)
                pe.wait_ge(sem("head_n"), n + 1)
                if n >= 1:
                    pe.wait_ge(sem("head_T"), n)
                else:
                    pe.wait_ge(sem("fold_t"), FOLD_O)
                turn(4, lambda k, m: stage[:, m, HD * k:HD * k + HD]).then_inc(sem("head_tr"), 1)

            for q in range(1, Q_GATES):
                if q >= 2:
                    if q == 2:
                        pe.wait_ge(sem("fold_lo"), FOLD_O)
                    pe.wait_ge(sem("chunk_out"), q - 1)
                    for s in range(4):
                        wide_piece(q, s, 2 * (q % 2))
                if q - 1 in head_quads:
                    head_turn(q - 1)

            heads = [(h, 6 + h, h) for h in range(6)]
            heads += [(16 + j, 22 + j // 3, 6 + j // 3) for j in range(B_HEADS)]
            heads += [(12 + j, None, j) for j in range(C_HEADS)]
            for n in range(48):
                q, s = divmod(4 * Q_GATES + n, 4)
                if s == 0:
                    pe.wait_ge(sem("chunk_out"), q - 1)
                wide_piece(q, s, 2 * (q % 2))
                h, part = divmod(n, 3)
                qi, ki, vi = heads[h]
                if part == 0:
                    if h == 0:
                        pe.wait_ge(sem("head_T"), 7)
                    if h >= 1:
                        pe.wait_ge(sem("att_e"), 2 * h)
                    if h < A_HEADS:
                        pe.wait_ge(sem(f"hank_in{h % 2}"), 16 * (h // 2 + 1))
                    for m in range(TOK):
                        keys = kcT[:, h - 12] if ki is None else qkT[:, ki]
                        out = ps[:, 4, SEQ * m:SEQ * m + SEQ]
                        ins = T.matmul(out, qkT[:, qi, P * m:P * m + P], keys, start=True, stop=h >= A_HEADS)
                        if h < A_HEADS:
                            at0 = P * (1 - m)
                            ins = T.matmul(out, anti[:], hank[:, h % 2, at0:at0 + SEQ], start=False, stop=True)
                    ins.then_inc(sem("att_s"), 1)
                elif part == 1:
                    pe.wait_ge(sem("att_e"), 2 * h + 2)
                    if h >= 1:
                        pe.wait_ge(sem("att_p"), h)
                    for m in range(TOK):
                        for k in range(TOK):
                            ins = T.transpose(ps[:, 5, SEQ * k + P * m:SEQ * k + P * m + P],
                                              probs[:, m, P * k:P * k + P], ident[:])
                    ins.then_inc(sem("att_t"), 1)
                else:
                    pe.wait_ge(sem("att_p"), h + 1)
                    if h == 0:
                        pe.wait_ge(sem("chunk_out"), Q_GATES)
                    if h >= 1:
                        pe.wait_ge(sem("att_o"), h)
                    for m in range(TOK):
                        for k in range(TOK):
                            val = vC[:, k, vi] if ki is None else vAB[:, k, vi]
                            ins = T.matmul(ps[:, 6, HD * m:HD * m + HD], probsT[:, k, P * m:P * m + P], val,
                                           start=k == 0, stop=k == 1)
                    ins.then_inc(sem("att_v"), 1)

            pe.wait_ge(sem("o_ready"), 1)
            pe.wait_ge(sem("att_o"), HEADS)
            for f in range(FOLD_O, FOLD_M):
                fold_turn(f, lambda k, m: obuf[:, m, 4 + 4 * (f - FOLD_O) + k])
            pe.wait_ge(sem("chunk_out"), Q_BRANCH)

            def merged_turn(j):
                pe.wait_ge(sem("merge"), j + 1)
                fold_turn(FOLD_M + j, lambda k, m: merged[:, m, P * (4 * j + k):P * (4 * j + k) + P])

            for n in range(12):
                q, s = divmod(4 * Q_BRANCH + n, 4)
                j, part = divmod(n, 3)
                if j == 0:
                    pe.wait_ge(sem("fold_lo"), FOLD_O + part + 1)
                if n == 2:
                    pe.wait_ge(sem("fold_t"), FOLD_M)
                pe.wait_ge(lo_done, 4 * q + s + 1)
                if part == 0 and j >= 1:
                    pe.wait_ge(sem("gated"), 3 * j - 1)
                if part == 2 and j >= 1:
                    pe.wait_ge(sem("gated"), 3 * j)
                for k in range(4):
                    kt = 4 * part + k
                    b = 0 if kt < 2 else 2 if kt < 8 else 6
                    for m in range(TOK):
                        ins = split_products(ps[:, b + m, :], oTh, oTl, (slice(None), kt, slice(P * m, P * m + P)), s,
                                             slice(512 * k, 512 * k + 512), kt in (0, 2, 8), kt in (1, 7, 11))
                ins.then_inc(piece_used, 1)
                if part == 1 and j >= 1:
                    merged_turn(j - 1)

            def ada_sum(a, b):
                pe.wait_ge(sem("ada_sum"), 16 * a + 16)
                for k in range(2):
                    ins = T.matmul(ps[0:1, b + k, :], ones[:, 0:1], adaacc[:, 512 * k:512 * k + 512],
                                   start=True, stop=True)
                ins.then_inc(sem("ada_mm"), 1)

            for n in range(16):
                q, s = divmod(4 * Q_WO + n, 4)
                c = q - Q_WO
                if s == 0 and c < 2:
                    pe.wait_ge(sem("gated"), 10 + c)
                elif s == 0:
                    pe.wait_ge(sem("wo_out"), c - 1)
                if c == 0:
                    pe.wait_ge(sem("fold_lo"), FOLD_M + s + 1)
                wide_piece(q, s, 2 * (c % 2))
                if n == 0:
                    merged_turn(3)
            pe.wait_ge(sem("gated"), 12)
            ada_sum(0, 6)
            pe.wait_ge(sem("modrow"), 2)

            def ffn_turn(b):
                pe.wait_ge(sem("fmul"), b + 1)
                turn(4, lambda k, m: fact[:, m, P * k:P * k + P]).then_inc(sem("ffn_tr"), 1)

            def ffn_down(b, q, s):
                if s == 0:
                    pe.wait_ge(sem("ffn_lo"), b + 1)
                if s >= 2:
                    pe.wait_ge(sem("x_sum"), 4 * b + s)
                elif s == 0 and not isinstance(b, int):
                    pe.wait_ge(sem("x_sum"), 4 * b + 1)
                down_piece(q, s, 6 if s % 2 == 0 else 0, factTh, factTl)

            normed_quad(FOLD_FFN, xn, 2, Q_FFN, 0)
            for s in range(4):
                wide_piece(Q_FFN + 1, s, 2)
            pe.wait_ge(sem("fold_t"), FOLD_MIX2)
            ada_sum(1, 4)
            with pe.Fori(0, FF_GROUPS - 1) as b:
                for j in range(12):
                    q, s = 3 * b + (Q_FFN + 2 + j // 4), j % 4
                    if j == 0:
                        pe.wait_ge(sem("silu"), b + 1)
                        pe.wait_ge(sem("x_sum"), 4 * b + 1)
                    if j == 4:
                        pe.wait_ge(sem("fmul"), b + 1)
                    if j == 9:
                        pe.wait_ge(sem("silu"), b + 2)
                    if j < 8:
                        wide_piece(q, s, 0 if j < 4 else 2)
                    else:
                        ffn_down(b, q, s)
                    if j == 1:
                        pe.wait_ge(sem("modrow"), 2 * b + 4)
                        ffn_turn(b)
                ada_sum(b + 2, 4)
            pe.wait_ge(sem("modrow"), 2 * ADA_SPLITS)
            ffn_turn(FF_GROUPS - 1)
            pe.wait_ge(sem("x_sum"), 4 * (FF_GROUPS - 1) + 1)
            for s in range(4):
                ffn_down(FF_GROUPS - 1, Q_IN2 - 1, s)

            def in_turn(c):
                pe.wait_ge(sem("in_out"), c + 1)
                if c == 0:
                    pe.wait_ge(sem("fold_t"), FOLD_ATT)
                elif c <= 2:
                    pe.wait_ge(sem("lx_T"), c)
                elif c <= 4:
                    pe.wait_ge(sem("gy_T"), c - 2)
                else:
                    pe.wait_ge(sem("qk_T"), c - 4)
                turn(4, lambda k, m: stage[:, m, P * k:P * k + P]).then_inc(sem("in_tr"), 1)

            for c in range(10):
                if c >= 2:
                    pe.wait_ge(sem("in_out"), c - 1)
                if c == 0:
                    normed_quad(FOLD_MIX2, xn, 3, Q_IN2, 0)
                else:
                    for s in range(4):
                        wide_piece(Q_IN2 + c, s, 2 * (c % 2))
                if 1 <= c <= 8:
                    in_turn(c - 1)
                if c == 4:
                    pe.wait_ge(sem("lw_in"), 32)
                    for n in range(8):
                        pe.wait_ge(sem("conv"), n + 1)
                        if n >= 2:
                            pe.wait_ge(sem("i_out"), n - 1)
                        T.matmul(ps[:, 6 + n % 2, 0:SEQ], lwa[:, n], bx[:, n], start=True, stop=True)
                        T.matmul(ps[:, 6 + n % 2, SEQ:2 * SEQ], lwx[:, n], bx[:, n], start=True, stop=True)\
                            .then_inc(sem("ri"), 1)
                if c == 7:
                    pe.wait_ge(sem("wfl"), 1)
                    pe.wait_ge(sem("i_out"), 8)
                    for m in range(TOK):
                        for k in range(KT):
                            for j, (a, b) in enumerate(((hTh, wfh), (hTh, wfl), (hTl, wfh))):
                                ins = T.matmul(ps[:, 7, 8 * m:8 * m + 8], a[:, k, P * m:P * m + P], b[:, k, :],
                                               start=k == 0 and j == 0, stop=k == KT - 1 and j == 2)
                    ins.then_inc(sem("f_mm"), 1)
                if c == 9:
                    pe.wait_ge(sem("fs"), 1)
                    for m in range(TOK):
                        ins = T.transpose(ps[0:8, 7, 128 + P * m:128 + P * m + P], fs[:, m, :], ident[:])
                    ins.then_inc(sem("f_tr"), 1)

            def scores2(h):
                if h >= 2:
                    pe.wait_ge(sem("e2"), 2 * h - 2)
                for m in range(TOK):
                    out = ps[:, h % 2, SEQ * m:SEQ * m + SEQ]
                    at0 = P * (1 - m)
                    T.matmul(out, qkT2[:, h, P * m:P * m + P], qkT2[:, 8 + h, :], start=True, stop=False)
                    T.matmul(out, lgate[:, 1, P * m:P * m + P], sel[:, h, :], start=False, stop=False)
                    T.matmul(out, sel[:, h, 0:P], lgate[:, 2, :], start=False, stop=False)
                    ins = T.matmul(out, ident[:], causal[:, at0:at0 + SEQ], start=False, stop=True)
                ins.then_inc(sem("s2"), 1)

            pe.wait_ge(sem("sel_in"), 16)
            pe.wait_ge(sem("cum"), 1)
            pe.wait_ge(sem("qk_T"), 4)
            pe.wait_ge(sem("in_out"), 10)
            scores2(0)
            for h in range(H2):
                if h + 1 < H2:
                    scores2(h + 1)
                pe.wait_ge(sem("e2"), 2 * h + 2)
                if h >= 2:
                    pe.wait_ge(sem("p2"), h - 1)
                for m in range(TOK):
                    for k in range(TOK):
                        ins = T.transpose(ps[:, 2 + h % 2, SEQ * k + P * m:SEQ * k + P * m + P],
                                          probs2[:, h % 2, m, P * k:P * k + P], ident[:])
                ins.then_inc(sem("t2"), 1)
                pe.wait_ge(sem("p2"), h + 1)
                if h >= 2:
                    pe.wait_ge(sem("o2"), h - 1)
                for m in range(TOK):
                    for k in range(TOK):
                        ins = T.matmul(ps[:, 4 + h % 2, HD * m:HD * m + HD], probsT2[:, h % 2, k, P * m:P * m + P],
                                       v2[:, k, HD * h:HD * h + HD], start=k == 0, stop=k == 1)
                ins.then_inc(sem("v2"), 1)
            pe.wait_ge(sem("lsq"), 1)
            pe.wait_ge(sem("p2"), H2)
            for n in range(8):
                ins = T.matmul(ps[:, 2, 0:SEQ], ones[:], lsq[:, n], start=n == 0, stop=n == 7)
            ins.then_inc(sem("lsum_mm"), 1)
            pe.wait_ge(sem("att2_s"), 2)
            pe.wait_ge(sem("o2"), H2)
            for g in range(2):
                fold_turn(FOLD_ATT + g, lambda k, m: att2[:, m, 4 * g + k])
            pe.wait_ge(sem("lru_ms"), 1)
            pe.wait_ge(sem("fold_lo"), FOLD_PEER)
            for c in range(4):
                if c >= 2:
                    pe.wait_ge(sem("out2"), c - 1)
                for s in range(4):
                    wide_piece(Q_OUT2 + c, s, 2 * (c % 2))

            def pq_turn(c):
                pe.wait_ge(sem("pq_out"), c + 1)
                if c == 0:
                    pe.wait_ge(sem("out2"), 4)
                    pe.wait_ge(sem("fold_t"), FOLD_PEER + 4)
                else:
                    pe.wait_ge(sem("pq_T"), c)
                turn(4, lambda k, m: stage[:, m, P * k:P * k + P]).then_inc(sem("pq_tr"), 1)

            def key_scores(c):
                pe.wait_ge(sem("keys_in"), 16)
                pe.wait_ge(sem("pq_T"), c + 1)
                if c >= 1:
                    pe.wait_ge(sem("sc_out"), c)
                for k in range(4):
                    for m in range(TOK):
                        ins = T.matmul(ps[:, 6 + m, P * k:P * k + P], pqT[:, 4 * c + k, P * m:P * m + P],
                                       keysT[:, 4 * c + k], start=True, stop=True)
                ins.then_inc(sem("psc"), 1)

            for c in range(4):
                if c >= 2:
                    pe.wait_ge(sem("pq_out"), c - 1)
                if c == 0:
                    normed_quad(FOLD_PEER, xn, 4, Q_PQ, 0)
                else:
                    for s in range(4):
                        wide_piece(Q_PQ + c, s, 2 * (c % 2))
                if c >= 1:
                    pq_turn(c - 1)
                if c >= 2:
                    key_scores(c - 2)
            pe.wait_ge(sem("pq_out"), 3)
            wide_piece(Q_PEER, 0, 0)
            pq_turn(3)
            wide_piece(Q_PEER, 1, 0)
            key_scores(2)
            wide_piece(Q_PEER, 2, 0)
            key_scores(3)
            wide_piece(Q_PEER, 3, 0)
            pe.wait_ge(sem("pq_out"), 4)

            def early_group(g, u, mid=lambda s: None):
                if not isinstance(g, int) or g >= 2:
                    pe.wait_ge(sem("gelu"), g - 1)
                for s in range(4):
                    wide_piece(g + Q_PEER, s, 2 * u)
                    mid(s)

            early_group(1, 1)
            with pe.Fori(1, EARLY_TOP // 2) as m:
                for u in range(2):
                    early_group(2 * m + u, u)
            pe.wait_ge(sem("picks"), 1)
            pe.wait_ge(sem("sc_out"), 4)
            for e in range(3):
                for m in range(TOK):
                    c0 = SEQ * e + P * m
                    ins = T.transpose(ps[:, 6 + c0 // 512, c0 % 512:c0 % 512 + P],
                                      picks[:, m, e].rearrange("p h n -> p (h n)"), ident[:])
            ins.then_inc(sem("picks_tr"), 1)

            def expert_weights(i, v):
                n = 2 * i + v
                pe.wait_ge(sem("oh"), n + 1)
                if n >= 2:
                    pe.wait_ge(sem("wst"), n - 1)
                for k in range(8):
                    ins = T.matmul(ps[:, 4 + 2 * v + k // 4, P * (k % 4):P * (k % 4) + P], oh[:, v, 0, k],
                                   oh[:, v, 1, k], start=True, stop=True)
                ins.then_inc(sem("wmm"), 1)

            def weights_pair(i):
                if i == 0:
                    pe.wait_ge(sem("picksT"), 1)
                for v in range(2):
                    expert_weights(i, v)

            for g in range(4):
                early_group(EARLY_TOP + g, g % 2, lambda s: weights_pair(4 * g + s))

            def peer_turn(b):
                pe.wait_ge(sem("pmul"), b + 1)
                turn(4, lambda k, m: pact[:, m, P * k:P * k + P]).then_inc(sem("peer_tr"), 1)

            def first_turn(s):
                if s == 2:
                    pe.wait_ge(sem("wst"), SEQ // 8)
                    peer_turn(0)

            early_group(EARLY - 1, 0, first_turn)

            def peer_down(b, q, s, u):
                if s == 0:
                    pe.wait_ge(sem("peer_lo"), b + 1)
                pe.wait_ge(sem("y_sum"), 4 * b + (s + 1))
                down_piece(q, s, 6 if s % 2 == 0 else 2, pactTh[:, u], pactTl[:, u])

            def down_group(b, u, turned=True):
                for s in range(4):
                    if s == 0:
                        pe.wait_ge(sem("peer_lo"), b + 1)
                    pe.wait_ge(sem("y_sum"), 4 * b + (s + 1))
                    down_piece(b + (Q_PEER + EARLY), s, 6 if s % 2 == 0 else 2, pactTh[:, u], pactTl[:, u])
                    if s == 1 and turned:
                        peer_turn(b + 1)

            pe.wait_ge(sem("y_sum"), 2)
            with pe.Fori(0, (EARLY - 1) // 2 - 1) as m:
                for u in range(2):
                    down_group(2 * m + u, u)
            down_group(EARLY - 3, 0)
            down_group(EARLY - 2, 1, turned=False)

            with pe.Fori(EARLY - 1, PEER_GROUPS - 1) as b:
                for j in range(8):
                    q, s = 2 * b + (Q_PEER + 1 + j // 4), j % 4
                    if j == 0:
                        pe.wait_ge(sem("gelu"), b + 1)
                    if j < 4:
                        wide_piece(q, s, 0)
                    else:
                        peer_down(b, q, s, 0)
                    if j == 1:
                        peer_turn(b)
            peer_turn(PEER_GROUPS - 1)
            for s in range(4):
                peer_down(PEER_GROUPS - 1, QUADS - 1, s, 0)


def _tables():
    eye = np.eye(P, dtype=np.float32)
    d = np.arange(-255, 257, dtype=np.int64)
    half = BUCKETS // 2
    exact = half // 2
    n = np.abs(d)
    large = exact + (np.log(np.maximum(n, 1).astype(np.float32) / np.float32(exact))
                     / np.float32(math.log(MAX_DIST / exact)) * np.float32(half - exact)).astype(np.int32)
    bucket = np.where(d > 0, half, 0) + np.where(n < exact, n, np.minimum(large, half - 1))
    oneh = (bucket[None, :] == np.arange(BUCKETS)[:, None]).astype(np.float32)
    dmask = np.zeros((6, 512), np.float32)
    for g, dil in enumerate(DILATIONS):
        dmask[2 * g:2 * g + 2] = np.where((d % dil == 0) & (n <= RADIUS_STEPS * dil), 0.0, NEG)
    r = np.repeat(np.arange(SEQ // 64), 64).astype(np.float32)
    c = np.tile(np.arange(64), SEQ // 64).astype(np.float32)
    inv = (np.float32(10000.0) ** (-np.arange(HD // 4, dtype=np.float32) / np.float32(HD // 4))).astype(np.float32)
    ang = np.concatenate([r[:, None] * inv, c[:, None] * inv], axis=-1)
    cos, sin = np.repeat(np.cos(ang), 2, axis=1), np.repeat(np.sin(ang), 2, axis=1)
    sin[:, 0::2] *= -1
    rope = np.stack([cos, sin]).reshape(2, TOK, P, HD).transpose(2, 0, 1, 3)
    f = np.arange(384)[None, :] - P
    causal = np.where(f <= np.arange(P)[:, None], 0.0, NEG)
    sel = np.repeat(np.eye(8, dtype=np.float32)[:, :, None], SEQ, axis=2)
    return {"ident": eye, "anti": eye[::-1], "iota": np.tile(np.arange(P, dtype=np.float32), (P, 1)),
            "oneh": oneh, "dmask": dmask, "rope": rope, "causal": causal, "sel": sel}


def _wide(w):
    k, n = w.shape
    return w.reshape(k // 2048, 4, 4, P, n // 512, 512).transpose(4, 0, 1, 3, 2, 5).reshape(-1, P, 2048)


def _down(w):
    k, n = w.shape
    return w.reshape(k // 512, 4, P, n // 512, 512).transpose(0, 3, 2, 1, 4).reshape(-1, P, 2048)


def _columns(v):
    return v.reshape(-1, P).T


def kernel(**inputs):
    import concourse.bacc as bacc
    from concourse.bass_utils import run_bass_kernel_spmd

    v = {k: np.asarray(a) for k, a in inputs.items()}
    w_in = v["w_in"][0]
    A_W, B_Q, B_K, C_W = 768, 768, 256, 512
    o = np.cumsum([0, A_W, A_W, A_W, B_Q, B_K, B_K, C_W, 3 * D])
    qa, ka, va, qb, kb, vb, qc, gt = [w_in[:, o[i]:o[i + 1]] for i in range(8)]
    w_mem = v["w_mem_kv"][0]
    first = np.concatenate([_wide(w_mem)] + [_wide(a) for a in (
        np.concatenate([qa, ka, qc, qb, kb, va, vb], axis=1), gt)])
    branch = np.concatenate([v["w_br_a"][0], v["w_br_b"][0], v["w_br_c"][0]])
    branch = branch.reshape(3, 4, P, 4, 512).transpose(3, 0, 2, 1, 4).reshape(-1, P, 2048)
    merge = np.concatenate([branch, _wide(v["w_o"][0])])
    gate, up = _wide(v["w_ffn_in"][0][:, :D_FF]), _wide(v["w_ffn_in"][0][:, D_FF:])
    down = _down(v["w_ffn_out"][0])
    g4, u4, d4 = (a.reshape(FF_GROUPS, 4, P, 2048) for a in (gate, up, down))
    order = [g4[0], u4[0]]
    for g in range(1, FF_GROUPS):
        order += [g4[g], u4[g], d4[g - 1]]
    ffn = np.concatenate(order + [d4[-1]])
    w2 = v["w_in_2"][0]
    second = np.concatenate([_wide(a) for a in (
        w2[:, 3080:4104], w2[:, 4104:5128], w2[:, 0:3072], v["w_out_2"][0], v["peer_w_q_2"][0])])
    pu = _wide(v["peer_u_2"][0].T).reshape(PEER_GROUPS, 4, P, 2048)
    pv = _down(v["peer_v_2"][0]).reshape(PEER_GROUPS, 4, P, 2048)
    order = [*pu[:EARLY], *pv[:EARLY - 1]]
    for g in range(EARLY, PEER_GROUPS):
        order += [pu[g], pv[g - 1]]
    peer = np.concatenate(order + [pv[-1]])
    cols = np.zeros((P, NCOLS), np.float32)
    for at0, name in ((C_GMEM, "g_mem"), (C_GMIX, "g_mix"), (C_GFFN, "g_ffn"), (C_GMIX2, "g_mix_2"), (C_GFFN2, "g_ffn_2")):
        cols[:, at0:at0 + 16] = _columns(v[name][0])
    for at0, n, name in ((0, 6, "g_qa"), (6, 6, "g_ka"), (12, 4, "g_qc"), (16, 4, "g_kc")):
        cols[:, C_HEAD + at0:C_HEAD + at0 + n] = v[name][0][:, None]
    for j in range(CONV):
        cols[:, C_CONVW + 8 * j:C_CONVW + 8 * j + 8] = _columns(v["conv_w_2"][0, j])
    for at0, name in ((C_CONVB, "conv_b_2"), (C_BA, "lru_b_a_2"), (C_BX, "lru_b_x_2"), (C_LAM, "lru_lambda_2"),
                      (C_GLRU, "g_lru_out_2"), (C_GATT, "g_attn_out_2")):
        cols[:, at0:at0 + 8] = _columns(v[name][0])
    cols[0:8, C_BF] = v["b_f_2"][0]
    keys = np.stack([v["peer_k1_2"][0], v["peer_k2_2"][0]], axis=1).reshape(16, N_KEYS, P).transpose(2, 0, 1)
    arrays = {
        "x": v["x"][0], "mem": v["mem"][0], "w_first": first, "w_merge": merge, "w_ffn": ffn,
        "w_second": second, "w_peer": peer, "cols": cols, "rel_bias": v["rel_bias"],
        "g_qb": v["g_qb"], "g_kb": v["g_kb"], "c": _columns(v["c_2"][0]),
        "w_ada": v["w_ada_2"][0].reshape(8, 2, P, ADA_SPLITS, 1024).transpose(3, 0, 2, 1, 4).reshape(-1, P, 2048),
        "b_ada": v["b_ada_2"][0].reshape(ADA_SPLITS, 1, 1024),
        "w_f": w2[:, 3072:3080].reshape(KT, P, 8).transpose(1, 0, 2),
        "lru_w_a": v["lru_w_a_2"][0].transpose(1, 0, 2), "lru_w_x": v["lru_w_x_2"][0].transpose(1, 0, 2),
        "keys": keys, "g_final": v["g_final_2"].reshape(1, D), **_tables()}
    arrays = {f"in_{k}": np.ascontiguousarray(a, dtype=np.float32) for k, a in arrays.items()}
    nc = bacc.Bacc("TRN2", target_bir_lowering=False, num_devices=1)
    aps = {k[3:]: nc.dram_tensor(k, a.shape, F32, kind="ExternalInput").ap() for k, a in arrays.items()}
    aps["out"] = nc.dram_tensor("out", (SEQ, D), F32, kind="ExternalOutput").ap()
    program(nc, aps)
    r = run_bass_kernel_spmd(nc, [arrays], core_ids=[0])
    return np.asarray(r.results[0]["out"]).reshape(1, SEQ, D)
```

```python
import math
import numpy as np
import concourse.bass as bass
from concourse import mybir

F32 = mybir.dt.float32
F32R = mybir.dt.float32r
U32 = mybir.dt.uint32
ALU = mybir.AluOpType
ACT = mybir.ActivationFunctionType
AX = mybir.AxisListType

P = 128
D = 2048
SEQ = 256
TOK = SEQ // P
KT = D // P
HD = 128
EPS = 1e-6
NEG = -1e30
SCALE = 1.0 / math.sqrt(HD)

A_HEADS, B_HEADS, B_KV, C_HEADS = 6, 6, 2, 4
ROPE_HEADS = B_HEADS + B_KV
HEADS = A_HEADS + B_HEADS + C_HEADS
D_FF = 5632
FF_GROUPS = D_FF // 512
ADA = 6 * D
ADA_SPLITS = ADA // 1024
H2 = 8
LRU = 1024
CONV = 4
N_KEYS = 128
EXPERTS = N_KEYS * N_KEYS
PEER_GROUPS = EXPERTS // 512
TOPK = 16
BUCKETS, MAX_DIST = 32, 1024
DILATIONS = (1, 4, 16)
RADIUS_STEPS = 64
EARLY_TOP = 6
EARLY = EARLY_TOP + 5
assert EARLY_TOP % 2 == 0 and (EARLY - 1) % 2 == 0

Q_MEM = 0
Q_HEADS = Q_MEM + 2
Q_GATES = Q_HEADS + 8
Q_BRANCH = Q_GATES + 12
Q_WO = Q_BRANCH + 3
Q_FFN = Q_WO + 4
Q_IN2 = Q_FFN + 3 * FF_GROUPS
Q_OUT2 = Q_IN2 + 10
Q_PQ = Q_OUT2 + 4
Q_PEER = Q_PQ + 4
QUADS = Q_PEER + 2 * PEER_GROUPS

IN_CHUNKS = 10
TURNED = (0, 1, 3, 4, 6, 7, 8, 9)
SCORES_AT = {1: 0, 3: 1, 5: 2, 7: 3, 9: 4, 12: 5, 14: 6, 16: 7}
TURN_AT = {2: 0, 4: 1, 6: 2, 8: 3, 10: 4, 13: 5, 15: 6, 17: 7}
OUTPUT_AT = {3: 0, 5: 1, 7: 2, 9: 3, 12: 4, 14: 5, 16: 6, 18: 7}
OUT_PIECES = [(0, 0), (0, 1), (1, 0), (1, 1), (0, 2), (0, 3), (1, 2), (1, 3)] + [(c, g) for c in (2, 3) for g in range(4)]
OUT_DONE = {5: 0, 7: 1, 11: 2, 15: 3}

C_GMEM, C_GMIX, C_GFFN, C_GMIX2, C_GFFN2 = (16 * i for i in range(5))
C_HEAD = 80
C_CONVW = C_HEAD + 20
C_CONVB = C_CONVW + CONV * 8
C_BA = C_CONVB + 8
C_BX = C_BA + 8
C_LAM = C_BX + 8
C_GLRU = C_LAM + 8
C_GATT = C_GLRU + 8
C_BF = C_GATT + 8
NCOLS = C_BF + 1

FOLD_MEM, FOLD_X, FOLD_O, FOLD_M, FOLD_FFN, FOLD_MIX2, FOLD_ATT, FOLD_LRU, FOLD_PEER = 0, 4, 8, 11, 15, 19, 23, 25, 27

SIGNALS = {
    "raw_in0": "DMA: piece in slot 0 is loaded (16 each)", "raw_in1": "slot 1", "raw_in2": "slot 2", "raw_in3": "slot 3",
    "hi_done": "ACT: pieces rounded", "lo_done": "DVE or Pool: pieces whose rest is there",
    "piece_used": "PE: pieces whose products are done",
    "ident_in": "DMA: identity", "mem_in0": "DMA: memory, columns 0-1023", "mem_in1": "DMA: memory, the others",
    "cols_in": "DMA: per-partition constants", "const_in": "DMA: the other constants", "x_in": "DMA: residual stream",
    "x_back": "DMA: residual stream back in its place", "x_st": "DMA: residual stream in DRAM",
    "bias_mm": "PE: biases by distance", "bvec": "DVE: masked biases", "bias_st": "DMA: biases in DRAM",
    "hank_in0": "DMA: bias of an even head", "hank_in1": "DMA: bias of an odd head",
    "warm": "ACT: the root's table is loaded", "sq_done": "ACT: sums of squares", "ms_done": "DVE: mean squares",
    "root_done": "ACT: their roots", "rstd_done": "DVE: one over the roots", "xn_done": "ACT: scaled copies",
    "fold_tr": "PE: groups turned", "fold_t": "DVE: groups with gain and shift", "fold_hi": "ACT: groups' leading parts",
    "fold_lo": "DVE: groups' rests", "dve_seq": "DVE: its own earlier instructions",
    "chunk_out": "ACT: chunks out of PSUM", "head_ms": "DVE: heads' mean squares", "head_root": "ACT: their roots",
    "head_n": "DVE: chunks normed", "head_tr": "PE: chunks turned", "head_T": "DVE: turned chunks out of PSUM",
    "att_s": "PE: heads' scores", "att_m": "DVE: maxima", "att_e": "ACT: exponentials (two a head)",
    "att_t": "PE: turned probabilities", "att_p": "DVE: these out of PSUM", "att_v": "PE: outputs",
    "att_o": "DVE: outputs out of PSUM", "cmb_d": "DVE: groups' maxima compared", "cmb_e": "ACT: their exponentials",
    "o_ready": "DVE: dilated groups joined", "gate_st": "DMA: gate chunks in DRAM",
    "gl_in0": "DMA: gate in ring slot 0", "gl_in1": "slot 1", "gl_in2": "slot 2", "gl_in3": "slot 3",
    "gated": "DVE: branch chunks gated", "merge": "DVE: chunks merged", "wo_out": "DVE: chunks of w_o added to x",
    "cs_done": "ACT: silu of c", "ada_in0": "DMA: even pieces", "ada_in1": "DMA: odd pieces",
    "ada_sum": "DVE: column tiles added up", "ada_used": "DVE: pieces used", "ada_mm": "PE: sums over partitions",
    "bada_in": "DMA: bias of a split", "modrow": "DVE: halves of a split", "mod_st": "DMA: splits in DRAM",
    "modT_in": "DMA: shifts and scales by column", "ga1_in": "DMA: first gate",
    "silu": "ACT: groups' gates", "ffn_product": "DVE: groups' products", "ffn_tr": "PE: these turned",
    "ffn_hi": "ACT: their leading parts", "ffn_lo": "DVE: and rests", "x_sum": "DVE: chunks added to x, from two",
    "in_out": "ACT: chunks out of PSUM", "in_tr": "PE: chunks turned", "lx_T": "DVE: turned inputs out of PSUM",
    "gy_T": "ACT: gelu of the turned gates", "qk_T": "DVE: turned queries and keys out of PSUM",
    "wf_in": "DMA: forget weights", "wfh": "ACT: their leading part", "wfl": "DVE: and rest", "f_mm": "PE: forget logits",
    "lg_abs": "DVE: logits' size", "lg_exp": "ACT: its exponential", "cum": "DVE: sums of log gates",
    "sel_in": "DMA: head selectors", "scores2": "PE: heads' scores", "max2": "DVE: maxima",
    "exp2": "ACT: exponentials (two a head)", "turned2": "PE: turned probabilities", "probs2": "DVE: these out of PSUM",
    "values2": "PE: outputs", "output2": "DVE: outputs over their denominators",
    "ssq2": "ACT: outputs' squares", "ms2": "DVE: mean squares", "ms2_root": "ACT: their roots",
    "rstd2": "DVE: one over the roots", "att2_s": "ACT: scaled outputs",
    "lam_n": "DVE: -|lambda|", "lam_e": "ACT: its exponential", "sp_done": "DVE: softplus(-lambda)",
    "tap": "DVE: taps of the convolution but the last", "conv": "DVE: convolved tiles", "lw_in": "DMA: gates' weights",
    "lru_mm": "PE: tiles times these", "r_out": "ACT: gates r", "i_out": "ACT: gates i", "i_used": "DVE: gated inputs",
    "dec": "ACT: decays", "tanh": "ACT: hyperbolic tangents", "root2": "ACT: input's factor", "scan": "DVE: scans",
    "lsq": "DVE: halves squared", "lsum_mm": "PE: sums of squares", "lru_ms": "DVE: mean squares",
    "lru_root": "ACT: their roots", "out2": "DVE: chunks out of PSUM", "out2_sum": "DVE: chunks added to x",
    "pq_out": "ACT: query chunks out of PSUM", "pq_tr": "PE: turned", "pq_T": "DVE: turned chunks out of PSUM",
    "keys_in": "DMA: both key sets", "key_scores": "PE: scores against them", "sc_out": "DVE: scores out of PSUM",
    "wexp_in": "DVE: chosen scores less their maximum", "wexp": "ACT: exponentials", "picks": "DVE: choice and weights",
    "picks_tr": "PE: turned", "picksT": "DVE: out of PSUM", "one_hots_raw": "DVE: one-hot rows",
    "one_hots": "DVE: and weighted", "weights_mm": "PE: eight tokens' dense weights", "weights_out": "ACT: out of PSUM",
    "w_st0": "DMA: even batches in DRAM", "w_st1": "DMA: odd batches in DRAM",
    "gelu": "ACT: groups' hidden values", "hid_st": "DMA: early groups' in DRAM", "hid_in0": "DMA: back, even groups",
    "hid_in1": "DMA: back, odd groups", "wc_in0": "DMA: weights of a group, slot 0", "wc_in1": "slot 1",
    "peer_product": "DVE: hidden values times weights", "peer_tr": "PE: turned", "peer_hi": "ACT: leading part",
    "peer_lo": "DVE: rest", "y_sum": "DVE: chunks added to y, from two", "tail_in": "DMA: last factors",
    "x_ready": "DVE: x's final chunks", "final": "DVE: scaled rows", "out_st": "DMA: output",
}


def program(nc, t):
    base0 = 16512
    K = 1024

    def at(name, shape, dt, off):
        return nc.alloc_sbuf_tensor_at(name, shape, dt, offset=base0 + off)

    raw = at("raw", [P, 4, 2048], F32, 0)
    hi = at("hi", [P, 4, 2048], F32R, 32 * K)
    lo = at("lo", [P, 4, 2048], F32R, 64 * K)
    XO = 96 * K
    x = at("x", [P, TOK, D], F32, XO)
    hTh = at("hTh", [P, KT, SEQ], F32R, 112 * K)
    hTl = at("hTl", [P, KT, SEQ], F32R, 128 * K)
    A = 144 * K
    memraw = at("memraw", [P, TOK, D], F32, 112 * K)
    memTh = at("memTh", [P, KT, SEQ], F32R, A)
    memTl = at("memTl", [P, KT, SEQ], F32R, A + 16 * K)
    qkT = at("qkT", [P, 24, SEQ], F32, A)
    vAB = at("vAB", [P, TOK, 8, HD], F32, A + 24 * K)
    kcT = at("kcT", [P, C_HEADS, SEQ], F32, A + 32 * K)
    vC = at("vC", [P, TOK, C_HEADS, HD], F32, A + 36 * K)
    hank = at("hank", [P, 2, 384], F32, A + 40 * K)
    rope = at("rope", [P, 2, TOK, HD], F32, A + 43 * K)
    stage = at("stage", [P, TOK, 512], F32, A + 45 * K)
    stage2 = at("stage2", [P, TOK, 512], F32, A + 49 * K)
    fold = at("fold", [P, 2, 4, SEQ], F32, A + 45 * K)
    probs = at("probs", [P, TOK, SEQ], F32, A + 45 * K)
    probsT = at("probsT", [P, TOK, SEQ], F32, A + 49 * K)
    gst = at("gst", [P, TOK, 512], F32, A + 53 * K)
    obuf = at("obuf", [P, TOK, HEADS, HD], F32, XO)
    tabs = at("tabs", [32, 6], F32, A + 38 * K)
    oneh = at("oneh", [32, 512], F32, A + 32 * K)
    dmask = at("dmask", [6, 512], F32, A + 34 * K)
    bvec = at("bvec", [6, 512], F32, A + 36 * K)
    oTh = at("oTh", [P, 12, SEQ], F32R, A)
    oTl = at("oTl", [P, 12, SEQ], F32R, A + 12 * K)
    merged = at("merged", [P, TOK, D], F32, A + 24 * K)
    gl = at("gl", [P, 4, TOK, 512], F32, XO)
    mt0 = at("mt0", [P, TOK, 512], F32, A + 40 * K)
    mt1 = at("mt1", [P, TOK, 512], F32, A + 53 * K)
    xn = at("xn", [P, TOK, D], F32, A + 24 * K)
    adaraw = at("adaraw", [P, 2, 2, 1024], F32, A)
    adaacc = at("adaacc", [P, 1024], F32, A + 16 * K)
    modrow = at("modrow", [1, 1024], F32, A + 20 * K)
    gact = at("gact", [P, TOK, 512], F32, A + 40 * K)
    fact = at("fact", [P, TOK, 512], F32, A + 53 * K)
    factTh = at("factTh", [P, 4, SEQ], F32R, A + 45 * K)
    factTl = at("factTl", [P, 4, SEQ], F32R, A + 49 * K)
    qkT2 = at("qkT2", [P, 16, SEQ], F32, A)
    v2 = at("v2", [P, TOK, LRU], F32, A + 16 * K)
    lxT = at("lxT", [P, 8, 260], F32, A + 24 * K)
    dec = at("dec", [P, 8, SEQ], F32, A + 24 * K)
    gyT = at("gyT", [P, 8, SEQ], F32, A + 16 * K)
    istage = at("istage", [P, 2, SEQ], F32, A + 41 * K)
    wf = at("wf", [P, KT, 8], F32, A + 43 * K)
    wfh = at("wfh", [P, KT, 8], F32R, A + 43 * K + 512)
    wfl = at("wfl", [P, KT, 8], F32R, A + 44 * K)
    lwx = at("lwx", [P, 8, P], F32, A + 49 * K)
    lwa = at("lwa", [P, 8, P], F32, A + 53 * K)
    uT = at("uT", [P, 8, SEQ], F32, XO)
    bx = at("bx", [P, 8, SEQ], F32, XO + 8 * K)
    sel = at("sel", [8, 8, SEQ], F32, XO)
    probs2 = at("probs2", [P, 2, TOK, SEQ], F32, A + 41 * K)
    probsT2 = at("probsT2", [P, 2, TOK, SEQ], F32, A + 53 * K)
    att2 = at("att2", [P, TOK, H2, HD], F32, A + 33 * K)
    attTh = at("attTh", [P, 8, SEQ], F32R, A)
    attTl = at("attTl", [P, 8, SEQ], F32R, A + 8 * K)
    lsq = at("lsq", [P, 8, SEQ], F32, XO + 8 * K)
    lgate = at("lgate", [8, 4, SEQ], F32, A + 49 * K)
    ga1 = at("ga1", [P, D], F32, A + 24 * K)
    mt2 = at("mt2", [P, TOK, 512], F32, A + 33 * K)
    lrs = at("lrs", [P, 2, SEQ], F32, A + 37 * K)
    pqT = at("pqT", [P, 16, SEQ], F32, A)
    keysT = at("keysT", [P, 16, P], F32, A + 16 * K)
    sc = at("sc", [P, TOK, 16, N_KEYS], F32, A + 24 * K)
    cand = at("cand", [P, 8, 256], F32, A)
    work = at("work", [P, 8, 256], F32, A + 8 * K)
    work2 = at("work2", [P, 8, 256], F32, A + 16 * K)
    top = at("top", [P, TOK, 16, TOPK], F32, A + 40 * K)
    topi = at("topi", [P, TOK, 16, TOPK], U32, A + 42 * K)
    topf = at("topf", [P, TOK, 16, TOPK], F32, A + 44 * K)
    picks = at("picks", [P, TOK, 3, 8, TOPK], F32, A + 46 * K)
    best = at("best", [P, TOK, 8, TOPK], F32, A + 49 * K)
    besti = at("besti", [P, TOK, 8, TOPK], U32, A + 50 * K)
    divi = at("divi", [P, 2, 8, TOPK], U32, A + 51 * K)
    divf = at("divf", [P, 2, 8, TOPK], F32, A + 52 * K)
    picksT = at("picksT", [P, 3, SEQ], F32, A + 40 * K)
    gacc = at("gacc", [P, TOK, 512], F32, A + 53 * K)
    oh = at("oh", [P, 2, 2, 8, P], F32, A + 24 * K)
    wst = at("wst", [P, 2, 8, P], F32, A + 16 * K)
    y = at("y", [P, TOK, D], F32, A)
    wc = at("wc", [P, 2, TOK, 512], F32, A + 16 * K)
    pact = at("pact", [P, TOK, 512], F32, A + 24 * K)
    pactTh = at("pactTh", [P, 2, 4, SEQ], F32R, A + 28 * K)
    pactTl = at("pactTl", [P, 2, 4, SEQ], F32R, A + 36 * K)
    hid = at("hid", [P, 2, TOK, 512], F32, A + 44 * K)
    ga2 = at("ga2", [P, D], F32, A + 40 * K)
    gfin = [at("gfin0", [P, 1024], F32, A + 48 * K), at("gfin1", [P, 1024], F32, A + 32 * K)]

    CO = A + 57 * K
    ident = at("ident", [P, P], F32, CO)
    anti = at("anti", [P, P], F32, CO + 512)
    ones = at("ones", [P, P], F32, CO + 1 * K)
    iota = at("iota", [P, P], F32, CO + 1 * K + 512)
    cols = at("cols", [P, NCOLS], F32, CO + 2 * K)
    gb = at("gb", [P, 2, HD], F32, CO + 3 * K)
    causal = at("causal", [P, P], F32, CO + 4 * K)
    small_at = [CO + 5 * K + 512]

    def small(name, shape, dt=F32):
        words = int(np.prod(shape[1:]))
        h = at(name, shape, dt, small_at[0])
        small_at[0] += -(-words * 4 // 32) * 32
        return h

    ssum = small("ssum", [P, TOK])
    warm = small("warm", [P, 1])
    sq = small("sq", [P, TOK, 4])
    rstd = small("rstd", [P, 2, TOK])
    hss = small("hss", [P, 3, 8])
    cs = small("cs", [P, 16])
    modT = small("modT", [P, 4, 16])
    gmod = small("gmod", [P, 16])
    lam = small("lam", [P, 4, 8])
    spn = small("spn", [P, 2, 8])
    negm = small("negm", [P, TOK, HEADS])
    lsum = small("lsum", [P, TOK, HEADS])
    fac = small("fac", [P, TOK, HEADS])
    cmb = small("cmb", [P, 2, TOK, 6])
    cmx = small("cmx", [P, 2, TOK, 2])
    assert base0 + small_at[0] <= 229368, small_at
    wsm = at("wsm", [P, TOK, 8, 2], F32, CO + 4 * K)

    ps = nc.alloc_psum_tensor("ps", [P, 8, 512], F32)

    def pair(b):
        return ps[:, b:b + 2, :]

    def quarters(b):
        return ps[:, b:b + 2, :].rearrange("p b (k t) -> p (b k) t", t=SEQ)

    def fold_bank(f):
        if FOLD_ATT <= f < FOLD_LRU:
            return 6
        return 4 if FOLD_M <= f < FOLD_FFN else 4 + 2 * (f % 2)

    bias_d = nc.dram_tensor("bias_scratch", [6, 512], F32, kind="Internal").ap()
    gates_d = nc.dram_tensor("gates_scratch", [12, P, TOK * 512], F32, kind="Internal").ap()
    mod_d = nc.dram_tensor("mod_scratch", [ADA], F32, kind="Internal").ap()
    x_d = nc.dram_tensor("x_scratch", [P, TOK * D], F32, kind="Internal").ap()
    w_d = nc.dram_tensor("w_scratch", [SEQ, EXPERTS], F32, kind="Internal").ap()
    hid_d = nc.dram_tensor("hidden_scratch", [EARLY - 1, P, TOK * 512], F32, kind="Internal").ap()

    sems = {}

    def sem(name):
        if name not in sems:
            assert name in SIGNALS, name
            sems[name] = nc.alloc_semaphore(name)
        return sems[name]

    raw_in = [sem(f"raw_in{s}") for s in range(4)]
    hi_done, lo_done, piece_used = sem("hi_done"), sem("lo_done"), sem("piece_used")
    head_quads = [0, 2, 3, 4, 5, 6, 7]
    ADA_IN = [sem("ada_in0"), sem("ada_in1")]

    with nc.Block() as block:

        @block.sync
        def _(sp):
            sp.dma_start(ident[:], t["ident"]).then_inc(sem("ident_in"), 16)
            for c in range(4):
                cut = slice(512 * c, 512 * c + 512)
                sp.dma_start(memraw[:, :, cut], t["mem"].rearrange("(k p) d -> p k d", p=P)[:, :, cut])\
                    .then_inc(sem(f"mem_in{c // 2}"), 16)
            sp.dma_start(cols[:], t["cols"]).then_inc(sem("cols_in"), 16)

            def load(src, q, n):
                for s in range(4):
                    if not isinstance(q, int) or q >= 1:
                        sp.wait_ge(lo_done, 4 * q + (s - 3))
                    sp.dma_start(raw[:, s, :], src[4 * n + s]).then_inc(raw_in[s], 16)

            load(t["w_first"], 0, 0)
            sp.dma_start(x[:], t["x"].rearrange("(k p) d -> p k d", p=P)).then_inc(sem("x_in"), 16)
            for dst, src in ((anti, "anti"), (cs, "c"), (iota, "iota"), (causal, "causal"), (tabs, "rel_bias"),
                             (oneh, "oneh"), (dmask, "dmask"), (rope, "rope")):
                sp.dma_start(dst[:], t[src]).then_inc(sem("const_in"), 16)
            sp.dma_start(gb[:, 0, :], t["g_qb"].to_broadcast([P, HD])).then_inc(sem("const_in"), 16)
            sp.dma_start(gb[:, 1, :], t["g_kb"].to_broadcast([P, HD])).then_inc(sem("const_in"), 16)
            with sp.Fori(1, Q_BRANCH) as n:
                load(t["w_first"], n, n)
            with sp.Fori(0, Q_FFN - Q_BRANCH) as n:
                load(t["w_merge"], n + Q_BRANCH, n)
            with sp.Fori(0, 3 * FF_GROUPS) as n:
                load(t["w_ffn"], n + Q_FFN, n)
            with sp.Fori(0, Q_PEER - Q_IN2) as n:
                load(t["w_second"], n + Q_IN2, n)
            with sp.Fori(0, 2 * PEER_GROUPS) as n:
                load(t["w_peer"], n + Q_PEER, n)
            for c in range(4):
                sp.wait_ge(sem("final"), 2 * c + 2)
                cut = slice(512 * c, 512 * c + 512)
                sp.dma_start(t["out"].rearrange("(k p) d -> p k d", p=P)[:, :, cut], x[:, :, cut])\
                    .then_inc(sem("out_st"), 16)
            sp.wait_ge(sem("out_st"), 64)

        @block.gpsimd
        def _(pool):
            def rest_piece(q, s):
                pool.wait_ge(hi_done, 4 * q + (s + 1))
                if not isinstance(q, int) or q >= 1:
                    pool.wait_ge(piece_used, 4 * q + (s - 3))
                nc.gpsimd.tensor_tensor(lo[:, s, :], raw[:, s, :], hi[:, s, :].bitcast(F32), ALU.subtract)\
                    .then_inc(lo_done, 1)

            for s in range(4):
                rest_piece(0, s)
            pool.wait_ge(sem("bvec"), 1)
            pool.dma_start(bias_d, bvec[:]).then_inc(sem("bias_st"), 16)
            pool.wait_ge(sem("bias_st"), 16)

            def load_hankel(h):
                if h >= 2:
                    pool.wait_ge(sem("att_s"), h - 1)
                src = bass.AP(bias_d.tensor, h * 512, [[1, P], [1, 384]])
                pool.dma_start(hank[:, h % 2, :], src).then_inc(sem(f"hank_in{h % 2}"), 16)

            load_hankel(0)
            load_hankel(1)

            def store_gates(c):
                pool.wait_ge(sem("chunk_out"), Q_GATES + c + 1)
                pool.dma_start(gates_d[c], gst[:].rearrange("p k n -> p (k n)")).then_inc(sem("gate_st"), 16)

            for n in range(48):
                if n % 3 == 0 and n // 3 + 2 < A_HEADS:
                    load_hankel(n // 3 + 2)
                if n % 4 == 3:
                    store_gates(n // 4)
            pool.wait_ge(lo_done, 4 * (Q_BRANCH + 1))
            for n in range(12):
                rest_piece(Q_BRANCH + 1 + n // 4, n % 4)
            pool.wait_ge(sem("merge"), 4)
            pool.dma_start(x[:], t["x"].rearrange("(k p) d -> p k d", p=P)).then_inc(sem("x_back"), 16)

            pool.wait_ge(piece_used, 4 * Q_WO)

            def ada_piece(a, j, first):
                if not first:
                    pool.wait_ge(sem("ada_used"), 8 * a + (j - 1))
                pool.dma_start(adaraw[:, j % 2, :, :].rearrange("p k n -> p (k n)"), t["w_ada"][8 * a + j])\
                    .then_inc(ADA_IN[j % 2], 16)

            def ada_row_in(a):
                pool.dma_start(modrow[:], t["b_ada"][a]).then_inc(sem("bada_in"), 16)

            def ada_row_out(a):
                pool.wait_ge(sem("modrow"), 2 * a)
                pool.dma_start(mod_d.rearrange("(a o n) -> a o n", o=1, n=1024)[a - 1],
                               modrow[0:1, :]).then_inc(sem("mod_st"), 16)
                pool.wait_ge(sem("mod_st"), 16 * a)

            for j in range(8):
                ada_piece(0, j, j < 2)
                if j == 3:
                    ada_row_in(0)
            with pool.Fori(1, ADA_SPLITS) as a:
                for j in range(8):
                    ada_piece(a, j, False)
                    if j == 3:
                        ada_row_out(a)
                        ada_row_in(a)
            for k, part in enumerate((0, 1, 3, 4)):
                with nc.allow_non_contiguous_dma(reason="a column of the modulation for each partition"):
                    pool.dma_start(modT[:, k, :], mod_d[part * D:(part + 1) * D].rearrange("(k p) -> p k", p=P))\
                        .then_inc(sem("modT_in"), 16)
            ada_row_out(ADA_SPLITS)
            pool.wait_ge(sem("xn_done"), 8 * 4)
            pool.dma_start(x_d, x[:].rearrange("p k n -> p (k n)")).then_inc(sem("x_st"), 16)
            pool.dma_start(wf[:], t["w_f"]).then_inc(sem("wf_in"), 16)
            pool.wait_ge(sem("x_st"), 16)
            pool.dma_start(sel[:], t["sel"]).then_inc(sem("sel_in"), 16)
            pool.wait_ge(sem("values2"), H2)
            pool.dma_start(lwa[:], t["lru_w_a"]).then_inc(sem("lw_in"), 16)
            pool.dma_start(lwx[:], t["lru_w_x"]).then_inc(sem("lw_in"), 16)
            pool.wait_ge(sem("scan"), 8)
            pool.dma_start(ga1[:], bass.AP(mod_d.tensor, 2 * D, [[0, P], [1, D]])).then_inc(sem("ga1_in"), 16)
            pool.wait_ge(sem("lru_ms"), 1)
            pool.dma_start(x[:].rearrange("p k n -> p (k n)"), x_d).then_inc(sem("x_back"), 16)
            pool.wait_ge(sem("xn_done"), 8 * 5)
            pool.dma_start(keysT[:], t["keys"]).then_inc(sem("keys_in"), 16)

            pool.wait_ge(lo_done, 4 * (Q_PEER + 1))
            with pool.Fori(0, EARLY - 1) as g:
                for s in range(4):
                    rest_piece(g + (Q_PEER + 1), s)

            def load_group(g, u):
                pool.dma_start(wc[:, u], (w_d[:, bass.ds(g * 512, 512)] if not isinstance(g, int) else
                                          w_d[:, 512 * g:512 * g + 512]).rearrange("(k p) n -> p k n", p=P))\
                    .then_inc(sem(f"wc_in{u}"), 16)
                if not isinstance(g, int) or g < EARLY - 1:
                    pool.dma_start(hid[:, u].rearrange("p k n -> p (k n)"), hid_d[g]).then_inc(sem(f"hid_in{u}"), 16)

            for u in range(2):
                pool.wait_ge(sem(f"w_st{u}"), 16 * (SEQ // 16))
            pool.wait_ge(sem("hid_st"), 16 * (EARLY - 1))
            load_group(0, 0)
            load_group(1, 1)
            with pool.Fori(1, (EARLY - 1) // 2) as m:
                for u in range(2):
                    pool.wait_ge(sem("peer_product"), 2 * m + (u - 1))
                    load_group(2 * m + u, u)
            pool.wait_ge(sem("peer_product"), EARLY - 2)
            load_group(EARLY - 1, 0)

            def load_weights(g):
                pool.wait_ge(sem("peer_product"), g)
                at0 = slice(512 * g, 512 * g + 512) if isinstance(g, int) else bass.ds(g * 512, 512)
                pool.dma_start(wc[:, 0], w_d[:, at0].rearrange("(k p) n -> p k n", p=P)).then_inc(sem("wc_in0"), 16)

            load_weights(EARLY)
            load_weights(EARLY + 1)
            pool.dma_start(ga2[:], bass.AP(mod_d.tensor, 5 * D, [[0, P], [1, D]])).then_inc(sem("tail_in"), 16)
            for k in range(2):
                pool.dma_start(gfin[k][:], t["g_final"][:, 1024 * k:1024 * k + 1024].to_broadcast([P, 1024]))\
                    .then_inc(sem("tail_in"), 16)
            with pool.Fori(EARLY + 2, PEER_GROUPS) as g:
                load_weights(g)

        @block.scalar
        def _(act):
            def round_piece(q, s):
                act.wait_ge(raw_in[s], 16 * q + 16)
                if not isinstance(q, int) or q >= 1:
                    act.wait_ge(piece_used, 4 * q + (s - 3))
                nc.scalar.copy(hi[:, s, :], raw[:, s, :]).then_inc(hi_done, 1)

            def squares(u, c, src):
                if c == (2 if u else 0):
                    nc.scalar.activation(warm[:], ident[:, 0:1], ACT.Sqrt).then_inc(sem("warm"), 1)
                for k in range(TOK):
                    n = 8 * u + 2 * c + k
                    if n >= 2:
                        act.wait_ge(sem("sq_done"), n - 1)
                    nc.scalar.activation(gst[:, k], src[:, k, 512 * c:512 * c + 512], ACT.Square,
                                         accum_out=sq[:, k, c:c + 1]).then_inc(sem("sq_done"), 1)

            def norm(u, src, f0, dst_t, held=None, between=lambda g: None):
                dst = src if u < 2 else xn
                act.wait_ge(sem("ms_done"), u + 1)
                nc.scalar.activation(rstd[:, 0, :], ssum[:], ACT.Sqrt).then_inc(sem("root_done"), 1)
                act.wait_ge(sem("rstd_done"), u + 1)

                def scaled(c):
                    for k in range(TOK):
                        cut = slice(512 * c, 512 * c + 512)
                        nc.scalar.activation(dst[:, k, cut], src[:, k, cut], ACT.Copy, scale=rstd[:, 1, k:k + 1])\
                            .then_inc(sem("xn_done"), 1)

                scaled(0)
                scaled(1)
                if held is not None:
                    round_piece(*held)
                for g in range(4):
                    fold_hi(f0 + g, dst_t, 4 * g)
                    between(g)
                    if g < 2:
                        scaled(g + 2)

            def fold_hi(f, dst, at0):
                act.wait_ge(sem("fold_t"), f + 1)
                nc.scalar.copy(dst[:, at0:at0 + 4, :], fold[:, f % 2]).then_inc(sem("fold_hi"), 1)

            act.wait_ge(sem("ident_in"), 16)
            for c in range(4):
                act.wait_ge(sem(f"mem_in{c // 2}"), 32)
                squares(0, c, memraw)

            def while_memory_folds(g):
                round_piece(0, g)
                if g == 2:
                    act.wait_ge(sem("x_in"), 16)
                    for c in range(4):
                        squares(1, c, x)

            norm(0, memraw, FOLD_MEM, memTh, between=while_memory_folds)
            for s in range(2):
                round_piece(1, s)
            act.wait_ge(sem("fold_tr"), FOLD_X)
            norm(1, x, FOLD_X, hTh, (1, 2), lambda g: round_piece(1, 3 + g) if g < 1 else None)
            for q in range(Q_GATES):
                if q >= 1:
                    for s in range(4):
                        round_piece(q + 1, s)
                act.wait_ge(piece_used, 4 * q + 4)
                if q in head_quads:
                    n = head_quads.index(q)
                    if n == 0:
                        act.wait_ge(sem("fold_lo"), FOLD_O)
                    else:
                        act.wait_ge(sem("head_tr"), n)
                    nc.scalar.copy(stage[:], pair(2 * (q % 2))).then_inc(sem("chunk_out"), 1)
                    act.wait_ge(sem("head_ms"), n + 1)
                    nc.scalar.activation(hss[:, 1, :], hss[:, 0, :], ACT.Sqrt).then_inc(sem("head_root"), 1)
                else:
                    if q == 1:
                        act.wait_ge(sem("bias_st"), 16)
                    dst = vC[:] if q == 1 else vAB[:, :, 4 * (q - 8):4 * (q - 8) + 4, :]
                    src = pair(2 * (q % 2)).rearrange("p k (h d) -> p k h d", d=HD)
                    nc.scalar.copy(dst, src).then_inc(sem("chunk_out"), 1)
            for n in range(48):
                q, s = divmod(4 * Q_GATES + n, 4)
                round_piece(q + 1, s)
                if s == 3:
                    c = q - Q_GATES
                    if c >= 1:
                        act.wait_ge(sem("gate_st"), 16 * c)
                    act.wait_ge(piece_used, 4 * q + 4)
                    nc.scalar.activation(gst[:], pair(2 * (q % 2)), ACT.Tanh, scale=0.5)\
                        .then_inc(sem("chunk_out"), 1)
                if n % 3 == 0:
                    h = n // 3
                    act.wait_ge(sem("att_m"), h + 1)
                    if h >= 1:
                        act.wait_ge(sem("att_t"), h)
                    for k in range(TOK):
                        nc.scalar.activation(probs[:, k, :], ps[:, 4, SEQ * k:SEQ * k + SEQ], ACT.Exp,
                                             bias=negm[:, k, h:h + 1], accum_out=lsum[:, k, h:h + 1])\
                            .then_inc(sem("att_e"), 1)
                if n == 19:
                    act.wait_ge(sem("cmb_d"), 1)
                    nc.scalar.activation(cmb[:, 1], cmb[:, 0], ACT.Exp).then_inc(sem("cmb_e"), 1)
            for f in range(3):
                fold_hi(FOLD_O + f, oTh, 4 * f)

            def load_gate(n):
                j, part = divmod(n, 3)
                act.dma_start(gl[:, n % 4].rearrange("p k n -> p (k n)"), gates_d[4 * part + j])\
                    .then_inc(sem(f"gl_in{n % 4}"), 16)

            act.wait_ge(sem("gate_st"), 16 * 12)
            act.wait_ge(sem("fold_tr"), FOLD_M)
            for n in range(3):
                load_gate(n)
            for n in range(12):
                q, s = divmod(4 * Q_BRANCH + n, 4)
                round_piece(q + 1, s)
                if n + 3 < 12:
                    if n >= 1:
                        act.wait_ge(sem("gated"), n)
                    load_gate(n + 3)
                if n % 3 == 1 and n >= 4:
                    fold_hi(FOLD_M + n // 3 - 1, hTh, 4 * (n // 3 - 1))
            nc.scalar.activation(cs[:], cs[:], ACT.Silu).then_inc(sem("cs_done"), 1)
            for n in range(16):
                q, s = divmod(4 * Q_WO + n, 4)
                if n < 15:
                    round_piece(q + 1, s)
                if n == 0:
                    fold_hi(FOLD_M + 3, hTh, 12)
                if n % 4 == 1 and n >= 4:
                    act.wait_ge(sem("wo_out"), n // 4)
                    squares(2, n // 4 - 1, x)
            act.wait_ge(sem("wo_out"), 4)
            squares(2, 3, x)
            norm(2, x, FOLD_FFN, hTh, (Q_FFN, 3))

            def silu(g):
                act.wait_ge(piece_used, 4 * Q_FFN + 4 if isinstance(g, int) else 12 * g + 4 * Q_FFN)
                if not isinstance(g, int):
                    act.wait_ge(sem("ffn_product"), g)
                nc.scalar.activation(gact[:], pair(0), ACT.Silu).then_inc(sem("silu"), 1)

            def gate_up_down(b, j):
                round_piece(3 * b + (Q_FFN + 2 + j // 4 + 1), j % 4)

            for j in range(8):
                q, s = divmod(4 * Q_FFN + j, 4)
                round_piece(q + 1, s)
                if j == 3:
                    silu(0)

            def ffn_hi(b):
                act.wait_ge(sem("ffn_tr"), b + 1)
                nc.scalar.copy(factTh[:], quarters(4)).then_inc(sem("ffn_hi"), 1)

            with act.Fori(0, FF_GROUPS - 1) as b:
                for j in range(12):
                    gate_up_down(b, j)
                    if j == 1:
                        ffn_hi(b)
                    if j == 3:
                        silu(b + 1)
            ffn_hi(FF_GROUPS - 1)
            for j in range(5):
                if j >= 1:
                    act.wait_ge(sem("x_sum"), 4 * (FF_GROUPS - 1) + j + 2)
                    squares(3, j - 1, x)
                if j < 3:
                    round_piece(Q_IN2, j)
            norm(3, x, FOLD_MIX2, hTh, (Q_IN2, 3))

            def exp2(h):
                act.wait_ge(sem("max2"), h + 1)
                if h >= 2:
                    act.wait_ge(sem("turned2"), h - 1)
                for k in range(TOK):
                    keys = P * (k + 1)
                    nc.scalar.activation(probs2[:, h % 2, k, 0:keys], ps[:, 6, SEQ * k:SEQ * k + keys], ACT.Exp,
                                         bias=negm[:, k, h:h + 1], accum_out=lsum[:, k, h:h + 1])\
                        .then_inc(sem("exp2"), 1)

            def attention_squares():
                act.wait_ge(sem("output2"), H2)
                for k in range(TOK):
                    nc.scalar.activation(probs2[:].rearrange("p a b n -> p (a b n)"),
                                         att2[:, k].rearrange("p h d -> p (h d)"), ACT.Square,
                                         accum_out=ssum[:, k:k + 1]).then_inc(sem("ssq2"), 1)
                    act.wait_ge(sem("ssq2"), k + 1)

            def attention_scaled():
                act.wait_ge(sem("ms2"), 1)
                nc.scalar.activation(rstd[:, 0, :], ssum[:], ACT.Sqrt).then_inc(sem("ms2_root"), 1)
                act.wait_ge(sem("rstd2"), 1)
                for k in range(TOK):
                    nc.scalar.activation(att2[:, k], att2[:, k], ACT.Copy, scale=rstd[:, 1, k:k + 1])\
                        .then_inc(sem("att2_s"), 1)

            def lru_gates(n):
                act.wait_ge(sem("lru_mm"), n + 1)
                nc.scalar.activation(uT[:, n, :], ps[:, 6 + n % 2, 0:SEQ], ACT.Sigmoid,
                                     bias=cols[:, C_BA + n:C_BA + n + 1]).then_inc(sem("r_out"), 1)
                if n >= 2:
                    act.wait_ge(sem("i_used"), n - 1)
                nc.scalar.activation(istage[:, n % 2, :], ps[:, 6 + n % 2, SEQ:2 * SEQ], ACT.Sigmoid,
                                     bias=cols[:, C_BX + n:C_BX + n + 1]).then_inc(sem("i_out"), 1)

            def decays(half):
                tiles = range(4 * half, 4 * half + 4)
                act.wait_ge(sem("sp_done"), 1)
                act.wait_ge(sem("conv"), 4 * half + 4)
                act.wait_ge(sem("r_out"), 4 * half + 4)
                for n in tiles:
                    nc.scalar.activation(dec[:, n, :], uT[:, n, :], ACT.Exp, scale=spn[:, 0, n:n + 1])\
                        .then_inc(sem("dec"), 1)
                for n in tiles:
                    nc.scalar.activation(uT[:, n, :], uT[:, n, :], ACT.Tanh, scale=spn[:, 1, n:n + 1])\
                        .then_inc(sem("tanh"), 1)

            def lru_gelu(n):
                act.wait_ge(sem("in_tr"), 7 + n)
                nc.scalar.activation(gyT[:, 4 * n:4 * n + 4, :], quarters(4), ACT.Gelu_apprx_tanh)\
                    .then_inc(sem("gy_T"), 1)

            for c in range(IN_CHUNKS):
                q = Q_IN2 + c
                for s in range(4):
                    i = 4 * (c - 3) + s
                    if (c, s) != (9, 3):
                        round_piece(q + 1, s)
                    if i in SCORES_AT:
                        exp2(SCORES_AT[i])
                    if (c, s) == (0, 1):
                        act.wait_ge(sem("wf_in"), 16)
                        nc.scalar.copy(wfh[:], wf[:]).then_inc(sem("wfh"), 1)
                    if (c, s) == (1, 3):
                        act.wait_ge(sem("lg_abs"), 1)
                        nc.scalar.activation(lgate[:, 1, :], lgate[:, 1, :], ACT.Exp, scale=-1.0)\
                            .then_inc(sem("lg_exp"), 1)
                    if (c, s) == (4, 1):
                        act.wait_ge(sem("lam_n"), 1)
                        nc.scalar.activation(lam[:, 1, :], lam[:, 0, :], ACT.Exp).then_inc(sem("lam_e"), 1)
                    if (c, s) == (7, 3):
                        attention_squares()
                    if (c, s) == (8, 0):
                        attention_scaled()
                    if c == 8:
                        lru_gates(2 * s)
                        lru_gates(2 * s + 1)
                        if s % 2:
                            decays(s // 2)
                    if (c, s) == (9, 0):
                        act.wait_ge(sem("tanh"), 8)
                        nc.scalar.activation(uT[:], uT[:], ACT.Sqrt).then_inc(sem("root2"), 1)
                    if (c, s) == (9, 1):
                        fold_hi(FOLD_ATT, attTh, 0)
                    if (c, s) == (9, 2):
                        fold_hi(FOLD_ATT + 1, attTh, 4)
                        lru_gelu(0)
                act.wait_ge(piece_used, 4 * q + 4)
                if c in TURNED:
                    n = TURNED.index(c)
                    if n >= 1:
                        act.wait_ge(sem("in_tr"), n)
                    if c == 9:
                        act.wait_ge(sem("fold_lo"), FOLD_LRU)
                    if c == 0:
                        act.wait_ge(sem("fold_lo"), FOLD_ATT)
                    nc.scalar.copy(stage[:], pair(2 * (c % 2))).then_inc(sem("in_out"), 1)
                else:
                    half = 0 if c == 2 else 512
                    nc.scalar.copy(v2[:, :, half:half + 512], pair(2 * (c % 2))).then_inc(sem("in_out"), 1)
            round_piece(Q_OUT2, 3)
            for n in range(16):
                q, s = divmod(4 * Q_OUT2 + n, 4)
                if n < 15:
                    round_piece(q + 1, s)
                if n == 0:
                    lru_gelu(1)
                if n == 2:
                    act.wait_ge(sem("lru_ms"), 1)
                    nc.scalar.activation(lrs[:, 0, :], lrs[:, 0, :], ACT.Sqrt).then_inc(sem("lru_root"), 1)
                    fold_hi(FOLD_LRU, hTh, 8)
                    fold_hi(FOLD_LRU + 1, hTh, 12)
                if n in (7, 9, 13):
                    c = (7, 9, 13).index(n)
                    act.wait_ge(sem("out2_sum"), c + 1)
                    squares(4, c, x)
            act.wait_ge(sem("out2_sum"), 4)
            squares(4, 3, x)
            norm(4, x, FOLD_PEER, hTh, (Q_PQ, 3))
            for c in range(4):
                q = Q_PQ + c
                for s in range(4):
                    round_piece(q + 1, s)
                act.wait_ge(piece_used, 4 * q + 4)
                if c >= 1:
                    act.wait_ge(sem("pq_tr"), c)
                else:
                    act.wait_ge(sem("fold_lo"), FOLD_PEER + 4)
                nc.scalar.copy(stage[:], pair(2 * (c % 2))).then_inc(sem("pq_out"), 1)

            def gelu(g, u, out=True):
                act.wait_ge(piece_used, 4 * g + 4 * (Q_PEER + 1))
                if not isinstance(g, int) or g > 0:
                    act.wait_ge(sem("hid_st"), 16 * g)
                nc.scalar.activation(gacc[:], pair(2 * u), ACT.Gelu_apprx_tanh).then_inc(sem("gelu"), 1)
                if out:
                    act.wait_ge(sem("gelu"), g + 1)
                    act.dma_start(hid_d[g], gacc[:].rearrange("p k n -> p (k n)")).then_inc(sem("hid_st"), 16)

            def early_group(g, u, mid):
                for s in range(4):
                    round_piece(g + (Q_PEER + 1), s)
                    mid(s)
                gelu(g, u)

            early_group(0, 0, lambda s: None)
            early_group(1, 1, lambda s: None)
            with act.Fori(1, EARLY_TOP // 2 - 1) as m:
                for u in range(2):
                    early_group(2 * m + u, u, lambda s: None)

            def choice_exp(s):
                if s == 1:
                    act.wait_ge(sem("wexp_in"), 1)
                    nc.scalar.activation(picks[:, :, 2], picks[:, :, 2], ACT.Exp).then_inc(sem("wexp"), 1)

            early_group(EARLY_TOP - 2, 0, lambda s: None)
            early_group(EARLY_TOP - 1, 1, choice_exp)

            def weights_out(i, v, first):
                act.wait_ge(sem("weights_mm"), 2 * i + (v + 1))
                if not first:
                    act.wait_ge(sem(f"w_st{v}"), 16 * i)
                nc.scalar.copy(wst[:, v].rearrange("p t b -> p (t b)"),
                               ps[:, 4 + 2 * v:6 + 2 * v, :].rearrange("p b n -> p (b n)")).then_inc(sem("weights_out"), 1)
                act.wait_ge(sem("weights_out"), 2 * i + (v + 1))
                rows = slice(16 * i + 8 * v, 16 * i + 8 * v + 8) if isinstance(i, int) else bass.ds(16 * i + 8 * v, 8)
                act.dma_start(w_d[rows].rearrange("t (a b) -> a t b", b=N_KEYS), wst[:, v]).then_inc(sem(f"w_st{v}"), 16)

            def weights_pair(i, first=False):
                for v in range(2):
                    weights_out(i, v, first)

            early_group(EARLY_TOP, 0, lambda s: weights_pair(s, s == 0))
            early_group(EARLY_TOP + 1, 1, lambda s: weights_pair(4 + s))
            early_group(EARLY_TOP + 2, 0, lambda s: weights_pair(8 + s))
            early_group(EARLY_TOP + 3, 1, lambda s: weights_pair(12 + s))

            def peer_hi(b, u):
                act.wait_ge(sem("peer_tr"), b + 1)
                nc.scalar.copy(pactTh[:, u], quarters(4)).then_inc(sem("peer_hi"), 1)

            for s in range(4):
                round_piece(Q_PEER + EARLY, s)
                if s == 2:
                    peer_hi(0, 0)
            gelu(EARLY - 1, 0, out=False)

            def down_group(b, u, turn=True):
                for j in range(4):
                    if j == 2 and turn:
                        act.wait_ge(piece_used, 4 * b + 4 * (Q_PEER + EARLY))
                        peer_hi(b + 1, 1 - u)
                    round_piece(b + (Q_PEER + EARLY + 1), j)

            with act.Fori(0, (EARLY - 1) // 2 - 1) as m:
                for u in range(2):
                    down_group(2 * m + u, u)
            down_group(EARLY - 3, 0)
            down_group(EARLY - 2, 1, turn=False)

            with act.Fori(EARLY - 1, PEER_GROUPS - 1) as b:
                for j in range(8):
                    round_piece(2 * b + (Q_PEER + 1 + j // 4 + 1), j % 4)
                    if j == 1:
                        peer_hi(b, 0)
                    if j == 3:
                        act.wait_ge(piece_used, 8 * b + (4 * Q_PEER + 8))
                        act.wait_ge(sem("peer_product"), b + 1)
                        nc.scalar.activation(gacc[:], pair(0), ACT.Gelu_apprx_tanh).then_inc(sem("gelu"), 1)
            peer_hi(PEER_GROUPS - 1, 0)
            for c in range(4):
                act.wait_ge(sem("x_ready"), c + 1)
                squares(5, c, x)
            act.wait_ge(sem("ms_done"), 6)
            nc.scalar.activation(rstd[:, 0, :], ssum[:], ACT.Sqrt).then_inc(sem("root_done"), 1)

        @block.vector
        def _(dve):
            seq = [0]

            def step(ins):
                seq[0] += 1
                ins.then_inc(sem("dve_seq"), 1)
                dve.wait_ge(sem("dve_seq"), seq[0])

            V = nc.vector

            def rest_piece(q, s):
                dve.wait_ge(hi_done, 4 * q + (s + 1))
                if not isinstance(q, int) or q >= 1:
                    dve.wait_ge(piece_used, 4 * q + (s - 3))
                V.tensor_tensor(lo[:, s, :], raw[:, s, :], hi[:, s, :].bitcast(F32), ALU.subtract).then_inc(lo_done, 1)

            def rest_quad(q):
                for s in range(4):
                    rest_piece(q, s)

            def fold_lo(f, dst, at0):
                dve.wait_ge(sem("fold_hi"), f + 1)
                V.tensor_tensor(dst[0][:, at0:at0 + 4, :], fold[:, f % 2], dst[1][:, at0:at0 + 4, :].bitcast(F32),
                                ALU.subtract).then_inc(sem("fold_lo"), 1)

            def fold_ready(f, turned):
                if turned is not None:
                    dve.wait_ge(sem("fold_tr"), turned)
                if f >= 2:
                    dve.wait_ge(sem("fold_hi"), f - 1)
                    dve.wait_ge(sem("fold_lo"), f - 1)

            def stats(u):
                dve.wait_ge(sem("sq_done"), 8 * u + 8)
                step(V.tensor_reduce(ssum[:], sq[:], AX.X, ALU.add))
                V.tensor_scalar(ssum[:], ssum[:], 1.0 / D, EPS, ALU.mult, ALU.add).then_inc(sem("ms_done"), 1)
                dve.wait_ge(sem("root_done"), u + 1)
                V.reciprocal(rstd[:, 1, :], rstd[:, 0, :]).then_inc(sem("rstd_done"), 1)

            def folds(u, f0, scale_at, shift, scale_tile=None, between=lambda g: None):
                src = cols if scale_tile is None else scale_tile
                th, tl = (memTh, memTl) if u == 0 else (hTh, hTl)
                for g in range(4):
                    f = f0 + g
                    turned = f + 1 if f < FOLD_LRU else f - 1
                    fold_ready(f, turned)
                    for k in range(4):
                        kt = 4 * g + k
                        col = src[:, scale_at + kt:scale_at + kt + 1]
                        if shift is None:
                            ins = V.tensor_scalar(fold[:, f % 2, k], quarters(fold_bank(f))[:, k], col, None, ALU.mult)
                        else:
                            ins = V.tensor_scalar(fold[:, f % 2, k], quarters(fold_bank(f))[:, k], col,
                                                  modT[:, shift, kt:kt + 1], ALU.mult, ALU.add)
                    ins.then_inc(sem("fold_t"), 1)
                    if g >= 1:
                        fold_lo(f - 1, (tl, th), 4 * g - 4)
                        between(g - 1)
                fold_lo(f0 + 3, (tl, th), 12)
                between(3)

            step(V.memset(ones[:], 1.0))
            stats(0)
            dve.wait_ge(sem("cols_in"), 16)
            folds(0, FOLD_MEM, C_GMEM, None)
            stats(1)
            dve.wait_ge(sem("const_in"), 16 * 10)
            dve.wait_ge(sem("bias_mm"), 1)
            V.tensor_tensor(bvec[:], ps[0:6, 7, :], dmask[:], ALU.add).then_inc(sem("bvec"), 1)
            dve.wait_ge(lo_done, 4)
            for s in range(3):
                rest_piece(1, s)
            folds(1, FOLD_X, C_GMIX, None, between=lambda g: rest_piece(1, 3) if g == 0 else None)

            def head_norm(q):
                n = head_quads.index(q)
                dve.wait_ge(sem("chunk_out"), q + 1)
                h8 = stage[:].rearrange("p k (h d) -> p (k h) d", d=HD)
                s8 = stage2[:].rearrange("p k (h d) -> p (k h) d", d=HD)
                step(V.tensor_tensor(s8, h8, h8, ALU.mult))
                step(V.tensor_reduce(hss[:, 0, :], s8, AX.X, ALU.add))
                V.tensor_scalar(hss[:, 0, :], hss[:, 0, :], 1.0 / HD, EPS, ALU.mult, ALU.add)\
                    .then_inc(sem("head_ms"), 1)
                dve.wait_ge(sem("head_root"), n + 1)
                step(V.reciprocal(hss[:, 2, :], hss[:, 1, :]))
                rs = hss[:, 2, :].rearrange("p (h o) -> p h o", o=1).to_broadcast([P, 8, HD])
                if q < 6:
                    V.tensor_tensor(h8, h8, rs, ALU.mult).then_inc(sem("head_n"), 1)
                    return
                step(V.tensor_tensor(h8, h8, rs, ALU.mult))
                for k in range(TOK):
                    hk = stage[:, k, :].rearrange("p (h d) -> p h d", d=HD)
                    sk = stage2[:, k, :].rearrange("p (h d) -> p h d", d=HD)
                    runs = [(0, 4, 0)] if q == 6 else [(0, 2, 0), (2, 4, 1)]
                    for a, b, g in runs:
                        gain = gb[:, g, :].rearrange("p (o d) -> p o d", o=1).to_broadcast([P, b - a, HD])
                        step(V.tensor_tensor(hk[:, a:b], hk[:, a:b], gain, ALU.mult))
                    sin = rope[:, 1, k, :].rearrange("p (o d e) -> p o d e", o=1, e=2)
                    cos = rope[:, 0, k, :].rearrange("p (o d) -> p o d", o=1).to_broadcast([P, 4, HD])
                    h4 = stage[:, k, :].rearrange("p (h d e) -> p h d e", d=HD // 2, e=2)
                    s4 = stage2[:, k, :].rearrange("p (h d e) -> p h d e", d=HD // 2, e=2)
                    for e in range(2):
                        step(V.tensor_tensor(s4[:, :, :, e], h4[:, :, :, 1 - e],
                                             sin[:, :, :, e].to_broadcast([P, 4, HD // 2]), ALU.mult))
                    step(V.tensor_tensor(hk, hk, cos, ALU.mult))
                    ins = V.tensor_tensor(hk, hk, sk, ALU.add)
                ins.then_inc(sem("head_n"), 1)

            def head_out(q):
                n = head_quads.index(q)
                if q == 0:
                    dve.wait_ge(sem("bias_st"), 16)
                dve.wait_ge(sem("head_tr"), n + 1)
                for k in range(4):
                    src = quarters(4)[:, k]
                    if q == 0:
                        ins = V.tensor_scalar(kcT[:, k], src, cols[:, C_HEAD + 16 + k:C_HEAD + 17 + k], None, ALU.mult)
                        continue
                    h = 4 * (q - 2) + k
                    if h < 16:
                        scale = 1.0 if 6 <= h < 12 else SCALE
                        ins = V.tensor_scalar(qkT[:, h], src, cols[:, C_HEAD + h:C_HEAD + h + 1], scale,
                                              ALU.mult, ALU.mult)
                    else:
                        ins = V.tensor_scalar(qkT[:, h], src, SCALE if h < 22 else 1.0, None, ALU.mult)
                ins.then_inc(sem("head_T"), 1)

            for q in range(Q_GATES):
                if q >= 1:
                    rest_quad(q + 1)
                if q - 1 in head_quads:
                    head_out(q - 1)
                if q in head_quads:
                    head_norm(q)

            nA = negm[:, :, 0:6].rearrange("p k (g j) -> p k g j", j=2)
            lA = lsum[:, :, 0:6].rearrange("p k (g j) -> p k g j", j=2)
            d4 = cmb[:, 0].rearrange("p k (g j) -> p k g j", j=2)
            e4 = cmb[:, 1].rearrange("p k (g j) -> p k g j", j=2)

            def group_maxima():
                step(V.tensor_tensor(cmx[:, 0], nA[:, :, 0], nA[:, :, 1], ALU.min))
                step(V.tensor_tensor(cmx[:, 0], cmx[:, 0], nA[:, :, 2], ALU.min))
                for g in range(3):
                    ins = V.tensor_tensor(d4[:, :, g], cmx[:, 0], nA[:, :, g], ALU.subtract)
                ins.then_inc(sem("cmb_d"), 1)

            def join_groups():
                dve.wait_ge(sem("cmb_e"), 1)
                step(V.tensor_tensor(d4[:], e4, lA, ALU.mult))
                step(V.tensor_tensor(cmx[:, 0], d4[:, :, 0], d4[:, :, 1], ALU.add))
                step(V.tensor_tensor(cmx[:, 0], cmx[:, 0], d4[:, :, 2], ALU.add))
                step(V.reciprocal(cmx[:, 1], cmx[:, 0]))
                fA = fac[:, :, 0:6].rearrange("p k (g j) -> p k g j", j=2)
                for g in range(3):
                    ins = V.tensor_tensor(fA[:, :, g], e4[:, :, g], cmx[:, 1], ALU.mult)
                step(ins)
                for k in range(TOK):
                    f6 = fac[:, k, 0:6].rearrange("p (h o) -> p h o", o=1).to_broadcast([P, 6, HD])
                    ins = V.tensor_tensor(obuf[:, k, 0:6], obuf[:, k, 0:6], f6, ALU.mult)
                step(ins)
                step(V.tensor_tensor(obuf[:, :, 4:6, :], obuf[:, :, 4:6, :], obuf[:, :, 2:4, :], ALU.add))
                V.tensor_tensor(obuf[:, :, 4:6, :], obuf[:, :, 4:6, :], obuf[:, :, 0:2, :], ALU.add)\
                    .then_inc(sem("o_ready"), 1)

            for n in range(48):
                q, s = divmod(4 * Q_GATES + n, 4)
                rest_piece(q + 1, s)
                h, part = divmod(n, 3)
                if part == 0:
                    dve.wait_ge(sem("att_s"), h + 1)
                    V.tensor_reduce(negm[:, :, h:h + 1], ps[:, 4, :].rearrange("p (k n) -> p k n", n=SEQ), AX.X,
                                    ALU.max, negate=True).then_inc(sem("att_m"), 1)
                elif part == 1:
                    dve.wait_ge(sem("att_t"), h + 1)
                    V.tensor_copy(probsT[:].rearrange("p k n -> p (k n)"), ps[:, 5, :]).then_inc(sem("att_p"), 1)
                else:
                    dve.wait_ge(sem("att_v"), h + 1)
                    if h < A_HEADS:
                        V.tensor_copy(obuf[:, :, h, :], ps[:, 6, 0:SEQ].rearrange("p (k d) -> p k d", d=HD))\
                            .then_inc(sem("att_o"), 1)
                    else:
                        step(V.reciprocal(fac[:, :, h:h + 1], lsum[:, :, h:h + 1]))
                        for k in range(TOK):
                            ins = V.tensor_scalar(obuf[:, k, h, :], ps[:, 6, HD * k:HD * k + HD], fac[:, k, h:h + 1],
                                                  None, ALU.mult)
                        ins.then_inc(sem("att_o"), 1)
                if n == 18:
                    group_maxima()
                if n == 20:
                    join_groups()
            for f in range(FOLD_O, FOLD_M):
                fold_ready(f, f + 1)
                V.tensor_copy(fold[:, f % 2], quarters(fold_bank(f))).then_inc(sem("fold_t"), 1)
                fold_lo(f, (oTl, oTh), 4 * (f - FOLD_O))

            def merge(j, part):
                n = 3 * j + part
                dve.wait_ge(sem(f"gl_in{n % 4}"), 16 * (n // 4 + 1))
                dve.wait_ge(piece_used, 4 * Q_BRANCH + n + 1)
                to, banks = (mt0, mt1, mt1)[part], (0, 2, 6)[part]
                V.scalar_tensor_tensor(to[:], gl[:, n % 4], 1.0, pair(banks), ALU.add, ALU.mult)\
                    .then_inc(sem("gated"), 1)
                dve.wait_ge(sem("gated"), n + 1)
                if part == 1:
                    step(V.tensor_tensor(mt0[:], mt0[:], mt1[:], ALU.add))
                if part == 2:
                    V.tensor_tensor(merged[:, :, 512 * j:512 * j + 512], mt0[:], mt1[:], ALU.add)\
                        .then_inc(sem("merge"), 1)
                    dve.wait_ge(sem("merge"), j + 1)

            def fold_merged(j):
                f = FOLD_M + j
                fold_ready(f, f + 1)
                V.tensor_scalar(fold[:, f % 2], quarters(fold_bank(f)), 0.5, None, ALU.mult).then_inc(sem("fold_t"), 1)
                fold_lo(f, (hTl, hTh), 4 * j)

            for n in range(12):
                merge(n // 3, n % 3)
                if n % 3 == 1 and n >= 4:
                    fold_merged(n // 3 - 1)

            def ada_piece(a, j, first):
                dve.wait_ge(ADA_IN[j % 2], 64 * a + 16 * (j // 2 + 1))
                for k in range(2):
                    m = 2 * j + k
                    col = cs[:, m:m + 1]
                    src = adaraw[:, j % 2, k, :]
                    if not (first and m == 0):
                        dve.wait_ge(sem("ada_sum"), 16 * a + m)
                    if m == 0:
                        ins = V.tensor_scalar(adaacc[:], src, col, None, ALU.mult)
                    else:
                        ins = V.scalar_tensor_tensor(adaacc[:], src, col, adaacc[:], ALU.mult, ALU.add)
                    ins.then_inc(sem("ada_sum"), 1)
                dve.wait_ge(sem("ada_sum"), 16 * a + (2 * j + 2))
                dve.sem_inc(sem("ada_used"), 1)

            def ada_row(a, b):
                dve.wait_ge(sem("ada_mm"), a + 1)
                dve.wait_ge(sem("bada_in"), 16 * a + 16)
                for k in range(2):
                    V.tensor_tensor(modrow[0:1, 512 * k:512 * k + 512], ps[0:1, b + k, :],
                                    modrow[0:1, 512 * k:512 * k + 512], ALU.add).then_inc(sem("modrow"), 1)

            dve.wait_ge(sem("cs_done"), 1)
            dve.wait_ge(lo_done, 4 * (Q_WO + 1))
            for n in range(16):
                q, s = divmod(4 * Q_WO + n, 4)
                if s == 3:
                    dve.wait_ge(sem("x_back"), 16)
                    dve.wait_ge(piece_used, 4 * q + 4)
                    c = q - Q_WO
                    xc = x[:, :, 512 * c:512 * c + 512]
                    V.tensor_tensor(xc, xc, pair(2 * (c % 2)), ALU.add).then_inc(sem("wo_out"), 1)
                if n < 15:
                    rest_piece(q + 1, s)
                if n == 0:
                    fold_merged(3)
                if n % 2 == 0:
                    ada_piece(0, n // 2, True)
            stats(2)
            ada_row(0, 6)
            folds(2, FOLD_FFN, C_GFFN, None, between=lambda g: rest_piece(Q_FFN, 3) if g == 0 else None)

            def ffn_mul(g):
                dve.wait_ge(sem("silu"), g + 1)
                dve.wait_ge(piece_used, 4 * Q_FFN + 8 if isinstance(g, int) and g == 0 else 12 * g + (4 * Q_FFN + 4))
                V.tensor_tensor(fact[:], gact[:], pair(2), ALU.mult).then_inc(sem("ffn_product"), 1)

            def ffn_lo(b):
                dve.wait_ge(sem("ffn_hi"), b + 1)
                V.tensor_tensor(factTl[:], quarters(4), factTh[:].bitcast(F32), ALU.subtract).then_inc(sem("ffn_lo"), 1)

            def ffn_down(b, s, used):
                dve.wait_ge(piece_used, used)
                if not isinstance(b, int):
                    dve.wait_ge(sem("x_sum"), 4 * b + (s + 2))
                xc = x[:, :, 512 * s:512 * s + 512]
                V.tensor_tensor(xc, xc, pair(6 * (s % 2)), ALU.add).then_inc(sem("x_sum"), 1)

            dve.sem_inc(sem("x_sum"), 2)
            for j in range(8):
                q, s = divmod(4 * Q_FFN + j, 4)
                rest_piece(q + 1, s)
                ada_piece(1, j, False)
            ffn_mul(0)
            with dve.Fori(0, FF_GROUPS - 1) as b:
                for j in range(12):
                    if j >= 8:
                        ffn_down(b, j - 8, 12 * b + (4 * Q_FFN + 8 + j + 1))
                    rest_piece(3 * b + (Q_FFN + 3 + j // 4), j % 4)
                    if j == 1:
                        ffn_lo(b)
                    if j == 7:
                        ffn_mul(b + 1)
                    if j == 0:
                        ada_row(b + 1, 4)
                    if j < 8:
                        ada_piece(b + 2, j, False)
            ffn_lo(FF_GROUPS - 1)
            for j in range(4):
                dve.wait_ge(sem("x_sum"), 4 * (FF_GROUPS - 1) + j + 2)
                ffn_down(FF_GROUPS - 1, j, 4 * Q_IN2 - 3 + j)
                if j < 3:
                    rest_piece(Q_IN2, j)
                if j == 0:
                    ada_row(ADA_SPLITS - 1, 4)
            stats(3)
            dve.wait_ge(sem("modT_in"), 64)
            step(V.scalar_tensor_tensor(gmod[:], modT[:, 1, :], 1.0, cols[:, C_GMIX2:C_GMIX2 + 16], ALU.add, ALU.mult))
            folds(3, FOLD_MIX2, 0, 0, gmod, between=lambda g: rest_piece(Q_IN2, 3) if g == 0 else None)
            def log1p(out, e, z, z2):
                step(V.tensor_scalar(z2, e, 2.0, None, ALU.add))
                step(V.reciprocal(z2, z2))
                step(V.tensor_tensor(z, e, z2, ALU.mult))
                step(V.tensor_tensor(z2, z, z, ALU.mult))
                step(V.tensor_scalar(out, z2, 2.0 / 17, 2.0 / 15, ALU.mult, ALU.add))
                for k in (13, 11, 9, 7, 5, 3, 1):
                    step(V.tensor_tensor(out, out, z2, ALU.mult))
                    step(V.tensor_scalar(out, out, 2.0 / k, None, ALU.add))
                step(V.tensor_tensor(out, out, z, ALU.mult))

            def softplus_in():
                step(V.tensor_scalar(lam[:, 0, :], cols[:, C_LAM:C_LAM + 8], -1.0, None, ALU.mult))
                V.tensor_tensor(lam[:, 0, :], lam[:, 0, :], cols[:, C_LAM:C_LAM + 8], ALU.min).then_inc(sem("lam_n"), 1)

            def softplus_out():
                dve.wait_ge(sem("lam_e"), 1)
                log1p(lam[:, 2, :], lam[:, 1, :], lam[:, 0, :], lam[:, 3, :])
                step(V.tensor_scalar(lam[:, 0, :], cols[:, C_LAM:C_LAM + 8], -1.0, 0.0, ALU.mult, ALU.max))
                step(V.tensor_tensor(lam[:, 0, :], lam[:, 0, :], lam[:, 2, :], ALU.add))
                V.tensor_scalar(spn[:, 0, :], lam[:, 0, :], -8.0, None, ALU.mult)
                V.tensor_scalar(spn[:, 1, :], lam[:, 0, :], 4.0, None, ALU.mult).then_inc(sem("sp_done"), 1)

            def convolve(half):
                for j in range(CONV):
                    for n in range(4 * half, 4 * half + 4):
                        win = lxT[:, n, j:j + SEQ]
                        w = cols[:, C_CONVW + 8 * j + n:C_CONVW + 8 * j + n + 1]
                        if j == 0:
                            ins = V.tensor_scalar(bx[:, n], win, w, cols[:, C_CONVB + n:C_CONVB + n + 1],
                                                  ALU.mult, ALU.add)
                        else:
                            dve.wait_ge(sem("tap"), 12 * half + 4 * (j - 1) + n % 4 + 1)
                            ins = V.scalar_tensor_tensor(bx[:, n], win, w, bx[:, n], ALU.mult, ALU.add)
                        ins.then_inc(sem("tap") if j < CONV - 1 else sem("conv"), 1)

            def forget_gates():
                L = [lgate[:, r, :] for r in range(4)]
                dve.wait_ge(sem("f_mm"), 1)
                step(V.tensor_scalar(L[0], ps[0:8, 7, 0:SEQ], cols[0:8, C_BF:C_BF + 1], None, ALU.add))
                step(V.tensor_scalar(L[1], L[0], -1.0, None, ALU.mult))
                V.tensor_tensor(L[1], L[1], L[0], ALU.max).then_inc(sem("lg_abs"), 1)
                dve.wait_ge(sem("lg_exp"), 1)
                log1p(L[1], L[1], L[2], L[3])
                step(V.tensor_scalar(L[0], L[0], 0.0, None, ALU.min))
                step(V.tensor_tensor(L[0], L[0], L[1], ALU.subtract))
                step(V.memset(L[3], 0.0))
                step(V.tensor_tensor_scan(L[1], L[0], L[3], 0.0, ALU.add, ALU.add))
                V.tensor_scalar(L[2], L[1], -1.0, None, ALU.mult).then_inc(sem("cum"), 1)

            def fold_attention(g):
                f = FOLD_ATT + g
                fold_ready(f, f + 1)
                for k in range(4):
                    col = cols[:, C_GATT + 4 * g + k:C_GATT + 4 * g + k + 1]
                    ins = V.tensor_scalar(fold[:, f % 2, k], quarters(fold_bank(f))[:, k], col, None, ALU.mult)
                ins.then_inc(sem("fold_t"), 1)
                fold_lo(f, (attTl, attTh), 4 * g)

            for c in range(IN_CHUNKS):
                for s in range(4):
                    i = 4 * (c - 3) + s
                    if (c, s) != (9, 3):
                        rest_piece(Q_IN2 + c + 1, s)
                    if i in OUTPUT_AT:
                        h = OUTPUT_AT[i]
                        dve.wait_ge(sem("values2"), h + 1)
                        step(V.reciprocal(fac[:, :, h:h + 1], lsum[:, :, h:h + 1]))
                        for k in range(TOK):
                            ins = V.tensor_scalar(att2[:, k, h, :], ps[:, 7, HD * k:HD * k + HD], fac[:, k, h:h + 1],
                                                  None, ALU.mult)
                        ins.then_inc(sem("output2"), 1)
                    if i in TURN_AT:
                        h = TURN_AT[i]
                        dve.wait_ge(sem("turned2"), h + 1)
                        V.tensor_copy(probsT2[:, h % 2, 0], ps[:, 7, 0:SEQ])
                        V.tensor_copy(probsT2[:, h % 2, 1, P:SEQ], ps[:, 7, SEQ + P:2 * SEQ]).then_inc(sem("probs2"), 1)
                    if i in SCORES_AT:
                        h = SCORES_AT[i]
                        dve.wait_ge(sem("scores2"), h + 1)
                        for k in range(TOK):
                            ins = V.tensor_reduce(negm[:, k, h:h + 1], ps[:, 6, SEQ * k:SEQ * k + P * (k + 1)], AX.X,
                                                  ALU.max, negate=True)
                        ins.then_inc(sem("max2"), 1)
                    if (c, s) in ((1, 0), (2, 0), (4, 0), (5, 0)):
                        n = TURNED.index(c - 1)
                        row = (0, 8, 4, 12)[n]
                        dve.wait_ge(sem("in_tr"), n + 1)
                        V.tensor_scalar(qkT2[:, row:row + 4, :], quarters(4), SCALE if n % 2 == 0 else 1.0, None,
                                        ALU.mult).then_inc(sem("qk_T"), 1)
                    if (c, s) == (0, 2):
                        dve.wait_ge(sem("wfh"), 1)
                        V.tensor_tensor(wfl[:], wf[:], wfh[:].bitcast(F32), ALU.subtract).then_inc(sem("wfl"), 1)
                    if (c, s) == (1, 3):
                        forget_gates()
                    if (c, s) == (3, 3):
                        softplus_in()
                    if (c, s) == (4, 3):
                        softplus_out()
                    if (c, s) == (6, 3):
                        dve.wait_ge(sem("fold_tr"), FOLD_ATT)
                        step(V.memset(lxT[:, :, 0:3], 0.0))
                    if (c, s) == (7, 3):
                        dve.wait_ge(sem("ssq2"), 2)
                        V.tensor_scalar(ssum[:], ssum[:], 1.0 / LRU, EPS, ALU.mult, ALU.add).then_inc(sem("ms2"), 1)
                    if (c, s) == (8, 0):
                        dve.wait_ge(sem("ms2_root"), 1)
                        V.reciprocal(rstd[:, 1, :], rstd[:, 0, :]).then_inc(sem("rstd2"), 1)
                    if c in (7, 8) and s == 0:
                        n = c - 7
                        dve.wait_ge(sem("in_tr"), 5 + n)
                        V.tensor_copy(lxT[:, 4 * n:4 * n + 4, 3:3 + SEQ], quarters(4)).then_inc(sem("lx_T"), 1)
                        dve.wait_ge(sem("lx_T"), n + 1)
                        dve.wait_ge(sem("x_st"), 16)
                        convolve(n)
                    if c == 8:
                        for n in (2 * s, 2 * s + 1):
                            dve.wait_ge(sem("i_out"), n + 1)
                            V.tensor_tensor(bx[:, n], bx[:, n], istage[:, n % 2], ALU.mult).then_inc(sem("i_used"), 1)
                    if (c, s) == (9, 0):
                        dve.wait_ge(sem("dec"), 8)
                        dve.wait_ge(sem("i_used"), 8)
                        step(V.scalar_tensor_tensor(bx[:], dec[:], 1.0, bx[:], ALU.add, ALU.mult))
                    if (c, s) == (9, 1):
                        fold_attention(0)
                        dve.wait_ge(sem("root2"), 1)
                        step(V.tensor_tensor(bx[:], bx[:], uT[:], ALU.mult))
                    if (c, s) == (9, 2):
                        fold_attention(1)
                        for n in range(8):
                            V.tensor_tensor_scan(uT[:, n], dec[:, n], bx[:, n], 0.0, ALU.mult, ALU.add)\
                                .then_inc(sem("scan"), 1)
                        dve.wait_ge(sem("scan"), 8)
                    if (c, s) == (9, 3):
                        rest_piece(Q_OUT2, 3)

            def gated_output(n):
                half = slice(4 * n, 4 * n + 4)
                dve.wait_ge(sem("gy_T"), n + 1)
                step(V.tensor_tensor(gyT[:, half], gyT[:, half], uT[:, half], ALU.mult))
                V.tensor_tensor(lsq[:, half], gyT[:, half], gyT[:, half], ALU.mult).then_inc(sem("lsq"), 1)

            gated_output(0)
            for n in range(16):
                q, s = divmod(4 * Q_OUT2 + n, 4)
                if n in OUT_DONE:
                    c = OUT_DONE[n]
                    if c == 0:
                        dve.wait_ge(sem("ga1_in"), 16)
                        dve.wait_ge(sem("x_back"), 32)
                    dve.wait_ge(piece_used, 4 * Q_OUT2 + n + 1)
                    cut = slice(512 * c, 512 * c + 512)
                    gain = ga1[:, cut].rearrange("p (o n) -> p o n", o=1).to_broadcast([P, TOK, 512])
                    V.tensor_tensor(mt2[:], pair(2 * (c % 2)), gain, ALU.mult).then_inc(sem("out2"), 1)
                    dve.wait_ge(sem("out2"), c + 1)
                    V.tensor_tensor(x[:, :, cut], x[:, :, cut], mt2[:], ALU.add).then_inc(sem("out2_sum"), 1)
                    dve.wait_ge(sem("out2_sum"), c + 1)
                if n < 15:
                    rest_piece(q + 1, s)
                if n == 0:
                    gated_output(1)
                if n == 2:
                    dve.wait_ge(sem("lsum_mm"), 1)
                    V.tensor_scalar(lrs[:, 0, :], ps[:, 4, 0:SEQ], 1.0 / LRU, EPS, ALU.mult, ALU.add)\
                        .then_inc(sem("lru_ms"), 1)
                    dve.wait_ge(sem("lru_root"), 1)
                    step(V.reciprocal(lrs[:, 1, :], lrs[:, 0, :]))
                for g in range(2 if n == 2 else 0):
                    f = FOLD_LRU + g
                    fold_ready(f, None)
                    for k in range(4):
                        m = 4 * g + k
                        ins = V.scalar_tensor_tensor(fold[:, f % 2, k], gyT[:, m], cols[:, C_GLRU + m:C_GLRU + m + 1],
                                                     lrs[:, 1, :], ALU.mult, ALU.mult)
                    ins.then_inc(sem("fold_t"), 1)
                    fold_lo(f, (hTl, hTh), 8 + 4 * g)
            stats(4)
            step(V.scalar_tensor_tensor(gmod[:], modT[:, 3, :], 1.0, cols[:, C_GFFN2:C_GFFN2 + 16], ALU.add, ALU.mult))
            folds(4, FOLD_PEER, 0, 2, gmod, between=lambda g: rest_piece(Q_PQ, 3) if g == 0 else None)

            def pq_turned(c):
                dve.wait_ge(sem("pq_tr"), c + 1)
                V.tensor_copy(pqT[:, 4 * c:4 * c + 4, :], quarters(4)).then_inc(sem("pq_T"), 1)

            def scores_out(c):
                dve.wait_ge(sem("key_scores"), c + 1)
                if c == 0:
                    dve.wait_ge(sem("fold_tr"), FOLD_PEER + 4 - 2)
                V.tensor_copy(sc[:, :, 4 * c:4 * c + 4, :].rearrange("p k h n -> p k (h n)"), pair(6))\
                    .then_inc(sem("sc_out"), 1)

            for c in range(4):
                rest_quad(Q_PQ + c + 1)
                if c >= 1:
                    pq_turned(c - 1)
                if c >= 2:
                    scores_out(c - 2)
            pq_turned(3)
            scores_out(2)
            scores_out(3)
            dve.wait_ge(sem("sc_out"), 4)

            def top16(vals, idx, src, tmp, rows):
                for r in range(rows):
                    ins = V.max(vals[:, r, 0:8], src[:, r])
                step(ins)
                for r in range(rows):
                    V.max_index(idx[:, r, 0:8], vals[:, r, 0:8], src[:, r])
                for r in range(rows):
                    ins = V.match_replace(tmp[:, r], vals[:, r, 0:8], src[:, r], -3e38)
                step(ins)
                for r in range(rows):
                    ins = V.max(vals[:, r, 8:16], tmp[:, r])
                step(ins)
                for r in range(rows):
                    ins = V.max_index(idx[:, r, 8:16], vals[:, r, 8:16], tmp[:, r])
                step(ins)

            for k in range(TOK):
                top16(top[:, k], topi[:, k], sc[:, k], work[:].rearrange("p a (b n) -> p (a b) n", n=N_KEYS), 16)
            step(V.tensor_copy(topf[:].rearrange("p k h n -> p (k h n)"), topi[:].rearrange("p k h n -> p (k h n)")))
            for k in range(TOK):
                pairs = top[:, k].rearrange("p (h e) n -> p h e n", e=2)
                first = pairs[:, :, 0].rearrange("p h (n o) -> p h n o", o=1).to_broadcast([P, 8, TOPK, TOPK])
                second = pairs[:, :, 1].rearrange("p h (o n) -> p h o n", o=1).to_broadcast([P, 8, TOPK, TOPK])
                step(V.tensor_tensor(cand[:].rearrange("p h (a b) -> p h a b", b=TOPK), first, second, ALU.add))
                top16(best[:, k], besti[:, k], cand, work, 8)
                bi = besti[:, k]
                V.tensor_scalar(divi[:, 0], bi, 4, None, ALU.logical_shift_right)
                step(V.tensor_scalar(divi[:, 1], bi, 15, None, ALU.bitwise_and))
                step(V.tensor_copy(divf[:].rearrange("p e h n -> p (e h n)"), divi[:].rearrange("p e h n -> p (e h n)")))
                for e in range(2):
                    w4 = work[:].rearrange("p h (a b) -> p h a b", b=TOPK)
                    v4 = work2[:].rearrange("p h (a b) -> p h a b", b=TOPK)
                    place = iota[:, 0:16].rearrange("p (o q n) -> p o q n", o=1, q=1).to_broadcast([P, 8, TOPK, TOPK])
                    want = divf[:, e].rearrange("p h (n o) -> p h n o", o=1).to_broadcast([P, 8, TOPK, TOPK])
                    have = topf[:, k].rearrange("p (h e) n -> p h e n", e=2)[:, :, e]\
                        .rearrange("p h (o n) -> p h o n", o=1).to_broadcast([P, 8, TOPK, TOPK])
                    step(V.tensor_tensor(w4, place, want, ALU.is_equal))
                    step(V.tensor_tensor(v4, w4, have, ALU.mult))
                    step(V.tensor_reduce(picks[:, k, e], v4, AX.X, ALU.add))
                lead = best[:, k, :, 0:1].to_broadcast([P, 8, TOPK])
                ins = V.tensor_tensor(picks[:, k, 2], best[:, k], lead, ALU.subtract)
            ins.then_inc(sem("wexp_in"), 1)
            dve.wait_ge(sem("wexp"), 1)
            for k in range(TOK):
                ins = V.tensor_reduce(wsm[:, k, :, 0:1], picks[:, k, 2], AX.X, ALU.add)
            step(ins)
            step(V.reciprocal(wsm[:, :, :, 1:2], wsm[:, :, :, 0:1]))
            for k in range(TOK):
                ins = V.tensor_tensor(picks[:, k, 2], picks[:, k, 2], wsm[:, k, :, 1:2].to_broadcast([P, 8, TOPK]),
                                      ALU.mult)
            ins.then_inc(sem("picks"), 1)
            dve.wait_ge(sem("picks_tr"), 1)
            V.tensor_copy(picksT[:].rearrange("p a t -> p (a t)"),
                          ps[:, 6:8, :].rearrange("p b n -> p (b n)")[:, 0:3 * SEQ]).then_inc(sem("picksT"), 1)
            dve.wait_ge(sem("picksT"), 1)

            def one_hots(i, v, first):
                if not first:
                    dve.wait_ge(sem("weights_mm"), 2 * i + (v - 1))
                tok = slice(16 * i + 8 * v, 16 * i + 8 * v + 8) if isinstance(i, int) else bass.ds(16 * i + 8 * v, 8)
                row = iota[:].rearrange("p (o b) -> p o b", o=1).to_broadcast([P, 8, P])
                for e in range(2):
                    key = picksT[:, e, tok].rearrange("p (t o) -> p t o", o=1).to_broadcast([P, 8, P])
                    ins = V.tensor_tensor(oh[:, v, e], row, key, ALU.is_equal)
                ins.then_inc(sem("one_hots_raw"), 1)
                dve.wait_ge(sem("one_hots_raw"), 2 * i + (v + 1))
                weight = picksT[:, 2, tok].rearrange("p (t o) -> p t o", o=1).to_broadcast([P, 8, P])
                V.tensor_tensor(oh[:, v, 1], oh[:, v, 1], weight, ALU.mult).then_inc(sem("one_hots"), 1)

            one_hots(0, 0, True)
            one_hots(0, 1, True)
            with dve.Fori(1, SEQ // 16) as i:
                for v in range(2):
                    one_hots(i, v, False)

            def peer_mul(g, u, hidden, used):
                dve.wait_ge(sem(f"wc_in{u}"), used)
                if not isinstance(g, int) or g > 0:
                    dve.wait_ge(sem("peer_tr"), g)
                V.tensor_tensor(pact[:], hidden, wc[:, u], ALU.mult).then_inc(sem("peer_product"), 1)

            def early_mul(g, u, m):
                dve.wait_ge(sem(f"hid_in{u}"), 16 * m + 16)
                peer_mul(g, u, hid[:, u], 16 * m + 16)

            def peer_lo(b, u):
                dve.wait_ge(sem("peer_hi"), b + 1)
                V.tensor_tensor(pactTl[:, u], quarters(4), pactTh[:, u].bitcast(F32), ALU.subtract)\
                    .then_inc(sem("peer_lo"), 1)

            def peer_down(b, s, used):
                dve.wait_ge(piece_used, used)
                dve.wait_ge(sem("y_sum"), 4 * b + (s + 2))
                yc = y[:, :, 512 * s:512 * s + 512]
                V.tensor_tensor(yc, yc, pair(6 if s % 2 == 0 else 2), ALU.add).then_inc(sem("y_sum"), 1)

            dve.wait_ge(sem("sc_out"), 4)
            V.memset(y[:], 0.0).then_inc(sem("y_sum"), 2)
            dve.wait_ge(sem("weights_mm"), SEQ // 8)
            dve.wait_ge(lo_done, 4 * (Q_PEER + EARLY))
            for j in range(4):
                rest_piece(Q_PEER + EARLY, j)
                if j == 1:
                    early_mul(0, 0, 0)
                if j == 2:
                    peer_lo(0, 0)
                    early_mul(1, 1, 0)

            def down_group(b, u, m):
                for j in range(4):
                    if j == 2:
                        peer_lo(b + 1, 1 - u)
                    rest_piece(b + (Q_PEER + EARLY + 1), j)
                    peer_down(b, j, 4 * b + (4 * (Q_PEER + EARLY) + j + 1))
                    if j == 2:
                        early_mul(b + 2, u, m + 1)

            with dve.Fori(0, (EARLY - 1) // 2 - 1) as m:
                for u in range(2):
                    down_group(2 * m + u, u, m)
            for b in (EARLY - 3, EARLY - 2):
                for j in range(4):
                    if j == 2 and b == EARLY - 3:
                        peer_lo(b + 1, 1)
                    rest_piece(b + (Q_PEER + EARLY + 1), j)
                    peer_down(b, j, 4 * b + (4 * (Q_PEER + EARLY) + j + 1))
                    if j == 2 and b == EARLY - 3:
                        dve.wait_ge(sem("gelu"), EARLY)
                        peer_mul(EARLY - 1, 0, gacc[:], 16 * ((EARLY + 1) // 2))
            with dve.Fori(EARLY - 1, PEER_GROUPS - 1) as b:
                for j in range(8):
                    if j >= 4:
                        peer_down(b, j - 4, 8 * b + (4 * Q_PEER + 4 + j + 1))
                    rest_piece(2 * b + (Q_PEER + 2 + j // 4), j % 4)
                    if j == 1:
                        peer_lo(b, 0)
                    if j == 4:
                        dve.wait_ge(sem("gelu"), b + 2)
                        peer_mul(b + 1, 0, gacc[:], 16 * b + 16 * (2 - EARLY + (EARLY + 1) // 2))
            peer_lo(PEER_GROUPS - 1, 0)
            for j in range(4):
                peer_down(PEER_GROUPS - 1, j, 4 * QUADS - 3 + j)
                if j == 0:
                    dve.wait_ge(sem("tail_in"), 48)
                dve.wait_ge(sem("y_sum"), 4 * PEER_GROUPS - 1 + j)
                cut = slice(512 * j, 512 * j + 512)
                step(V.tensor_tensor(y[:, :, cut], y[:, :, cut], ga2[:, cut].rearrange("p (o n) -> p o n", o=1)
                                     .to_broadcast([P, TOK, 512]), ALU.mult))
                V.tensor_tensor(x[:, :, cut], x[:, :, cut], y[:, :, cut], ALU.add).then_inc(sem("x_ready"), 1)
            stats(5)
            dve.wait_ge(sem("rstd_done"), 6)
            for c in range(4):
                for k in range(TOK):
                    xc = x[:, k, 512 * c:512 * c + 512]
                    V.scalar_tensor_tensor(xc, xc, rstd[:, 1, k:k + 1], gfin[c // 2][:, 512 * (c % 2):512 * (c % 2) + 512],
                                           ALU.mult, ALU.mult).then_inc(sem("final"), 1)

        @block.tensor
        def _(pe):
            T = nc.tensor

            def split_products(out, th, tl, stat, s, cut, start, stop):
                T.matmul(out, th[stat], hi[:, s, cut], start=start, stop=False)
                T.matmul(out, th[stat], lo[:, s, cut], start=False, stop=False)
                return T.matmul(out, tl[stat], hi[:, s, cut], start=False, stop=stop)

            def wide_piece(q, s, b, th=None, tl=None):
                th, tl = (hTh, hTl) if th is None else (th, tl)
                pe.wait_ge(lo_done, 4 * q + (s + 1))
                for k in range(4):
                    for m in range(TOK):
                        ins = split_products(ps[:, b + m, :], th, tl,
                                             (slice(None), 4 * s + k, slice(P * m, P * m + P)), s,
                                             slice(512 * k, 512 * k + 512), s == 0 and k == 0, s == 3 and k == 3)
                ins.then_inc(piece_used, 1)

            def down_piece(q, s, b, th, tl):
                pe.wait_ge(lo_done, 4 * q + (s + 1))
                for m in range(TOK):
                    for k in range(4):
                        ins = split_products(ps[:, b + m, :], th, tl, (slice(None), k, slice(P * m, P * m + P)), s,
                                             slice(512 * k, 512 * k + 512), k == 0, k == 3)
                ins.then_inc(piece_used, 1)

            def turn(b, tiles):
                for k in range(4):
                    for m in range(TOK):
                        ins = T.transpose(quarters(b)[:, k, P * m:P * m + P], tiles(k, m), ident[:])
                return ins

            def fold_turn(f, tiles):
                free = f if FOLD_M <= f < FOLD_FFN else f - 1
                if free >= 1:
                    pe.wait_ge(sem("fold_t"), free)
                turn(fold_bank(f), tiles).then_inc(sem("fold_tr"), 1)

            def norm_turn(f0, g, src, u):
                pe.wait_ge(sem("xn_done"), 8 * u + 2 * g + 2)
                fold_turn(f0 + g, lambda k, m: src[:, m, P * (4 * g + k):P * (4 * g + k) + P])

            def normed_quad(f0, src, u, q, b, th=None, tl=None, after=lambda s: None):
                for g in range(3):
                    norm_turn(f0, g, src, u)
                for s in range(4):
                    pe.wait_ge(sem("fold_lo"), f0 + s + 1)
                    wide_piece(q, s, b, th, tl)
                    if s == 0:
                        norm_turn(f0, 3, src, u)
                    after(s)

            pe.wait_ge(sem("ident_in"), 16)

            def bias_by_distance(s):
                if s == 1:
                    pe.wait_ge(sem("const_in"), 16 * 10)
                    pe.wait_ge(sem("fold_t"), FOLD_X)
                    T.matmul(ps[0:6, 7, :], tabs[:], oneh[:], start=True, stop=True).then_inc(sem("bias_mm"), 1)

            normed_quad(FOLD_MEM, memraw, 0, 0, 0, memTh, memTl, bias_by_distance)
            pe.wait_ge(sem("bvec"), 1)
            norm_turn(FOLD_X, 0, x, 1)
            norm_turn(FOLD_X, 1, x, 1)
            wide_piece(1, 0, 2, memTh, memTl)
            norm_turn(FOLD_X, 2, x, 1)
            norm_turn(FOLD_X, 3, x, 1)
            for s in range(1, 4):
                wide_piece(1, s, 2, memTh, memTl)

            def head_turn(q):
                n = head_quads.index(q)
                pe.wait_ge(sem("head_n"), n + 1)
                if n >= 1:
                    pe.wait_ge(sem("head_T"), n)
                else:
                    pe.wait_ge(sem("fold_t"), FOLD_O)
                turn(4, lambda k, m: stage[:, m, HD * k:HD * k + HD]).then_inc(sem("head_tr"), 1)

            for q in range(1, Q_GATES):
                if q >= 2:
                    if q == 2:
                        pe.wait_ge(sem("fold_lo"), FOLD_O)
                    pe.wait_ge(sem("chunk_out"), q - 1)
                    for s in range(4):
                        wide_piece(q, s, 2 * (q % 2))
                if q - 1 in head_quads:
                    head_turn(q - 1)

            heads = [(h, 6 + h, h) for h in range(6)]
            heads += [(16 + j, 22 + j // 3, 6 + j // 3) for j in range(B_HEADS)]
            heads += [(12 + j, None, j) for j in range(C_HEADS)]
            for n in range(48):
                q, s = divmod(4 * Q_GATES + n, 4)
                if s == 0:
                    pe.wait_ge(sem("chunk_out"), q - 1)
                wide_piece(q, s, 2 * (q % 2))
                h, part = divmod(n, 3)
                qi, ki, vi = heads[h]
                if part == 0:
                    if h == 0:
                        pe.wait_ge(sem("head_T"), 7)
                    if h >= 1:
                        pe.wait_ge(sem("att_e"), 2 * h)
                    if h < A_HEADS:
                        pe.wait_ge(sem(f"hank_in{h % 2}"), 16 * (h // 2 + 1))
                    for m in range(TOK):
                        keys = kcT[:, h - 12] if ki is None else qkT[:, ki]
                        out = ps[:, 4, SEQ * m:SEQ * m + SEQ]
                        ins = T.matmul(out, qkT[:, qi, P * m:P * m + P], keys, start=True, stop=h >= A_HEADS)
                        if h < A_HEADS:
                            at0 = P * (1 - m)
                            ins = T.matmul(out, anti[:], hank[:, h % 2, at0:at0 + SEQ], start=False, stop=True)
                    ins.then_inc(sem("att_s"), 1)
                elif part == 1:
                    pe.wait_ge(sem("att_e"), 2 * h + 2)
                    if h >= 1:
                        pe.wait_ge(sem("att_p"), h)
                    for m in range(TOK):
                        for k in range(TOK):
                            ins = T.transpose(ps[:, 5, SEQ * k + P * m:SEQ * k + P * m + P],
                                              probs[:, m, P * k:P * k + P], ident[:])
                    ins.then_inc(sem("att_t"), 1)
                else:
                    pe.wait_ge(sem("att_p"), h + 1)
                    if h == 0:
                        pe.wait_ge(sem("chunk_out"), Q_GATES)
                    if h >= 1:
                        pe.wait_ge(sem("att_o"), h)
                    for m in range(TOK):
                        for k in range(TOK):
                            val = vC[:, k, vi] if ki is None else vAB[:, k, vi]
                            ins = T.matmul(ps[:, 6, HD * m:HD * m + HD], probsT[:, k, P * m:P * m + P], val,
                                           start=k == 0, stop=k == 1)
                    ins.then_inc(sem("att_v"), 1)

            pe.wait_ge(sem("o_ready"), 1)
            pe.wait_ge(sem("att_o"), HEADS)
            for f in range(FOLD_O, FOLD_M):
                fold_turn(f, lambda k, m: obuf[:, m, 4 + 4 * (f - FOLD_O) + k])
            pe.wait_ge(sem("chunk_out"), Q_BRANCH)

            def merged_turn(j):
                pe.wait_ge(sem("merge"), j + 1)
                fold_turn(FOLD_M + j, lambda k, m: merged[:, m, P * (4 * j + k):P * (4 * j + k) + P])

            for n in range(12):
                q, s = divmod(4 * Q_BRANCH + n, 4)
                j, part = divmod(n, 3)
                if j == 0:
                    pe.wait_ge(sem("fold_lo"), FOLD_O + part + 1)
                if n == 2:
                    pe.wait_ge(sem("fold_t"), FOLD_M)
                pe.wait_ge(lo_done, 4 * q + s + 1)
                if part == 0 and j >= 1:
                    pe.wait_ge(sem("gated"), 3 * j - 1)
                if part == 2 and j >= 1:
                    pe.wait_ge(sem("gated"), 3 * j)
                for k in range(4):
                    kt = 4 * part + k
                    b = 0 if kt < 2 else 2 if kt < 8 else 6
                    for m in range(TOK):
                        ins = split_products(ps[:, b + m, :], oTh, oTl, (slice(None), kt, slice(P * m, P * m + P)), s,
                                             slice(512 * k, 512 * k + 512), kt in (0, 2, 8), kt in (1, 7, 11))
                ins.then_inc(piece_used, 1)
                if part == 1 and j >= 1:
                    merged_turn(j - 1)

            def ada_sum(a, b):
                pe.wait_ge(sem("ada_sum"), 16 * a + 16)
                for k in range(2):
                    ins = T.matmul(ps[0:1, b + k, :], ones[:, 0:1], adaacc[:, 512 * k:512 * k + 512],
                                   start=True, stop=True)
                ins.then_inc(sem("ada_mm"), 1)

            for n in range(16):
                q, s = divmod(4 * Q_WO + n, 4)
                c = q - Q_WO
                if s == 0 and c < 2:
                    pe.wait_ge(sem("gated"), 10 + c)
                elif s == 0:
                    pe.wait_ge(sem("wo_out"), c - 1)
                if c == 0:
                    pe.wait_ge(sem("fold_lo"), FOLD_M + s + 1)
                wide_piece(q, s, 2 * (c % 2))
                if n == 0:
                    merged_turn(3)
            pe.wait_ge(sem("gated"), 12)
            ada_sum(0, 6)
            pe.wait_ge(sem("modrow"), 2)

            def ffn_turn(b):
                pe.wait_ge(sem("ffn_product"), b + 1)
                turn(4, lambda k, m: fact[:, m, P * k:P * k + P]).then_inc(sem("ffn_tr"), 1)

            def ffn_down(b, q, s):
                if s == 0:
                    pe.wait_ge(sem("ffn_lo"), b + 1)
                if s >= 1:
                    pe.wait_ge(sem("x_sum"), 4 * b + (s + 1))
                down_piece(q, s, 6 * (s % 2), factTh, factTl)

            normed_quad(FOLD_FFN, xn, 2, Q_FFN, 0)
            for s in range(4):
                wide_piece(Q_FFN + 1, s, 2)
            pe.wait_ge(sem("fold_t"), FOLD_MIX2)
            with pe.Fori(0, FF_GROUPS - 1) as b:
                for j in range(12):
                    q, s = 3 * b + (Q_FFN + 2 + j // 4), j % 4
                    if j == 0:
                        pe.wait_ge(sem("silu"), b + 1)
                        pe.wait_ge(sem("x_sum"), 4 * b + 1)
                    if j == 4:
                        pe.wait_ge(sem("ffn_product"), b + 1)
                    if j == 8:
                        pe.wait_ge(sem("silu"), b + 2)
                    if j < 8:
                        wide_piece(q, s, 0 if j < 4 else 2)
                    else:
                        ffn_down(b, q, s)
                    if j == 0:
                        ada_sum(b + 1, 4)
                    if j == 1:
                        pe.wait_ge(sem("modrow"), 2 * b + 4)
                        ffn_turn(b)
            ffn_turn(FF_GROUPS - 1)
            for s in range(4):
                ffn_down(FF_GROUPS - 1, Q_IN2 - 1, s)
                if s == 0:
                    ada_sum(ADA_SPLITS - 1, 4)

            def in_turn(c):
                n = TURNED.index(c)
                pe.wait_ge(sem("in_out"), c + 1)
                if n == 0:
                    pe.wait_ge(sem("fold_t"), FOLD_ATT)
                elif n <= 4:
                    pe.wait_ge(sem("qk_T"), n)
                elif n <= 6:
                    pe.wait_ge(sem("lx_T"), n - 4)
                else:
                    pe.wait_ge(sem("gy_T"), 1)
                turn(4, lambda k, m: stage[:, m, P * k:P * k + P]).then_inc(sem("in_tr"), 1)

            def forget_logits():
                pe.wait_ge(sem("wfl"), 1)
                for k in range(KT):
                    for j, (a, b) in enumerate(((wfh, hTh), (wfl, hTh), (wfh, hTl))):
                        ins = T.matmul(ps[0:8, 7, 0:SEQ], a[:, k, :], b[:, k, :],
                                       start=k == 0 and j == 0, stop=k == KT - 1 and j == 2)
                ins.then_inc(sem("f_mm"), 1)

            def scores2(h):
                if h == 0:
                    pe.wait_ge(sem("sel_in"), 16)
                    pe.wait_ge(sem("cum"), 1)
                    pe.wait_ge(sem("qk_T"), 2)
                else:
                    pe.wait_ge(sem("exp2"), 2 * h)
                if h == 4:
                    pe.wait_ge(sem("qk_T"), 4)
                for m in range(TOK):
                    keys = P * (m + 1)
                    out = ps[:, 6, SEQ * m:SEQ * m + keys]
                    T.matmul(out, qkT2[:, h, P * m:P * m + P], qkT2[:, 8 + h, 0:keys], start=True, stop=False)
                    T.matmul(out, lgate[:, 1, P * m:P * m + P], sel[:, h, 0:keys], start=False, stop=False)
                    T.matmul(out, sel[:, h, 0:P], lgate[:, 2, 0:keys], start=False, stop=False)
                    ins = T.matmul(ps[:, 6, SEQ * m + P * m:SEQ * m + keys], ident[:], causal[:], start=False, stop=True)
                ins.then_inc(sem("scores2"), 1)

            def turn2(h):
                pe.wait_ge(sem("exp2"), 2 * h + 2)
                if h >= 1:
                    pe.wait_ge(sem("output2"), h)
                for m in range(TOK):
                    for k in range(m + 1):
                        ins = T.transpose(ps[:, 7, SEQ * k + P * m:SEQ * k + P * m + P],
                                          probs2[:, h % 2, m, P * k:P * k + P], ident[:])
                ins.then_inc(sem("turned2"), 1)

            def output2(h):
                pe.wait_ge(sem("probs2"), h + 1)
                if h % 4 == 0:
                    pe.wait_ge(sem("in_out"), 3 if h == 0 else 6)
                for m in range(TOK):
                    for k in range(m + 1):
                        ins = T.matmul(ps[:, 7, HD * m:HD * m + HD], probsT2[:, h % 2, k, P * m:P * m + P],
                                       v2[:, k, HD * h:HD * h + HD], start=k == 0, stop=k == m)
                ins.then_inc(sem("values2"), 1)

            def lru_products(n):
                if n == 0:
                    pe.wait_ge(sem("lw_in"), 32)
                    pe.wait_ge(sem("output2"), H2)
                pe.wait_ge(sem("conv"), n + 1)
                if n >= 2:
                    pe.wait_ge(sem("i_out"), n - 1)
                T.matmul(ps[:, 6 + n % 2, 0:SEQ], lwa[:, n], bx[:, n], start=True, stop=True)
                T.matmul(ps[:, 6 + n % 2, SEQ:2 * SEQ], lwx[:, n], bx[:, n], start=True, stop=True)\
                    .then_inc(sem("lru_mm"), 1)

            def attention_turn(g):
                pe.wait_ge(sem("att2_s"), 2)
                if g == 0:
                    pe.wait_ge(sem("i_out"), 8)
                else:
                    pe.wait_ge(sem("fold_t"), FOLD_ATT + 1)
                turn(fold_bank(FOLD_ATT + g), lambda k, m: att2[:, m, 4 * g + k]).then_inc(sem("fold_tr"), 1)

            for c in range(IN_CHUNKS):
                if c >= 2:
                    pe.wait_ge(sem("in_out"), c - 1)
                if c == 0:
                    normed_quad(FOLD_MIX2, xn, 3, Q_IN2, 0)
                    continue
                for s in range(4):
                    i = 4 * (c - 3) + s
                    wide_piece(Q_IN2 + c, s, 2 * (c % 2))
                    if s == 0 and c - 1 in TURNED:
                        in_turn(c - 1)
                    if (c, s) == (1, 0):
                        forget_logits()
                    if i in OUTPUT_AT:
                        output2(OUTPUT_AT[i])
                    if i in TURN_AT:
                        turn2(TURN_AT[i])
                    if i in SCORES_AT:
                        scores2(SCORES_AT[i])
                    if c == 8:
                        lru_products(2 * s)
                        lru_products(2 * s + 1)
                    if c == 9 and s in (0, 2):
                        attention_turn(s // 2)

            def lru_squares(n):
                pe.wait_ge(sem("lsq"), n + 1)
                if n == 0:
                    pe.wait_ge(sem("gy_T"), 2)
                for k in range(4 * n, 4 * n + 4):
                    ins = T.matmul(ps[:, 4, 0:SEQ], ones[:], lsq[:, k], start=k == 0, stop=k == 7)
                if n == 1:
                    ins.then_inc(sem("lsum_mm"), 1)

            for n, (c, g) in enumerate(OUT_PIECES):
                q, s = divmod(4 * Q_OUT2 + n, 4)
                if g == 0:
                    pe.wait_ge(sem("in_out"), 9 + c) if c < 2 else pe.wait_ge(sem("out2"), c - 1)
                if c == 0:
                    pe.wait_ge(sem("fold_lo"), FOLD_ATT + g + 1)
                pe.wait_ge(lo_done, 4 * q + s + 1)
                th, tl = (attTh, attTl) if g < 2 else (hTh, hTl)
                for k in range(4):
                    for m in range(TOK):
                        ins = split_products(ps[:, 2 * (c % 2) + m, :], th, tl,
                                             (slice(None), 4 * g + k, slice(P * m, P * m + P)), s,
                                             slice(512 * k, 512 * k + 512), g == 0 and k == 0, g == 3 and k == 3)
                ins.then_inc(piece_used, 1)
                if n == 0:
                    in_turn(9)
                if n in (1, 2):
                    lru_squares(n - 1)

            def pq_turn(c):
                pe.wait_ge(sem("pq_out"), c + 1)
                if c == 0:
                    pe.wait_ge(sem("out2"), 4)
                    pe.wait_ge(sem("fold_t"), FOLD_PEER + 4)
                else:
                    pe.wait_ge(sem("pq_T"), c)
                turn(4, lambda k, m: stage[:, m, P * k:P * k + P]).then_inc(sem("pq_tr"), 1)

            def key_scores(c):
                pe.wait_ge(sem("keys_in"), 16)
                pe.wait_ge(sem("pq_T"), c + 1)
                if c >= 1:
                    pe.wait_ge(sem("sc_out"), c)
                for k in range(4):
                    for m in range(TOK):
                        ins = T.matmul(ps[:, 6 + m, P * k:P * k + P], pqT[:, 4 * c + k, P * m:P * m + P],
                                       keysT[:, 4 * c + k], start=True, stop=True)
                ins.then_inc(sem("key_scores"), 1)

            for c in range(4):
                if c >= 2:
                    pe.wait_ge(sem("pq_out"), c - 1)
                if c == 0:
                    normed_quad(FOLD_PEER, xn, 4, Q_PQ, 0)
                else:
                    for s in range(4):
                        wide_piece(Q_PQ + c, s, 2 * (c % 2))
                if c >= 1:
                    pq_turn(c - 1)
                if c >= 2:
                    key_scores(c - 2)
            pe.wait_ge(sem("pq_out"), 3)
            wide_piece(Q_PEER, 0, 0)
            pq_turn(3)
            wide_piece(Q_PEER, 1, 0)
            key_scores(2)
            wide_piece(Q_PEER, 2, 0)
            key_scores(3)
            wide_piece(Q_PEER, 3, 0)
            pe.wait_ge(sem("pq_out"), 4)

            def early_group(g, u, mid=lambda s: None):
                if not isinstance(g, int) or g >= 2:
                    pe.wait_ge(sem("gelu"), g - 1)
                for s in range(4):
                    wide_piece(g + Q_PEER, s, 2 * u)
                    mid(s)

            early_group(1, 1)
            with pe.Fori(1, EARLY_TOP // 2) as m:
                for u in range(2):
                    early_group(2 * m + u, u)
            pe.wait_ge(sem("picks"), 1)
            pe.wait_ge(sem("sc_out"), 4)
            for e in range(3):
                for m in range(TOK):
                    c0 = SEQ * e + P * m
                    ins = T.transpose(ps[:, 6 + c0 // 512, c0 % 512:c0 % 512 + P],
                                      picks[:, m, e].rearrange("p h n -> p (h n)"), ident[:])
            ins.then_inc(sem("picks_tr"), 1)

            def expert_weights(i, v):
                n = 2 * i + v
                pe.wait_ge(sem("one_hots"), n + 1)
                if n >= 2:
                    pe.wait_ge(sem("weights_out"), n - 1)
                for k in range(8):
                    ins = T.matmul(ps[:, 4 + 2 * v + k // 4, P * (k % 4):P * (k % 4) + P], oh[:, v, 0, k],
                                   oh[:, v, 1, k], start=True, stop=True)
                ins.then_inc(sem("weights_mm"), 1)

            def weights_pair(i):
                if i == 0:
                    pe.wait_ge(sem("picksT"), 1)
                for v in range(2):
                    expert_weights(i, v)

            for g in range(4):
                early_group(EARLY_TOP + g, g % 2, lambda s: weights_pair(4 * g + s))

            def peer_turn(b):
                pe.wait_ge(sem("peer_product"), b + 1)
                turn(4, lambda k, m: pact[:, m, P * k:P * k + P]).then_inc(sem("peer_tr"), 1)

            def first_turn(s):
                if s == 2:
                    pe.wait_ge(sem("weights_out"), SEQ // 8)
                    peer_turn(0)

            early_group(EARLY - 1, 0, first_turn)

            def peer_down(b, q, s, u):
                if s == 0:
                    pe.wait_ge(sem("peer_lo"), b + 1)
                pe.wait_ge(sem("y_sum"), 4 * b + (s + 1))
                down_piece(q, s, 6 if s % 2 == 0 else 2, pactTh[:, u], pactTl[:, u])

            def down_group(b, u, turned=True):
                for s in range(4):
                    if s == 0:
                        pe.wait_ge(sem("peer_lo"), b + 1)
                    pe.wait_ge(sem("y_sum"), 4 * b + (s + 1))
                    down_piece(b + (Q_PEER + EARLY), s, 6 if s % 2 == 0 else 2, pactTh[:, u], pactTl[:, u])
                    if s == 1 and turned:
                        peer_turn(b + 1)

            pe.wait_ge(sem("y_sum"), 2)
            with pe.Fori(0, (EARLY - 1) // 2 - 1) as m:
                for u in range(2):
                    down_group(2 * m + u, u)
            down_group(EARLY - 3, 0)
            down_group(EARLY - 2, 1, turned=False)

            with pe.Fori(EARLY - 1, PEER_GROUPS - 1) as b:
                for j in range(8):
                    q, s = 2 * b + (Q_PEER + 1 + j // 4), j % 4
                    if j == 0:
                        pe.wait_ge(sem("gelu"), b + 1)
                    if j < 4:
                        wide_piece(q, s, 0)
                    else:
                        peer_down(b, q, s, 0)
                    if j == 1:
                        peer_turn(b)
            peer_turn(PEER_GROUPS - 1)
            for s in range(4):
                peer_down(PEER_GROUPS - 1, QUADS - 1, s, 0)


def _tables():
    eye = np.eye(P, dtype=np.float32)
    d = np.arange(-255, 257, dtype=np.int64)
    half = BUCKETS // 2
    exact = half // 2
    n = np.abs(d)
    large = exact + (np.log(np.maximum(n, 1).astype(np.float32) / np.float32(exact))
                     / np.float32(math.log(MAX_DIST / exact)) * np.float32(half - exact)).astype(np.int32)
    bucket = np.where(d > 0, half, 0) + np.where(n < exact, n, np.minimum(large, half - 1))
    oneh = (bucket[None, :] == np.arange(BUCKETS)[:, None]).astype(np.float32)
    dmask = np.zeros((6, 512), np.float32)
    for g, dil in enumerate(DILATIONS):
        dmask[2 * g:2 * g + 2] = np.where((d % dil == 0) & (n <= RADIUS_STEPS * dil), 0.0, NEG)
    r = np.repeat(np.arange(SEQ // 64), 64).astype(np.float32)
    c = np.tile(np.arange(64), SEQ // 64).astype(np.float32)
    inv = (np.float32(10000.0) ** (-np.arange(HD // 4, dtype=np.float32) / np.float32(HD // 4))).astype(np.float32)
    ang = np.concatenate([r[:, None] * inv, c[:, None] * inv], axis=-1)
    cos, sin = np.repeat(np.cos(ang), 2, axis=1), np.repeat(np.sin(ang), 2, axis=1)
    sin[:, 0::2] *= -1
    rope = np.stack([cos, sin]).reshape(2, TOK, P, HD).transpose(2, 0, 1, 3)
    causal = np.where(np.arange(P)[None, :] <= np.arange(P)[:, None], 0.0, NEG)
    sel = np.repeat(np.eye(8, dtype=np.float32)[:, :, None], SEQ, axis=2)
    return {"ident": eye, "anti": eye[::-1], "iota": np.tile(np.arange(P, dtype=np.float32), (P, 1)),
            "oneh": oneh, "dmask": dmask, "rope": rope, "causal": causal, "sel": sel}


def _wide(w):
    k, n = w.shape
    return w.reshape(k // 2048, 4, 4, P, n // 512, 512).transpose(4, 0, 1, 3, 2, 5).reshape(-1, P, 2048)


def _down(w):
    k, n = w.shape
    return w.reshape(k // 512, 4, P, n // 512, 512).transpose(0, 3, 2, 1, 4).reshape(-1, P, 2048)


def _columns(v):
    return v.reshape(-1, P).T


def kernel(**inputs):
    import concourse.bacc as bacc
    from concourse.bass_utils import run_bass_kernel_spmd

    v = {k: np.asarray(a) for k, a in inputs.items()}
    w_in = v["w_in"][0]
    A_W, B_Q, B_K, C_W = 768, 768, 256, 512
    o = np.cumsum([0, A_W, A_W, A_W, B_Q, B_K, B_K, C_W, 3 * D])
    qa, ka, va, qb, kb, vb, qc, gt = [w_in[:, o[i]:o[i + 1]] for i in range(8)]
    w_mem = v["w_mem_kv"][0]
    first = np.concatenate([_wide(w_mem)] + [_wide(a) for a in (
        np.concatenate([qa, ka, qc, qb, kb, va, vb], axis=1), gt)])
    branch = np.concatenate([v["w_br_a"][0], v["w_br_b"][0], v["w_br_c"][0]])
    branch = branch.reshape(3, 4, P, 4, 512).transpose(3, 0, 2, 1, 4).reshape(-1, P, 2048)
    merge = np.concatenate([branch, _wide(v["w_o"][0])])
    gate, up = _wide(v["w_ffn_in"][0][:, :D_FF]), _wide(v["w_ffn_in"][0][:, D_FF:])
    down = _down(v["w_ffn_out"][0])
    g4, u4, d4 = (a.reshape(FF_GROUPS, 4, P, 2048) for a in (gate, up, down))
    order = [g4[0], u4[0]]
    for g in range(1, FF_GROUPS):
        order += [g4[g], u4[g], d4[g - 1]]
    ffn = np.concatenate(order + [d4[-1]])
    w2 = v["w_in_2"][0]
    q2, k2, v2, lx, ly = (_wide(w2[:, a:a + 1024]).reshape(2, 4, P, 2048) for a in (0, 1024, 2048, 3080, 4104))
    out2 = _wide(v["w_out_2"][0]).reshape(4, 4, P, 2048)
    second = np.concatenate([q2[0], k2[0], v2[0], q2[1], k2[1], v2[1], lx[0], lx[1], ly[0], ly[1],
                             np.stack([out2[c, g] for c, g in OUT_PIECES]), _wide(v["peer_w_q_2"][0])])
    pu = _wide(v["peer_u_2"][0].T).reshape(PEER_GROUPS, 4, P, 2048)
    pv = _down(v["peer_v_2"][0]).reshape(PEER_GROUPS, 4, P, 2048)
    order = [*pu[:EARLY], *pv[:EARLY - 1]]
    for g in range(EARLY, PEER_GROUPS):
        order += [pu[g], pv[g - 1]]
    peer = np.concatenate(order + [pv[-1]])
    cols = np.zeros((P, NCOLS), np.float32)
    for at0, name in ((C_GMEM, "g_mem"), (C_GMIX, "g_mix"), (C_GFFN, "g_ffn"), (C_GMIX2, "g_mix_2"), (C_GFFN2, "g_ffn_2")):
        cols[:, at0:at0 + 16] = _columns(v[name][0])
    for at0, n, name in ((0, 6, "g_qa"), (6, 6, "g_ka"), (12, 4, "g_qc"), (16, 4, "g_kc")):
        cols[:, C_HEAD + at0:C_HEAD + at0 + n] = v[name][0][:, None]
    for j in range(CONV):
        cols[:, C_CONVW + 8 * j:C_CONVW + 8 * j + 8] = _columns(v["conv_w_2"][0, j])
    for at0, name in ((C_CONVB, "conv_b_2"), (C_BA, "lru_b_a_2"), (C_BX, "lru_b_x_2"), (C_LAM, "lru_lambda_2"),
                      (C_GLRU, "g_lru_out_2"), (C_GATT, "g_attn_out_2")):
        cols[:, at0:at0 + 8] = _columns(v[name][0])
    cols[0:8, C_BF] = v["b_f_2"][0]
    keys = np.stack([v["peer_k1_2"][0], v["peer_k2_2"][0]], axis=1).reshape(16, N_KEYS, P).transpose(2, 0, 1)
    arrays = {
        "x": v["x"][0], "mem": v["mem"][0], "w_first": first, "w_merge": merge, "w_ffn": ffn,
        "w_second": second, "w_peer": peer, "cols": cols, "rel_bias": v["rel_bias"],
        "g_qb": v["g_qb"], "g_kb": v["g_kb"], "c": _columns(v["c_2"][0]),
        "w_ada": v["w_ada_2"][0].reshape(8, 2, P, ADA_SPLITS, 1024).transpose(3, 0, 2, 1, 4).reshape(-1, P, 2048),
        "b_ada": v["b_ada_2"][0].reshape(ADA_SPLITS, 1, 1024),
        "w_f": w2[:, 3072:3080].reshape(KT, P, 8).transpose(1, 0, 2),
        "lru_w_a": v["lru_w_a_2"][0].transpose(1, 0, 2), "lru_w_x": v["lru_w_x_2"][0].transpose(1, 0, 2),
        "keys": keys, "g_final": v["g_final_2"].reshape(1, D), **_tables()}
    arrays = {f"in_{k}": np.ascontiguousarray(a, dtype=np.float32) for k, a in arrays.items()}
    nc = bacc.Bacc("TRN2", target_bir_lowering=False, num_devices=1)
    aps = {k[3:]: nc.dram_tensor(k, a.shape, F32, kind="ExternalInput").ap() for k, a in arrays.items()}
    aps["out"] = nc.dram_tensor("out", (SEQ, D), F32, kind="ExternalOutput").ap()
    program(nc, aps)
    r = run_bass_kernel_spmd(nc, [arrays], core_ids=[0])
    return np.asarray(r.results[0]["out"]).reshape(1, SEQ, D)
```
